# Optimizing a Trainium2 kernel written in Bass

```python
import math
import numpy as np
import jax
import jax.numpy as jnp
from jax import lax

D_MODEL = 2048
BATCH = 1
SEQ = 256
DEPTH = 1

GRID_W = 64
N_MIXERS = 3
NORM_EPS = 1e-6
NEG_INF = -1e30

DA_HEADS = 8
DA_HEAD_DIM = 128
DA_WIDTH = DA_HEADS * 2 * DA_HEAD_DIM
DA_Q_BLOCK = 128

GLA_HEADS = 4
GLA_KEY_DIM = D_MODEL // 2
GLA_VAL_DIM = D_MODEL
GLA_DK = GLA_KEY_DIM // GLA_HEADS
GLA_DV = GLA_VAL_DIM // GLA_HEADS
GLA_GATE_RANK = 16
GLA_TAU = 16.0
GLA_CHUNK = 64

NA_HEADS = 64
NA_HEAD_DIM = 32
NA_WIDTH = NA_HEADS * NA_HEAD_DIM
NA_ROWS = 8
NA_COLS = 16

MOE_GROUPS = 4
MOE_EXPERTS_PER_GROUP = 8
MOE_EXPERTS = MOE_GROUPS * MOE_EXPERTS_PER_GROUP
MOE_TOP_K = 2
MOE_D_FF = 512
MOE_BLOCK = 128

kernel_name = "hybrid_diffattn_gla_natten_hmoe_encoder"

def rms_norm(x, g):
    xf = x.astype(jnp.float32)
    y = xf * lax.rsqrt(jnp.mean(xf * xf, axis=-1, keepdims=True) + NORM_EPS)
    return (y * g.astype(jnp.float32)).astype(x.dtype)

def lambda_init(layer_idx):
    return 0.8 - 0.6 * math.exp(-0.3 * layer_idx)

def alibi_slopes(n_heads):
    return jnp.asarray(2.0 ** (-8.0 * np.arange(1, n_heads + 1) / n_heads), dtype=jnp.float32)

def diff_attention(h, w_in, w_out, lam_q1, lam_k1, lam_q2, lam_k2, subln_g, lam_init):
    bsz, t, _ = h.shape
    f32 = jnp.float32
    q, k, v = jnp.split(h @ w_in, 3, axis=-1)
    q = q.reshape(bsz, t, DA_HEADS, 2, DA_HEAD_DIM) * DA_HEAD_DIM ** -0.5
    k = k.reshape(bsz, t, DA_HEADS, 2, DA_HEAD_DIM)
    v = v.reshape(bsz, t, DA_HEADS, 2 * DA_HEAD_DIM)
    lam = (jnp.exp(jnp.sum(lam_q1.astype(f32) * lam_k1.astype(f32)))
           - jnp.exp(jnp.sum(lam_q2.astype(f32) * lam_k2.astype(f32))) + lam_init)
    slopes = alibi_slopes(DA_HEADS)
    n_blk = t // DA_Q_BLOCK
    q_blocks = q.reshape(bsz, n_blk, DA_Q_BLOCK, DA_HEADS, 2, DA_HEAD_DIM).transpose(1, 0, 3, 4, 2, 5)
    k_t = k.transpose(0, 2, 3, 1, 4)
    v_t = v.transpose(0, 2, 1, 3)
    key_pos = jnp.arange(t)

    def block(args):
        q_blk, start = args
        s = jnp.einsum('bhiqd,bhikd->bhiqk', q_blk, k_t).astype(f32)
        q_pos = start + jnp.arange(DA_Q_BLOCK)
        dist = jnp.abs(q_pos[:, None] - key_pos[None, :]).astype(f32)
        p = jax.nn.softmax(s - slopes[None, :, None, None, None] * dist, axis=-1)
        a = p[:, :, 0] - lam * p[:, :, 1]
        return jnp.einsum('bhqk,bhkv->bhqv', a.astype(v_t.dtype), v_t)

    o = lax.map(block, (q_blocks, jnp.arange(n_blk, dtype=jnp.int32) * DA_Q_BLOCK))
    o = o.transpose(1, 0, 3, 2, 4).reshape(bsz, t, DA_HEADS, 2 * DA_HEAD_DIM)
    o = rms_norm(o, subln_g) * (1.0 - lam_init)
    return o.reshape(bsz, t, DA_WIDTH) @ w_out

def _gla_chunked(q, k, v, log_a):
    bsz, nh, t, dk = q.shape
    dv = v.shape[-1]
    cs = GLA_CHUNK
    n = t // cs
    q = q.reshape(bsz, nh, n, cs, dk)
    k = k.reshape(bsz, nh, n, cs, dk)
    v = v.reshape(bsz, nh, n, cs, dv)
    b = jnp.cumsum(log_a.reshape(bsz, nh, n, cs, dk), axis=3)
    b_end = b[:, :, :, -1:, :]
    q_in = q * jnp.exp(b)
    k_in = k * jnp.exp(-b)
    k_out = k * jnp.exp(b_end - b)
    lower = jnp.tril(jnp.ones((cs, cs), dtype=bool))
    att = jnp.where(lower, jnp.einsum('bhncd,bhnsd->bhncs', q_in, k_in), 0.0)
    o_intra = jnp.einsum('bhncs,bhnsv->bhncv', att, v)

    def step(state, xs):
        q_c, k_c, v_c, dec_c = xs
        o_c = jnp.einsum('bhcd,bhdv->bhcv', q_c, state)
        state = dec_c[..., None] * state + jnp.einsum('bhcd,bhcv->bhdv', k_c, v_c)
        return state, o_c

    xs = (jnp.moveaxis(q_in, 2, 0), jnp.moveaxis(k_out, 2, 0), jnp.moveaxis(v, 2, 0),
          jnp.moveaxis(jnp.exp(b_end[:, :, :, 0, :]), 2, 0))
    state0 = jnp.zeros((bsz, nh, dk, dv), jnp.float32)
    _, o_inter = lax.scan(step, state0, xs)
    return (o_intra + jnp.moveaxis(o_inter, 0, 2)).reshape(bsz, nh, t, dv)

def gla_mixer(h, w_in, gate_w2_f, gate_b_f, gate_w2_b, gate_b_b, norm_g, w_out):
    bsz, t, _ = h.shape
    f32 = jnp.float32
    cuts = [GLA_KEY_DIM, 2 * GLA_KEY_DIM, 2 * GLA_KEY_DIM + GLA_VAL_DIM, 2 * GLA_KEY_DIM + 2 * GLA_VAL_DIM]
    q, k, v, r, g_lr = jnp.split(h @ w_in, cuts, axis=-1)
    g_f, g_b = jnp.split(g_lr, 2, axis=-1)
    log_a_f = jax.nn.log_sigmoid((g_f @ gate_w2_f + gate_b_f).astype(f32)) / GLA_TAU
    log_a_b = jax.nn.log_sigmoid((g_b @ gate_w2_b + gate_b_b).astype(f32)) / GLA_TAU

    def heads(z, dh):
        return z.astype(f32).reshape(bsz, t, GLA_HEADS, dh).transpose(0, 2, 1, 3)

    qh = heads(q, GLA_DK) * GLA_DK ** -0.5
    kh = heads(k, GLA_DK)
    vh = heads(v, GLA_DV)
    o_fwd = _gla_chunked(qh, kh, vh, heads(log_a_f, GLA_DK))
    flip = lambda z: jnp.flip(z, axis=2)
    o_bwd = flip(_gla_chunked(flip(qh), flip(kh), flip(vh), flip(heads(log_a_b, GLA_DK))))
    o = (o_fwd + o_bwd).transpose(0, 2, 1, 3)
    o = rms_norm(o, norm_g) * jax.nn.silu(r.astype(f32)).reshape(bsz, t, GLA_HEADS, GLA_DV)
    return o.reshape(bsz, t, GLA_VAL_DIM).astype(h.dtype) @ w_out

def neighborhood_attention(h, w_in, rpb, w_out):
    bsz, t, _ = h.shape
    rows = t // GRID_W
    kr = min(NA_ROWS, rows)
    q, k, v = jnp.split(h @ w_in, 3, axis=-1)
    shape5 = (bsz, rows, GRID_W, NA_HEADS, NA_HEAD_DIM)
    q = q.reshape(shape5) * NA_HEAD_DIM ** -0.5
    k = k.reshape(shape5)
    v = v.reshape(shape5)
    col = np.arange(GRID_W)
    col_start = np.clip(col - NA_COLS // 2, 0, GRID_W - NA_COLS)
    in_window = (col[None, :] >= col_start[:, None]) & (col[None, :] < col_start[:, None] + NA_COLS)
    col_off = np.clip(col[None, :] - col[:, None] + NA_COLS - 1, 0, 2 * NA_COLS - 2)

    def row_block(r):
        r0 = jnp.clip(r - kr // 2, 0, rows - kr)
        k_band = lax.dynamic_slice_in_dim(k, r0, kr, axis=1)
        v_band = lax.dynamic_slice_in_dim(v, r0, kr, axis=1)
        q_row = lax.dynamic_index_in_dim(q, r, axis=1, keepdims=False)
        s = jnp.einsum('bqhd,bikhd->bhqik', q_row, k_band).astype(jnp.float32)
        row_off = r0 + jnp.arange(kr) - r + NA_ROWS - 1
        bias = rpb[:, row_off][:, :, col_off].transpose(0, 2, 1, 3)
        s = jnp.where(in_window[None, None, :, None, :], s + bias[None].astype(jnp.float32), NEG_INF)
        p = jax.nn.softmax(s.reshape(bsz, NA_HEADS, GRID_W, kr * GRID_W), axis=-1).reshape(s.shape)
        return jnp.einsum('bhqik,bikhd->bqhd', p.astype(v_band.dtype), v_band)

    o = lax.map(row_block, jnp.arange(rows, dtype=jnp.int32))
    o = o.transpose(1, 0, 2, 3, 4).reshape(bsz, t, NA_WIDTH)
    return o @ w_out

def _experts_sorted(hf, expert_id, weight, w_gu, w_d):
    n_tok, d = hf.shape
    n_exp = w_gu.shape[0]
    flat_e = expert_id.reshape(-1)
    n_asg = flat_e.shape[0]
    order = jnp.argsort(flat_e)
    sorted_e = flat_e[order]
    tok = order // MOE_TOP_K
    counts = jnp.bincount(flat_e, length=n_exp)
    start = jnp.cumsum(counts) - counts
    padded = (counts + MOE_BLOCK - 1) // MOE_BLOCK * MOE_BLOCK
    pad_end = jnp.cumsum(padded)
    pad_start = pad_end - padded
    slot = pad_start[sorted_e] + jnp.arange(n_asg) - start[sorted_e]
    n_blocks = -(-n_asg // MOE_BLOCK) + n_exp
    buf = jnp.zeros((n_blocks * MOE_BLOCK, d), hf.dtype).at[slot].set(hf[tok])
    block_e = jnp.minimum(jnp.searchsorted(pad_end, jnp.arange(n_blocks) * MOE_BLOCK, side='right'), n_exp - 1)

    def block(args):
        xb, e = args
        g, u = jnp.split(xb @ w_gu[e], 2, axis=-1)
        return (jax.nn.silu(g) * u) @ w_d[e]

    out = lax.map(block, (buf.reshape(n_blocks, MOE_BLOCK, d), block_e)).reshape(-1, d)
    contrib = out[slot] * weight.reshape(-1)[order][:, None].astype(out.dtype)
    return jnp.zeros((n_tok, d), out.dtype).at[tok].add(contrib)

def hierarchical_moe(h, rg_w, rg_b, re_w, re_b, w_gu, w_d):
    bsz, t, d = h.shape
    f32 = jnp.float32
    hf = h.reshape(-1, d)
    n_tok = hf.shape[0]
    g_prob = jax.nn.softmax((hf @ rg_w).astype(f32) + rg_b.astype(f32), axis=-1)
    g_p, g_idx = lax.top_k(g_prob, 1)
    e_logits = ((hf @ re_w).astype(f32) + re_b.astype(f32)).reshape(n_tok, MOE_GROUPS, MOE_EXPERTS_PER_GROUP)
    e_logits = e_logits[jnp.arange(n_tok), g_idx[:, 0]]
    e_p, e_idx = lax.top_k(jax.nn.softmax(e_logits, axis=-1), MOE_TOP_K)
    e_p = e_p / jnp.sum(e_p, axis=-1, keepdims=True)
    weight = g_p * e_p
    expert_id = g_idx * MOE_EXPERTS_PER_GROUP + e_idx
    return _experts_sorted(hf, expert_id, weight, w_gu, w_d).reshape(bsz, t, d)

def setup_inputs(seed: int = 0) -> dict:
    key = jax.random.key(seed)
    keys = jax.random.split(key, 40)
    D = D_MODEL
    n_da = len(range(0, DEPTH, N_MIXERS))
    n_gla = len(range(1, DEPTH, N_MIXERS))
    n_na = len(range(2, DEPTH, N_MIXERS))

    def nrm(i, shape, scale):
        return jax.random.normal(keys[i], shape, jnp.float32) * scale

    def gain(i, shape):
        return 1.0 + nrm(i, shape, 0.05)

    gla_in_cols = 2 * GLA_KEY_DIM + 2 * GLA_VAL_DIM + 2 * GLA_GATE_RANK
    return {
        "x": nrm(0, (BATCH, SEQ, D), 1.0),
        "c": nrm(1, (BATCH, D), 1.0),
        "ada_w": nrm(2, (DEPTH, D, 6 * D), 0.5 * D ** -0.5),
        "ada_b": nrm(3, (DEPTH, 6 * D), 0.02),
        "norm1_g": gain(4, (DEPTH, D)),
        "norm2_g": gain(5, (DEPTH, D)),
        "router_g_w": nrm(6, (DEPTH, D, MOE_GROUPS), D ** -0.5),
        "router_g_b": nrm(7, (DEPTH, MOE_GROUPS), 0.01),
        "router_e_w": nrm(8, (DEPTH, D, MOE_EXPERTS), D ** -0.5),
        "router_e_b": nrm(9, (DEPTH, MOE_EXPERTS), 0.01),
        "moe_w_gu": nrm(10, (DEPTH, MOE_EXPERTS, D, 2 * MOE_D_FF), D ** -0.5),
        "moe_w_d": nrm(11, (DEPTH, MOE_EXPERTS, MOE_D_FF, D), MOE_D_FF ** -0.5),
        "da_w_in": nrm(12, (n_da, D, 3 * DA_WIDTH), D ** -0.5),
        "da_w_out": nrm(13, (n_da, DA_WIDTH, D), DA_WIDTH ** -0.5),
        "da_lam_q1": nrm(14, (n_da, DA_HEAD_DIM), 0.1),
        "da_lam_k1": nrm(15, (n_da, DA_HEAD_DIM), 0.1),
        "da_lam_q2": nrm(16, (n_da, DA_HEAD_DIM), 0.1),
        "da_lam_k2": nrm(17, (n_da, DA_HEAD_DIM), 0.1),
        "da_subln_g": gain(18, (n_da, 2 * DA_HEAD_DIM)),
        "gla_w_in": nrm(19, (n_gla, D, gla_in_cols), D ** -0.5),
        "gla_gate_w2_f": nrm(20, (n_gla, GLA_GATE_RANK, GLA_KEY_DIM), GLA_GATE_RANK ** -0.5),
        "gla_gate_b_f": nrm(21, (n_gla, GLA_KEY_DIM), 0.1),
        "gla_gate_w2_b": nrm(22, (n_gla, GLA_GATE_RANK, GLA_KEY_DIM), GLA_GATE_RANK ** -0.5),
        "gla_gate_b_b": nrm(23, (n_gla, GLA_KEY_DIM), 0.1),
        "gla_norm_g": gain(24, (n_gla, GLA_DV)),
        "gla_w_out": nrm(25, (n_gla, GLA_VAL_DIM, D), GLA_VAL_DIM ** -0.5),
        "na_w_in": nrm(26, (n_na, D, 3 * NA_WIDTH), D ** -0.5),
        "na_rpb": nrm(27, (n_na, NA_HEADS, 2 * NA_ROWS - 1, 2 * NA_COLS - 1), 0.1),
        "na_w_out": nrm(28, (n_na, NA_WIDTH, D), NA_WIDTH ** -0.5),
        "final_g": gain(29, (D,)),
    }

def reference(x, c, ada_w, ada_b, norm1_g, norm2_g, router_g_w, router_g_b, router_e_w, router_e_b,
              moe_w_gu, moe_w_d, da_w_in, da_w_out, da_lam_q1, da_lam_k1, da_lam_q2, da_lam_k2, da_subln_g,
              gla_w_in, gla_gate_w2_f, gla_gate_b_f, gla_gate_w2_b, gla_gate_b_b, gla_norm_g, gla_w_out,
              na_w_in, na_rpb, na_w_out, final_g):
    cond = jax.nn.silu(c)
    for i in range(DEPTH):
        mod = (cond @ ada_w[i] + ada_b[i])[:, None, :]
        sh1, sc1, g1, sh2, sc2, g2 = jnp.split(mod, 6, axis=-1)
        hm = rms_norm(x, norm1_g[i]) * (1.0 + sc1) + sh1
        kind = i % N_MIXERS
        j = i // N_MIXERS
        if kind == 0:
            y = diff_attention(hm, da_w_in[j], da_w_out[j], da_lam_q1[j], da_lam_k1[j],
                               da_lam_q2[j], da_lam_k2[j], da_subln_g[j], lambda_init(i))
        elif kind == 1:
            y = gla_mixer(hm, gla_w_in[j], gla_gate_w2_f[j], gla_gate_b_f[j], gla_gate_w2_b[j],
                          gla_gate_b_b[j], gla_norm_g[j], gla_w_out[j])
        else:
            y = neighborhood_attention(hm, na_w_in[j], na_rpb[j], na_w_out[j])
        x = x + g1 * y
        hf = rms_norm(x, norm2_g[i]) * (1.0 + sc2) + sh2
        x = x + g2 * hierarchical_moe(hf, router_g_w[i], router_g_b[i], router_e_w[i], router_e_b[i],
                                      moe_w_gu[i], moe_w_d[i])
    return rms_norm(x, final_g)


_drawn_inputs = setup_inputs


def setup_inputs(seed=0):
    import zlib

    import numpy as np

    out = dict(_drawn_inputs(seed))
    spreads = {}
    factors = {'norm1_g': 2.988,
     'norm2_g': 3.071,
     'router_g_b': 8.0,
     'router_e_b': 8.0,
     'da_subln_g': 3.582}
    for name, (base, spread) in spreads.items():
        noise = np.random.default_rng([zlib.crc32(name.encode()), seed]).standard_normal(out[name].shape)
        drawn = base * np.exp(spread * noise) if base else spread * noise
        out[name] = jnp.asarray(drawn.astype(out[name].dtype))
    for name, factor in factors.items():
        out[name] = (out[name] * factor).astype(out[name].dtype)
    return out
```

```python
import math
from contextlib import ExitStack

import concourse.bass as bass
from concourse import mybir

P = 128
T = 256
TT = T // P
D = 2048
KT = D // P
HEADS, HD = 8, 128
VD = 2 * HD
EXPERTS, GROUPS, PER_GROUP = 32, 4, 8
FF = 512
FT = FF // P
SLOTS = 32
QUAD = 4
MAIN = EXPERTS // QUAD
EXTRA = 16
ITEMS = EXPERTS + EXTRA
EPS = 1e-6
LAM_INIT = 0.8 - 0.6 * math.exp(-0.3 * 0)
RING = 6
CH = 4096
OUT_CH = 8
QKV_CH = 3 * HEADS
MOE_CH0 = QKV_CH + OUT_CH
ADA_BLK = 512
ADA_CH = 4
BIG = 1e30


class Chain:

    def __init__(self, engine, sem):
        self.engine, self.sem, self.base, self.n = engine, sem, 0, 0

    def link(self, ins):
        self.n += 1
        ins.then_inc(self.sem, 1)
        self.engine.wait_ge(self.sem, self.base + self.n)

    def start_loop(self, turn, per_turn):
        self.before, self.per_turn = self.base + self.n, per_turn
        self.base, self.n = turn * per_turn + self.before, 0

    def end_loop(self, turns):
        assert self.n == self.per_turn, (self.n, self.per_turn)
        self.base, self.n = self.before + turns * self.per_turn, 0


def encoder_layer(nc, x, c, ada_w, ada_b, norm1_g, norm2_g, router_g_w, router_g_b, router_e_w, router_e_b,
                  moe_w_gu, moe_w_d, da_w_in, da_w_out, da_lam_q1, da_lam_k1, da_lam_q2, da_lam_k2,
                  da_subln_g, final_g, out):
    f32, i32 = mybir.dt.float32, mybir.dt.int32
    ALU, ACT, AX = mybir.AluOpType, mybir.ActivationFunctionType, mybir.AxisListType
    X = AX.X

    ctx = ExitStack()
    with ctx:
        def sb(name, shape, dt=f32):
            return ctx.enter_context(nc.sbuf_tensor(name, shape, dt))

        def sem(name):
            return ctx.enter_context(nc.semaphore(name))

        ring = sb("ring", [P, RING, CH])
        ada_ring = sb("ada_ring", [P, ADA_CH, 2048])
        region_a = sb("region_a", [P, 4096])
        region_b = sb("region_b", [P, 4096])
        arena = sb("arena", [P, 6656])
        ident = sb("ident", [P, P])
        ones = sb("ones", [P, P])
        before = sb("before", [P, P])
        vcols = sb("vcols", [P, 70])
        adab = sb("adab", [P, 96])
        mod = sb("mod", [P, 96])
        a1 = sb("a1", [P, KT])
        a2 = sb("a2", [P, KT])
        silu_c = sb("silu_c", [P, KT])
        router_w = sb("router_w", [P, KT, GROUPS + EXPERTS])
        router_b = sb("router_b", [P, GROUPS + EXPERTS])
        slot_no = sb("slot_no", [P, SLOTS])
        stat = sb("stat", [P, 48])

        x_tok = region_a[:].rearrange("p (a d) -> p a d", a=TT)
        attn_t = region_a[:].rearrange("p (k t) -> p k t", k=KT)
        h2_t = attn_t
        y_acc = x_tok
        h_t = region_b[:].rearrange("p (k t) -> p k t", k=KT)
        x_res = region_b[:].rearrange("p (a d) -> p a d", a=TT)
        xn = ada_ring[:, 0:2, :]
        x_items = ada_ring[:, 2, :].rearrange("p (k s) -> p k s", k=KT)
        diag = ada_ring[:, 3, :].rearrange("p (k s) -> p k s", k=KT)
        gate1 = ada_ring[:, 2, :]

        def carve(start, *shape):
            n = math.prod(shape)
            v = arena[:, start:start + n]
            if len(shape) == 2:
                v = v.rearrange("p (a b) -> p a b", a=shape[0])
            if len(shape) == 3:
                v = v.rearrange("p (a b c) -> p a b c", a=shape[0], b=shape[1])
            return v

        q_t = carve(0, 2, 2, T)
        k_t = carve(1024, 2, 2, T)
        v_tok = carve(2048, 2, TT, VD)
        prob = carve(3072, TT, 2, T)
        prob_t = carve(4096, TT, TT, P)
        neg_dist = carve(4608, TT, T)
        o_norm = carve(5120, TT, VD)
        acc = carve(5632, 2, ADA_BLK)
        raw_vecs, raw_adab = o_norm[:, 0, 0:P], o_norm[:, 1, 0:P]
        o_items = carve(0, D)
        over = [carve(512 * i, EXTRA, EXPERTS) for i in range(3)]
        gate2 = carve(2048, D)
        sel = carve(4096, TT, QUAD, SLOTS)
        sel_w = carve(4352, TT, QUAD, SLOTS)
        sel_t = carve(4608, TT, P)
        hid_s = [carve(4864 + 128 * i, P) for i in range(4)]
        hid_t = carve(5376, FT, SLOTS)
        y_tmp = carve(5504, TT, T)
        rank1 = carve(6016, TT, ITEMS)
        weight = carve(6112, TT, ITEMS)
        rt = carve(6208, 448)
        logits = rt[:, 0:72].rearrange("p (a n) -> p a n", a=TT)
        by_group = rt[:, 72:136].rearrange("p (a n) -> p a n", a=TT * GROUPS)
        chosen = rt[:, 136:200].rearrange("p (a n) -> p a n", a=TT)
        e_log, e_log2, e_hot1, e_hot2 = (rt[:, 200 + 16 * i:216 + 16 * i].rearrange("p (a n) -> p a n", a=TT)
                                         for i in range(4))
        g_hot, rt_exp_in = (rt[:, 264 + 8 * i:272 + 8 * i].rearrange("p (a n) -> p a n", a=TT) for i in range(2))
        r_top, r_got, r_e1, r_e2, rt_gap = (rt[:, 280 + 2 * i:282 + 2 * i] for i in range(5))
        back8 = rt[:, 290:298]
        rt_n = [rt[:, 298 + 32 * i:330 + 32 * i] for i in range(4)]
        item_no, item_a, item_b = rt[:, 0:16], rt[:, 16:32], rt[:, 32:48]
        extra_i = sb("extra_i", [P, EXTRA + 1], i32)

        psum = ctx.enter_context(nc.psum_tensor("psum", [P, 8, 512], f32))
        B_Q, B_K, B_V, B_S, B_AT, B_O, B_MOD = 0, 1, 2, 3, 5, 6, 7
        B_G, B_GU, B_HT, B_D = 0, 4, 5, 6

        C_G, N1_G, N2_G, F_G, SUB_G, LAM = 0, 16, 32, 48, 64, 66
        SH1, SC1, G1, SH2, SC2, G2 = (KT * i for i in range(6))
        ssq, rstd = stat[:, 0:2], stat[:, 2:4]
        neg_max = stat[:, 4:8].rearrange("p (a b) -> p a b", a=2)
        den = stat[:, 8:12].rearrange("p (a b) -> p a b", a=2)
        rden = stat[:, 12:16].rearrange("p (a b) -> p a b", a=2)
        neg_lam = stat[:, 16:17]
        lam_tmp = stat[:, 17:21]
        osq, omid = stat[:, 21:23], stat[:, 23:25]
        ssq8 = stat[:, 26:42].rearrange("p (a b) -> p a b", a=2)

        w_loaded = [sem(f"w_loaded{i}") for i in range(RING)]
        w_used = sem("w_used")
        ada_loaded = [sem(f"ada_loaded{i}") for i in range(ADA_CH)]
        ada_used = sem("ada_used")
        vecs_loaded, x_loaded, router_loaded, x_again = map(sem, ("vecs_loaded", "x_loaded", "router_loaded",
                                                                  "x_again"))
        consts_step, consts_ready = sem("consts_step"), sem("consts_ready")
        dist_ready = sem("dist_ready")
        dve_step, act_step = sem("dve_step"), sem("act_step")
        vecs_transposed, cols_ready = sem("vecs_transposed"), sem("cols_ready")
        silu_exp, silu_ready = sem("silu_exp"), sem("silu_ready")
        lam_prod, lam_summed, lam_exp = sem("lam_prod"), sem("lam_summed"), sem("lam_exp")
        x_squared, x_mean, x_root, x_scaled = map(sem, ("x_squared", "x_mean", "x_root", "x_scaled"))
        x_transposed, x_copied = sem("x_transposed"), sem("x_copied")
        mod_summed, mod_ready = sem("mod_summed"), sem("mod_ready")
        h_ready = sem("h_ready")
        qkv_ready = sem("qkv_ready")
        s_done, s_read, max_ready, e_done, a_ready = map(sem, ("s_done", "s_read", "max_ready", "e_done", "a_ready"))
        at_done, at_copied, o_done, o_squared, o_mean, o_root, o_rstd, o_normed, ot_done, ot_copied = map(
            sem, ("at_done", "at_copied", "o_done", "o_squared", "o_mean", "o_root", "o_rstd", "o_normed",
                  "ot_done", "ot_copied"))
        diag_ready, gate_spread, gate_ready = sem("diag_ready"), sem("gate_spread"), sem("gate_ready")
        y_read, x1_ready, x1_squared = sem("y_read"), sem("x1_ready"), sem("x1_squared")
        x1_mean, x1_root, x1_rstd = sem("x1_mean"), sem("x1_root"), sem("x1_rstd")
        xn_dve, xn_act, h2_transposed, h2_dve, h2_act = map(sem, ("xn_dve", "xn_act", "h2_transposed", "h2_dve",
                                                                  "h2_act"))
        logits_done, shifted, route_exp, assigned, ranked, tables_ready = map(
            sem, ("logits_done", "shifted", "route_exp", "assigned", "ranked", "tables_ready"))
        sel_ready, selt_done, selt_copied, gathered, items_ready = map(
            sem, ("sel_ready", "selt_done", "selt_copied", "gathered", "items_ready"))
        gu_done, gate_exp, hid_ready, ht_done, ht_copied, d_done, o_dve, o_act, y_done, y_added = map(
            sem, ("gu_done", "gate_exp", "hid_ready", "ht_done", "ht_copied", "d_done", "o_dve", "o_act",
                  "y_done", "y_added"))
        x2_ready, x2_squared, x2_mean, x2_root, fin_spread, out_ready, stored, fin_step = map(
            sem, ("x2_ready", "x2_squared", "x2_mean", "x2_root", "fin_spread", "out_ready", "stored", "fin_step"))

        w_in = da_w_in[0].rearrange("(k p) n -> p k n", p=P)
        w_out = da_w_out[0].rearrange("(k p) n -> p k n", p=P)
        w_ada = ada_w[0].rearrange("(k p) n -> p k n", p=P)

        def w_gu(e):
            return moe_w_gu[0, bass.ds(e, 1), :, :].rearrange("e (k p) n -> p (e k) n", p=P)

        def w_d(e):
            return moe_w_d[0, bass.ds(e, 1), :, :].rearrange("e (k p) n -> p (e k) n", p=P)

        def slot16(s):
            return ring[:, s, :].rearrange("p (k n) -> p k n", k=KT)

        def moe_slot(j):
            return (MOE_CH0 + j) % RING

        def moe_loads(m, j):
            return m + (MOE_CH0 + j) // RING + 1

        block = ctx.enter_context(nc.Block())

        @block.sync
        def _(sp):
            for row, v, n in ((C_G, c[0], KT), (N1_G, norm1_g[0], KT), (N2_G, norm2_g[0], KT), (F_G, final_g, KT),
                              (SUB_G, da_subln_g[0], 2), (LAM, da_lam_q1[0], 1), (LAM + 1, da_lam_q2[0], 1),
                              (LAM + 2, da_lam_k1[0], 1), (LAM + 3, da_lam_k2[0], 1)):
                sp.dma_start(raw_vecs[row:row + n, :], v.rearrange("(k p) -> k p", p=P)).then_inc(vecs_loaded, 16)
            sp.dma_start(raw_adab[0:96, :], ada_b[0].rearrange("(k p) -> k p", p=P)).then_inc(vecs_loaded, 16)
            sp.dma_start(x_tok, x[0].rearrange("(a p) d -> p a d", p=P)).then_inc(x_loaded, 16)
            sp.dma_start(router_w[:, :, 0:GROUPS],
                         router_g_w[0].rearrange("(k p) n -> p k n", p=P)).then_inc(router_loaded, 16)
            sp.dma_start(router_w[:, :, GROUPS:],
                         router_e_w[0].rearrange("(k p) n -> p k n", p=P)).then_inc(router_loaded, 16)
            sp.dma_start(router_b[:, 0:GROUPS], router_g_b[0:1, :].to_broadcast([P, GROUPS])).then_inc(router_loaded, 16)
            sp.dma_start(router_b[:, GROUPS:],
                         router_e_b[0:1, :].to_broadcast([P, EXPERTS])).then_inc(router_loaded, 16)

            def load_head(h, par):
                for j in range(3):
                    if not isinstance(h, int):
                        sp.wait_ge(w_used, h * 3 + (j - RING + 1))
                    sp.dma_start(slot16(3 * par + j), w_in[:, :, bass.ds(h * VD + D * j, VD)])\
                        .then_inc(w_loaded[3 * par + j], 16)

            sp.wait_ge(ada_used, 24)
            load_head(0, 0)
            load_head(1, 1)
            with sp.Fori(1, HEADS // 2) as pair:
                load_head(pair * 2, 0)
                load_head(pair * 2 + 1, 1)
            for ch in range(OUT_CH):
                n = QKV_CH + ch
                sp.wait_ge(w_used, n - RING + 1)
                sp.dma_start(slot16(n % RING), w_out[:, :, VD * ch:VD * (ch + 1)]).then_inc(w_loaded[n % RING], 16)

            def load_item(m, e):
                gu, dn = w_gu(e), w_d(e)
                for j in range(RING):
                    sp.wait_ge(w_used, m * RING + (MOE_CH0 + j - RING + 1))
                    s = moe_slot(j)
                    if j < 4:
                        sp.dma_start(ring[:, s, :].rearrange("p (k n) -> p k n", k=4),
                                     gu[:, 4 * j:4 * j + 4, :]).then_inc(w_loaded[s], 16)
                    else:
                        sp.dma_start(ring[:, s, :].rearrange("p (k n) -> p k n", k=2),
                                     dn[:, 2 * (j - 4):2 * (j - 4) + 2, :]).then_inc(w_loaded[s], 16)

            with sp.Fori(0, EXPERTS) as m:
                load_item(m, m)
            sp.wait_ge(tables_ready, 1)
            extra_groups = sp.value_load(extra_i[0:1, EXTRA:EXTRA + 1], min_val=0, max_val=EXTRA // QUAD)
            with sp.Fori(0, EXTRA // QUAD) as g:
                with sp.If(g < extra_groups):
                    for j in range(QUAD):
                        e = sp.value_load(extra_i[0:1, bass.ds(g * QUAD + j, 1)], min_val=0, max_val=EXPERTS - 1)
                        load_item(g * QUAD + (EXPERTS + j), e)
                sp.end_ifs()
            for a in range(TT):
                sp.wait_ge(out_ready, a + 1)
                sp.dma_start(out[0, P * a:P * (a + 1), :], x_res[:, a, :]).then_inc(stored, 16)
            sp.wait_ge(stored, 16 * TT)

        @block.gpsimd
        def _(gp):
            step = Chain(gp, consts_step)
            nc.gpsimd.memset(ones[:], 1.0).then_inc(consts_ready, 1)
            step.link(nc.gpsimd.memset(ident[:], 0.0))
            nc.gpsimd.affine_select(out=ident[:], in_=ident[:], compare_op=ALU.not_equal, fill=1.0, base=0,
                                    pattern=[[-1, P]], channel_multiplier=1).then_inc(consts_ready, 1)
            step.link(nc.gpsimd.memset(before[:], 0.0))
            nc.gpsimd.affine_select(out=before[:], in_=before[:], compare_op=ALU.is_ge, fill=1.0, base=0,
                                    pattern=[[-1, P]], channel_multiplier=1).then_inc(consts_ready, 1)
            nc.gpsimd.iota(slot_no[:], pattern=[[1, SLOTS]], base=1, channel_multiplier=0,
                           allow_small_or_imprecise_dtypes=True).then_inc(consts_ready, 1)
            nc.gpsimd.iota(neg_dist, pattern=[[P, TT], [-1, T]], base=0, channel_multiplier=1,
                           allow_small_or_imprecise_dtypes=True).then_inc(dist_ready, 1)

            def load_ada(b, cols):
                for j in range(ADA_CH):
                    if not (isinstance(b, int) and b == 0):
                        gp.wait_ge(ada_used, b * ADA_CH + (j - ADA_CH + 1))
                    gp.dma_start(ada_ring[:, j, :].rearrange("p (k n) -> p k n", k=4),
                                 w_ada[:, 4 * j:4 * j + 4, bass.ds(cols, ADA_BLK)]).then_inc(ada_loaded[j], 16)

            load_ada(0, 0)
            load_ada(1, D)
            with gp.Fori(1, 4) as m:
                load_ada(m * 2, m * ADA_BLK)
                load_ada(m * 2 + 1, m * ADA_BLK + D)
            with gp.Fori(8, 24) as b:
                load_ada(b, b * ADA_BLK)
            gp.wait_ge(ada_used, 24 * ADA_CH)
            gp.wait_ge(mod_ready, 12)
            nc.gpsimd.tensor_tensor(diag, ident[:].unsqueeze(1).to_broadcast([P, KT, P]),
                                    mod[:, G1:G1 + KT].unsqueeze(2).to_broadcast([P, KT, P]), ALU.mult)\
                .then_inc(diag_ready, 1)
            gp.wait_ge(w_used, QKV_CH)
            gp.dma_start(x_res, x[0].rearrange("(a p) d -> p a d", p=P)).then_inc(x_again, 16)
            gp.wait_ge(gate_spread, 4)
            gp.wait_ge(mod_ready, 24)
            nc.gpsimd.tensor_tensor(diag, ident[:].unsqueeze(1).to_broadcast([P, KT, P]),
                                    mod[:, G2:G2 + KT].unsqueeze(2).to_broadcast([P, KT, P]), ALU.mult)\
                .then_inc(diag_ready, 1)
            gp.wait_ge(gate_spread, 8)
            nc.gpsimd.tensor_tensor(diag, ident[:].unsqueeze(1).to_broadcast([P, KT, P]),
                                    vcols[:, F_G:F_G + KT].unsqueeze(2).to_broadcast([P, KT, P]), ALU.mult)\
                .then_inc(diag_ready, 1)

        @block.tensor
        def _(pe):
            mm = nc.tensor.matmul
            pe.wait_ge(vecs_loaded, 160)
            pe.wait_ge(consts_ready, 4)
            nc.tensor.transpose(psum[:, B_MOD, 0:70], raw_vecs[0:70, :], ident[0:70, 0:70])\
                .then_inc(vecs_transposed, 1)
            nc.tensor.transpose(psum[:, B_MOD, 128:224], raw_adab[0:96, :], ident[0:96, 0:96])\
                .then_inc(vecs_transposed, 1)
            pe.wait_ge(lam_prod, 1)
            mm(psum[:, B_O, 0:2], ones[:], lam_tmp[:, 0:2], start=True, stop=True).then_inc(lam_summed, 1)

            def sum_mod(b, par):
                pe.wait_ge(ada_used, b * ADA_CH + ADA_CH)
                if isinstance(b, int) and b == 0:
                    pe.wait_ge(cols_ready, 2)
                else:
                    pe.wait_ge(mod_ready, b)
                for j in range(4):
                    last = mm(psum[:, B_MOD, 4 * par + j:4 * par + j + 1], acc[:, par, P * j:P * (j + 1)],
                              ones[:, 0:1], start=True, stop=True)
                last.then_inc(mod_summed, 1)

            sum_mod(0, 0)
            for r in range(8):
                if r == 0:
                    pe.wait_ge(x_scaled, 2)
                if r >= 4:
                    pe.wait_ge(x_copied, r - 3)
                for k in (2 * r, 2 * r + 1):
                    for a in range(TT):
                        at = (k % 2) * T + a * P
                        last = nc.tensor.transpose(psum[:, r % 4, at:at + P], x_tok[:, a, P * k:P * (k + 1)], ident[:])
                last.then_inc(x_transposed, 1)
            for b in range(1, 8):
                sum_mod(b, b % 2)

            def scores(h, par):
                pe.wait_ge(qkv_ready, h * 3 + 2)
                for a in range(TT):
                    if not (isinstance(h, int) and h == 0):
                        pe.wait_ge(s_read, h * 2 + (a - 1))
                    for i in range(2):
                        last = mm(psum[:, B_S + a, T * i:T * (i + 1)], q_t[:, par, i, P * a:P * (a + 1)],
                                  k_t[:, par, i, :], start=True, stop=True)
                    last.then_inc(s_done, 1)

            def transpose_probs(h):
                if not (isinstance(h, int) and h == 0):
                    pe.wait_ge(ot_copied, h * 2)
                for a in range(TT):
                    pe.wait_ge(a_ready, h * 2 + (a + 1))
                    for kk in range(TT):
                        at = (TT * a + kk) * P
                        last = nc.tensor.transpose(psum[:, B_AT, at:at + P], prob[:, a, 0, P * kk:P * (kk + 1)],
                                                   ident[:])
                last.then_inc(at_done, 1)

            def attend(h, par):
                pe.wait_ge(at_copied, h + 1)
                pe.wait_ge(qkv_ready, h * 3 + 3)
                for a in range(TT):
                    for kk in range(TT):
                        last = mm(psum[:, B_O, VD * a:VD * (a + 1)], prob_t[:, a, kk, :], v_tok[:, par, kk, :],
                                  start=kk == 0, stop=kk == TT - 1)
                last.then_inc(o_done, 1)

            def transpose_out(h):
                for a in range(TT):
                    pe.wait_ge(o_normed, h * 2 + (a + 1))
                    for half in range(2):
                        at = half * T + a * P
                        last = nc.tensor.transpose(psum[:, B_AT, at:at + P], o_norm[:, a, P * half:P * (half + 1)],
                                                   ident[:])
                last.then_inc(ot_done, 1)

            def qk_product(h, par, j):
                s = 3 * par + j
                pe.wait_ge(w_loaded[s], w_turn(h, par))
                if not (isinstance(h, int) and h == 0):
                    pe.wait_ge(qkv_ready, h * 3 + (j - 2))
                for i in range(2):
                    for k in range(KT):
                        if isinstance(h, int) and h == 0 and j == 0 and i == 0 and k % 4 == 0:
                            pe.wait_ge(h_ready, k // 4 + 1)
                        last = mm(psum[:, B_Q + j, T * i:T * (i + 1)], slot16(s)[:, k, P * i:P * (i + 1)],
                                  h_t[:, k, :], start=k == 0, stop=k == KT - 1)
                last.then_inc(w_used, 1)

            def v_product(h, par):
                s = 3 * par + 2
                pe.wait_ge(w_loaded[s], w_turn(h, par))
                if not (isinstance(h, int) and h == 0):
                    pe.wait_ge(qkv_ready, h * 3)
                for a in range(TT):
                    for k in range(KT):
                        last = mm(psum[:, B_V, VD * a:VD * (a + 1)], h_t[:, k, P * a:P * (a + 1)],
                                  slot16(s)[:, k, :], start=k == 0, stop=k == KT - 1)
                last.then_inc(w_used, 1)

            def w_turn(h, par):
                return 16 if isinstance(h, int) else (h - par) * 8 + 16

            def head(h, par):
                prev = not (isinstance(h, int) and h == 0)
                if prev:
                    scores(h - 1, 1 - par)
                qk_product(h, par, 0)
                if prev:
                    transpose_probs(h - 1)
                qk_product(h, par, 1)
                sum_mod(h * 2 + 8, 0)
                if prev:
                    attend(h - 1, 1 - par)
                v_product(h, par)
                if prev:
                    transpose_out(h - 1)
                sum_mod(h * 2 + 9, 1)

            head(0, 0)
            head(1, 1)
            with pe.Fori(1, HEADS // 2) as pair:
                head(pair * 2, 0)
                head(pair * 2 + 1, 1)
            last_head = HEADS - 1
            scores(last_head, 1)
            pe.wait_ge(diag_ready, 1)
            pe.wait_ge(qkv_ready, QKV_CH)
            pe.wait_ge(mod_ready, 24)
            for n, b in enumerate((B_Q, B_K, B_V, B_MOD)):
                mm(psum[:, b, :], ones[:], diag[:, 4 * n:4 * n + 4, :].rearrange("p a b -> p (a b)"),
                   start=True, stop=True).then_inc(gate_spread, 1)
            transpose_probs(last_head)
            attend(last_head, 1)
            transpose_out(last_head)
            pe.wait_ge(ot_copied, 2 * HEADS)
            for ch in range(OUT_CH):
                n = QKV_CH + ch
                pe.wait_ge(w_loaded[n % RING], 16 * (n // RING + 1))
                if ch >= 4:
                    pe.wait_ge(y_read, ch - 3)
                for a in range(TT):
                    for k in range(KT):
                        last = mm(psum[:, 3 + ch % 4, VD * a:VD * (a + 1)], attn_t[:, k, P * a:P * (a + 1)],
                                  slot16(n % RING)[:, k, :], start=k == 0, stop=k == KT - 1)
                last.then_inc(w_used, 1)
            pe.wait_ge(xn_dve, 1)
            pe.wait_ge(xn_act, 1)
            pe.wait_ge(gate_ready, 4)
            pe.wait_ge(y_read, OUT_CH)
            for r in range(8):
                if r >= 4 and r % 2 == 0:
                    pe.wait_ge(h2_act, r // 2 - 1)
                if r >= 4 and r % 2 == 1:
                    pe.wait_ge(h2_dve, r // 2 - 1)
                for k in (2 * r, 2 * r + 1):
                    for a in range(TT):
                        at = (k % 2) * T + a * P
                        last = nc.tensor.transpose(psum[:, r % 4, at:at + P], xn[:, a, P * k:P * (k + 1)], ident[:])
                last.then_inc(h2_transposed, 1)
            pe.wait_ge(h2_act, 4)
            pe.wait_ge(h2_dve, 4)
            pe.wait_ge(router_loaded, 64)
            for a in range(TT):
                for k in range(KT):
                    last = mm(psum[:, B_GU, 36 * a:36 * (a + 1)], h2_t[:, k, P * a:P * (a + 1)], router_w[:, k, :],
                              start=k == 0, stop=k == KT - 1)
            last.then_inc(logits_done, 1)
            pe.wait_ge(diag_ready, 2)
            for n in range(4):
                mm(psum[:, B_G + n, :], ones[:], diag[:, 4 * n:4 * n + 4, :].rearrange("p a b -> p (a b)"),
                   start=True, stop=True).then_inc(gate_spread, 1)
            pe.wait_ge(assigned, 1)
            mm(psum[:, B_HT, 0:32], before[:], chosen[:, 0, :], start=True, stop=True)
            mm(psum[:, B_HT, 32:64], before[:], chosen[:, 1, :], start=True, stop=False)
            mm(psum[:, B_HT, 32:64], ones[:], chosen[:, 0, :], start=False, stop=True)
            mm(psum[:, B_HT, 64:96], ones[:], chosen[:, 0, :], start=True, stop=False)
            mm(psum[:, B_HT, 64:96], ones[:], chosen[:, 1, :], start=False, stop=True).then_inc(ranked, 1)
            pe.wait_ge(gate_ready, 8)
            pe.wait_ge(tables_ready, 1)

            def moe_group(g, first=False):
                pe.wait_ge(sel_ready, g + 1)
                if not first:
                    pe.wait_ge(ht_copied, g * QUAD)
                for a in range(TT):
                    last = nc.tensor.transpose(psum[:, B_HT, P * a:P * (a + 1)],
                                               sel_w[:, a, :, :].rearrange("p a b -> p (a b)"), ident[:])
                last.then_inc(selt_done, 1)
                if not first:
                    pe.wait_ge(y_added, g * 8)
                for q in range(4):
                    for kk in range(4):
                        for a in range(TT):
                            k = 4 * q + kk
                            last = mm(psum[:, B_G + q, P * kk:P * (kk + 1)], xn[:, a, P * k:P * (k + 1)],
                                      sel[:, a, :, :].rearrange("p a b -> p (a b)"), start=a == 0, stop=a == TT - 1)
                    last.then_inc(gathered, 1)
                for i in range(QUAD):
                    m = g * QUAD + i
                    for j in range(4):
                        s = moe_slot(j)
                        w = ring[:, s, :].rearrange("p (k two n f) -> p k two n f", k=4, two=2, n=4)
                        pe.wait_ge(w_loaded[s], moe_loads(m, j) * 16)
                        if i == 0:
                            pe.wait_ge(items_ready, g * 4 + (j + 1))
                        if j == 0 and not (first and i == 0):
                            pe.wait_ge(hid_ready, m)
                        for kk in range(4):
                            k = 4 * j + kk
                            for n in range(4):
                                last = mm(psum[32 * n:32 * n + 32, B_GU, 0:256].rearrange("p (a b) -> p a b", a=2),
                                          x_items[:, k, SLOTS * i:SLOTS * (i + 1)], w[:, kk, :, n, :],
                                          start=k == 0, stop=k == KT - 1)
                        if j < 3:
                            last.then_inc(w_used, 1)
                    last.then_inc(w_used, 1)
                    pe.wait_ge(hid_ready, m + 1)
                    if i == 0:
                        pe.wait_ge(selt_copied, g + 1)
                    nc.tensor.transpose(psum[:, B_HT, 0:P], hid_s[3], ident[:]).then_inc(ht_done, 1)
                    pe.wait_ge(ht_copied, m + 1)
                    if not (first and i < 2):
                        pe.wait_ge(o_act, m * 2 - 2)
                        pe.wait_ge(o_dve, m * 2 - 2)
                    for j in (4, 5):
                        s = moe_slot(j)
                        w = ring[:, s, :].rearrange("p (k n f) -> p k n f", k=2, n=4)
                        pe.wait_ge(w_loaded[s], moe_loads(m, j) * 16)
                        for kk in range(2):
                            k = 2 * (j - 4) + kk
                            for n in range(4):
                                last = mm(psum[32 * n:32 * n + 32, B_D + i % 2, :], hid_t[:, k, :], w[:, kk, n, :],
                                          start=k == 0, stop=k == FT - 1)
                        last.then_inc(w_used, 1)
                pe.wait_ge(o_act, g * 2 * QUAD + 2 * QUAD)
                pe.wait_ge(o_dve, g * 2 * QUAD + 2 * QUAD)
                for a in range(TT):
                    for n in range(4):
                        if a:
                            pe.wait_ge(y_added, g * 8 + (n + 1))
                        mm(psum[:, B_G + n, :], sel_t[:, a, :], o_items[:, 512 * n:512 * (n + 1)],
                           start=True, stop=True).then_inc(y_done, 1)

            moe_group(0, first=True)
            with pe.Fori(1, MAIN) as g:
                moe_group(g)
            extra_groups = pe.value_load(extra_i[0:1, EXTRA:EXTRA + 1], min_val=0, max_val=EXTRA // QUAD)
            with pe.Fori(0, EXTRA // QUAD) as g:
                with pe.If(g < extra_groups):
                    moe_group(g + MAIN)
                pe.end_ifs()
            pe.wait_ge(diag_ready, 3)
            for n in range(4):
                last = mm(psum[:, B_GU + n, :], ones[:], diag[:, 4 * n:4 * n + 4, :].rearrange("p a b -> p (a b)"),
                          start=True, stop=True)
            last.then_inc(fin_spread, 1)

        @block.scalar
        def _(act):
            A = nc.scalar.activation
            act.wait_ge(cols_ready, 1)
            A(silu_c[:], vcols[:, C_G:C_G + KT], ACT.Exp, scale=-1.0).then_inc(silu_exp, 1)
            act.wait_ge(lam_summed, 1)
            A(lam_tmp[:, 2:4], psum[:, B_O, 0:2], ACT.Exp).then_inc(lam_exp, 1)
            act.wait_ge(x_loaded, 16)
            for a in range(TT):
                A(region_b[:, D * a:D * (a + 1)], x_tok[:, a, :], ACT.Square,
                  accum_out=ssq[:, a:a + 1]).then_inc(x_squared, 1)
            act.wait_ge(x_mean, 1)
            A(rstd, rstd, ACT.Sqrt).then_inc(x_root, 1)
            for r in range(8):
                act.wait_ge(x_transposed, r + 1)
                A(region_b[:, 512 * r:512 * (r + 1)], psum[:, r % 4, :], ACT.Copy).then_inc(x_copied, 1)

            def exps(h):
                for a in range(TT):
                    act.wait_ge(max_ready, h * 2 + (a + 1))
                    for i in range(2):
                        A(prob[:, a, i, :], prob[:, a, i, :], ACT.Exp, bias=neg_max[:, a, i:i + 1],
                          accum_out=den[:, a, i:i + 1]).then_inc(e_done, 1)

            def copy_qkv(h, par, j):
                dst = (q_t, k_t, v_tok)[j][:, par, :, :].rearrange("p a b -> p (a b)")
                act.wait_ge(w_used, h * 3 + (j + 1))
                A(dst, psum[:, B_Q + j, :], ACT.Copy, scale=HD ** -0.5 if j == 0 else 1.0).then_inc(qkv_ready, 1)

            def copy_probs(h):
                act.wait_ge(at_done, h + 1)
                A(prob_t.rearrange("p a b c -> p (a b c)"), psum[:, B_AT, :], ACT.Copy).then_inc(at_copied, 1)

            def norm_out(h):
                act.wait_ge(o_done, h + 1)
                for a in range(TT):
                    A(o_norm[:, a, :], psum[:, B_O, VD * a:VD * (a + 1)], ACT.Square,
                      accum_out=osq[:, a:a + 1]).then_inc(o_squared, 1)
                act.wait_ge(o_mean, h + 1)
                A(omid, omid, ACT.Sqrt).then_inc(o_root, 1)
                act.wait_ge(o_rstd, h + 1)
                for a in range(TT):
                    A(o_norm[:, a, :], psum[:, B_O, VD * a:VD * (a + 1)], ACT.Copy,
                      scale=omid[:, a:a + 1]).then_inc(o_normed, 1)

            def copy_out(h):
                act.wait_ge(ot_done, h + 1)
                for half in range(2):
                    A(attn_t[:, bass.ds(h * 2 + half, 1), :].rearrange("p a b -> p (a b)"),
                      psum[:, B_AT, T * half:T * (half + 1)], ACT.Copy,
                      scale=vcols[:, SUB_G + half:SUB_G + half + 1]).then_inc(ot_copied, 1)

            def head(h, par):
                prev = not (isinstance(h, int) and h == 0)
                if prev:
                    exps(h - 1)
                copy_qkv(h, par, 0)
                if prev:
                    copy_probs(h - 1)
                copy_qkv(h, par, 1)
                if prev:
                    norm_out(h - 1)
                copy_qkv(h, par, 2)
                if prev:
                    copy_out(h - 1)

            act.wait_ge(cols_ready, 3)
            head(0, 0)
            head(1, 1)
            with act.Fori(1, HEADS // 2) as pair:
                head(pair * 2, 0)
                head(pair * 2 + 1, 1)
            exps(HEADS - 1)
            for n, b in enumerate((B_Q, B_K, B_V, B_MOD)):
                act.wait_ge(gate_spread, n + 1)
                A(gate1[:, 512 * n:512 * (n + 1)], psum[:, b, :], ACT.Copy).then_inc(gate_ready, 1)
            copy_probs(HEADS - 1)
            norm_out(HEADS - 1)
            copy_out(HEADS - 1)
            for ch in range(OUT_CH):
                act.wait_ge(x1_ready, ch + 1)
                for a in range(TT):
                    if ch + a:
                        act.wait_ge(x1_squared, TT * ch + a)
                    A(gate2[:, 0:VD], x_res[:, a, VD * ch:VD * (ch + 1)], ACT.Square,
                      accum_out=ssq8[:, a, ch:ch + 1]).then_inc(x1_squared, 1)
            act.wait_ge(x1_mean, 1)
            A(rstd, rstd, ACT.Sqrt).then_inc(x1_root, 1)
            act.wait_ge(x1_rstd, 1)
            A(xn[:, 1, :], x_res[:, 1, :], ACT.Copy, scale=rstd[:, 1:2]).then_inc(xn_act, 1)
            for r in range(0, 8, 2):
                act.wait_ge(h2_transposed, r + 1)
                for k in (2 * r, 2 * r + 1):
                    at = (k % 2) * T
                    last = A(h2_t[:, k, :], psum[:, r % 4, at:at + T], ACT.Identity,
                             bias=mod[:, SH2 + k:SH2 + k + 1], scale=a2[:, k:k + 1])
                last.then_inc(h2_act, 1)
            act.wait_ge(shifted, 1)
            A(rt_exp_in, rt_exp_in, ACT.Exp).then_inc(route_exp, 1)
            act.wait_ge(shifted, 2)
            A(rt_gap, rt_gap, ACT.Exp).then_inc(route_exp, 1)
            act.wait_ge(x1_squared, OUT_CH * TT)
            for n in range(4):
                act.wait_ge(gate_spread, 5 + n)
                A(gate2[:, 512 * n:512 * (n + 1)], psum[:, B_G + n, :], ACT.Copy).then_inc(gate_ready, 1)
            act.wait_ge(tables_ready, 1)

            def moe_group(g):
                act.wait_ge(selt_done, g + 1)
                A(sel_t.rearrange("p a b -> p (a b)"), psum[:, B_HT, 0:T], ACT.Copy).then_inc(selt_copied, 1)
                for i in range(QUAD):
                    m = g * QUAD + i
                    act.wait_ge(w_used, m * RING + (MOE_CH0 + 4))
                    A(hid_s[0], psum[:, B_GU, 0:P], ACT.Exp, scale=-1.0).then_inc(gate_exp, 1)
                    act.wait_ge(ht_done, m + 1)
                    A(hid_t.rearrange("p a b -> p (a b)"), psum[:, B_HT, 0:P], ACT.Copy).then_inc(ht_copied, 1)
                    act.wait_ge(w_used, m * RING + (MOE_CH0 + 6))
                    for n in (0, 1):
                        A(o_items[32 * i:32 * i + 32, 512 * n:512 * (n + 1)],
                          psum[32 * n:32 * n + 32, B_D + i % 2, :], ACT.Copy).then_inc(o_act, 1)

            with act.Fori(0, MAIN) as g:
                moe_group(g)
            extra_groups = act.value_load(extra_i[0:1, EXTRA:EXTRA + 1], min_val=0, max_val=EXTRA // QUAD)
            with act.Fori(0, EXTRA // QUAD) as g:
                with act.If(g < extra_groups):
                    moe_group(g + MAIN)
                act.end_ifs()
            for a in range(TT):
                act.wait_ge(x2_ready, a + 1)
                A(y_acc[:, a, :], x_res[:, a, :], ACT.Square, accum_out=ssq[:, a:a + 1]).then_inc(x2_squared, 1)
                act.wait_ge(x2_mean, a + 1)
                A(rstd[:, a:a + 1], rstd[:, a:a + 1], ACT.Sqrt).then_inc(x2_root, 1)

        @block.vector
        def _(dve):
            v = nc.vector
            step = Chain(dve, dve_step)
            dve.wait_ge(vecs_transposed, 2)
            v.tensor_copy(vcols[:], psum[:, B_MOD, 0:70]).then_inc(cols_ready, 1)
            v.tensor_copy(adab[:], psum[:, B_MOD, 128:224]).then_inc(cols_ready, 1)
            dve.wait_ge(cols_ready, 1)
            v.tensor_tensor(lam_tmp[:, 0:2], vcols[:, LAM:LAM + 2], vcols[:, LAM + 2:LAM + 4], ALU.mult)\
                .then_inc(lam_prod, 1)
            dve.wait_ge(silu_exp, 1)
            step.link(v.tensor_scalar_add(silu_c[:], silu_c[:], 1.0))
            step.link(v.reciprocal(silu_c[:], silu_c[:]))
            step.link(v.tensor_tensor(silu_c[:], silu_c[:], vcols[:, C_G:C_G + KT], ALU.mult))
            v.tensor_scalar(vcols[:, SUB_G:SUB_G + 2], vcols[:, SUB_G:SUB_G + 2], 1.0 - LAM_INIT, None, ALU.mult)\
                .then_inc(cols_ready, 1)
            dve.wait_ge(dist_ready, 1)
            step.link(v.scalar_tensor_tensor(out=neg_dist, in0=neg_dist, scalar=-1.0, in1=neg_dist, op0=ALU.mult,
                                             op1=ALU.min))
            dve.wait_ge(lam_exp, 1)
            step.link(v.tensor_tensor(neg_lam, lam_tmp[:, 3:4], lam_tmp[:, 2:3], ALU.subtract))
            step.link(v.tensor_scalar_add(neg_lam, neg_lam, -LAM_INIT))

            def ada_chunk(b, par, j):
                dve.wait_ge(ada_loaded[j], b * 16 + 16)
                if j == 0 and not (isinstance(b, int) and b < 2):
                    dve.wait_ge(mod_summed, b - 1)
                for kk in range(4):
                    k = 4 * j + kk
                    w = ada_ring[:, j, ADA_BLK * kk:ADA_BLK * (kk + 1)]
                    if k == 0:
                        ins = v.tensor_scalar(acc[:, par, :], w, silu_c[:, k:k + 1], None, ALU.mult)
                    else:
                        ins = v.scalar_tensor_tensor(out=acc[:, par, :], in0=w, scalar=silu_c[:, k:k + 1],
                                                     in1=acc[:, par, :], op0=ALU.mult, op1=ALU.add)
                    if kk < 3:
                        step.link(ins)
                ins.then_inc(ada_used, 1)
                dve.wait_ge(ada_used, b * ADA_CH + (j + 1))

            def keep_mod(b, par, col):
                dve.wait_ge(mod_summed, b + 1)
                v.tensor_tensor(mod[:, bass.ds(col, 4)], psum[:, B_MOD, 4 * par:4 * par + 4],
                                adab[:, bass.ds(col, 4)], ALU.add).then_inc(mod_ready, 1)

            def early_col(b):
                return (b % 2) * SC1 + (b // 2) * 4

            def make_h(m):
                dve.wait_ge(mod_ready, 2 * m + 2)
                step.link(v.scalar_tensor_tensor(out=a1[:, 4 * m:4 * m + 4], in0=mod[:, SC1 + 4 * m:SC1 + 4 * m + 4],
                                                 scalar=1.0, in1=vcols[:, N1_G + 4 * m:N1_G + 4 * m + 4],
                                                 op0=ALU.add, op1=ALU.mult))
                for k in range(4 * m, 4 * m + 4):
                    last = v.tensor_scalar(h_t[:, k, :], h_t[:, k, :], a1[:, k:k + 1], mod[:, SH1 + k:SH1 + k + 1],
                                           ALU.mult, ALU.add)
                last.then_inc(h_ready, 1)

            for j in range(ADA_CH):
                ada_chunk(0, 0, j)
            dve.wait_ge(x_squared, TT)
            v.tensor_scalar(rstd, ssq, 1.0 / D, EPS, ALU.mult, ALU.add).then_inc(x_mean, 1)
            dve.wait_ge(x_root, 1)
            step.link(v.reciprocal(rstd, rstd))
            for a in range(TT):
                v.tensor_scalar(x_tok[:, a, :], x_tok[:, a, :], rstd[:, a:a + 1], None, ALU.mult).then_inc(x_scaled, 1)
            for b in range(1, 8):
                for j in range(ADA_CH):
                    ada_chunk(b, b % 2, j)
                keep_mod(b - 1, (b - 1) % 2, early_col(b - 1))
                if b == 7:
                    keep_mod(7, 1, early_col(7))
                if b == 3:
                    dve.wait_ge(x_copied, 8)
                if b % 2 and b > 1:
                    make_h(b // 2 - 1)
            make_h(3)

            def add_bias(h):
                step.link(v.tensor_scalar(neg_dist, neg_dist, 0.5, None, ALU.mult))
                for a in range(TT):
                    dve.wait_ge(s_done, h * 2 + (a + 1))
                    if a == 0 and not (isinstance(h, int) and h == 0):
                        dve.wait_ge(at_done, h)
                    v.tensor_tensor(prob[:, a, :, :], psum[:, B_S + a, :].rearrange("p (i k) -> p i k", i=2),
                                    neg_dist[:, a:a + 1, :].to_broadcast([P, 2, T]), ALU.add).then_inc(s_read, 1)
                    dve.wait_ge(s_read, h * 2 + (a + 1))
                    v.reduce_max(neg_max[:, a, :], prob[:, a, :, :], X, negate=True).then_inc(max_ready, 1)

            def combine(h):
                for a in range(TT):
                    dve.wait_ge(e_done, h * 4 + (2 * a + 2))
                    step.link(v.reciprocal(rden[:, a, :], den[:, a, :]))
                    step.link(v.tensor_tensor(rden[:, a, 1:2], rden[:, a, 1:2], neg_lam, ALU.mult))
                    step.link(v.tensor_scalar(prob[:, a, 0, :], prob[:, a, 0, :], rden[:, a, 0:1], None, ALU.mult))
                    v.scalar_tensor_tensor(out=prob[:, a, 0, :], in0=prob[:, a, 1, :], scalar=rden[:, a, 1:2],
                                           in1=prob[:, a, 0, :], op0=ALU.mult, op1=ALU.add).then_inc(a_ready, 1)

            def out_rstd(h):
                dve.wait_ge(o_squared, h * 2 + 2)
                v.tensor_scalar(omid, osq, 1.0 / VD, EPS, ALU.mult, ALU.add).then_inc(o_mean, 1)
                dve.wait_ge(o_root, h + 1)
                v.reciprocal(omid, omid).then_inc(o_rstd, 1)

            def head(h):
                prev = not (isinstance(h, int) and h == 0)
                b = h * 2 + 8
                if prev:
                    add_bias(h - 1)
                ada_chunk(b, 0, 0)
                ada_chunk(b, 0, 1)
                if prev:
                    combine(h - 1)
                ada_chunk(b, 0, 2)
                ada_chunk(b, 0, 3)
                if prev:
                    keep_mod(b - 1, 1, b * 4 - 4)
                for j in range(ADA_CH):
                    ada_chunk(b + 1, 1, j)
                keep_mod(b, 0, b * 4)
                if prev:
                    out_rstd(h - 1)

            head(0)
            head(1)
            per_head = 8 * 3 + 1 + 3 * TT
            with dve.Fori(1, HEADS // 2) as pair:
                step.start_loop(pair - 1, 2 * per_head)
                head(pair * 2)
                head(pair * 2 + 1)
            step.end_loop(HEADS // 2 - 1)
            add_bias(HEADS - 1)
            keep_mod(23, 1, 92)
            combine(HEADS - 1)
            dve.wait_ge(mod_ready, 24)
            step.link(v.scalar_tensor_tensor(out=a2[:], in0=mod[:, SC2:SC2 + KT], scalar=1.0,
                                             in1=vcols[:, N2_G:N2_G + KT], op0=ALU.add, op1=ALU.mult))
            out_rstd(HEADS - 1)
            dve.wait_ge(gate_ready, 4)
            dve.wait_ge(x_again, 16)
            for ch in range(OUT_CH):
                cols = slice(VD * ch, VD * (ch + 1))
                dve.wait_ge(w_used, QKV_CH + ch + 1)
                if ch:
                    dve.wait_ge(x1_ready, ch)
                v.tensor_tensor(y_tmp, psum[:, 3 + ch % 4, :].rearrange("p (a n) -> p a n", a=TT),
                                gate1[:, cols].unsqueeze(1).to_broadcast([P, TT, VD]), ALU.mult).then_inc(y_read, 1)
                dve.wait_ge(y_read, ch + 1)
                v.tensor_tensor(x_res[:, :, cols], x_res[:, :, cols], y_tmp, ALU.add).then_inc(x1_ready, 1)
            dve.wait_ge(x1_squared, OUT_CH * TT)
            step.link(v.reduce_sum(ssq, ssq8, X))
            v.tensor_scalar(rstd, ssq, 1.0 / D, EPS, ALU.mult, ALU.add).then_inc(x1_mean, 1)
            dve.wait_ge(x1_root, 1)
            v.reciprocal(rstd, rstd).then_inc(x1_rstd, 1)
            dve.wait_ge(x1_rstd, 1)
            v.tensor_scalar(xn[:, 0, :], x_res[:, 0, :], rstd[:, 0:1], None, ALU.mult).then_inc(xn_dve, 1)
            for r in range(1, 8, 2):
                dve.wait_ge(h2_transposed, r + 1)
                for k in (2 * r, 2 * r + 1):
                    at = (k % 2) * T
                    last = v.tensor_scalar(h2_t[:, k, :], psum[:, r % 4, at:at + T], a2[:, k:k + 1],
                                           mod[:, SH2 + k:SH2 + k + 1], ALU.mult, ALU.add)
                last.then_inc(h2_dve, 1)

            dve.wait_ge(logits_done, 1)
            dve.wait_ge(router_loaded, 64)
            step.link(v.tensor_tensor(logits, psum[:, B_GU, 0:72].rearrange("p (a n) -> p a n", a=TT),
                                      router_b[:].unsqueeze(1).to_broadcast([P, TT, 36]), ALU.add))
            lg = logits[:, :, 0:GROUPS]

            def first_max(hot, src, n, top, back, got):
                shape = [P, TT, n]
                step.link(v.reduce_max(top, src, X))
                step.link(v.tensor_tensor(hot, src, top.unsqueeze(2).to_broadcast(shape), ALU.is_equal))
                step.link(v.tensor_tensor(hot, hot, back.unsqueeze(1).to_broadcast(shape), ALU.mult))
                step.link(v.reduce_max(got, hot, X))
                step.link(v.tensor_tensor(hot, hot, got.unsqueeze(2).to_broadcast(shape), ALU.is_equal))

            step.link(v.tensor_scalar(back8, slot_no[:, 0:8], -1.0, 9.0, ALU.mult, ALU.add))
            first_max(g_hot, lg, GROUPS, r_top, back8[:, 4:8], r_got)
            v.tensor_tensor(rt_exp_in, lg, r_top.unsqueeze(2).to_broadcast([P, TT, GROUPS]), ALU.subtract)\
                .then_inc(shifted, 1)
            for a in range(TT):
                part = by_group[:, GROUPS * a:GROUPS * (a + 1), :]
                step.link(v.tensor_tensor(part, logits[:, a, GROUPS:].rearrange("p (g e) -> p g e", g=GROUPS),
                                          g_hot[:, a, :].unsqueeze(2).to_broadcast([P, GROUPS, PER_GROUP]),
                                          ALU.mult))
                step.link(v.reduce_sum(e_log[:, a, :], part.rearrange("p g e -> p e g"), X))
            first_max(e_hot1, e_log, PER_GROUP, r_e1, back8, r_got)
            step.link(v.scalar_tensor_tensor(out=e_log2, in0=e_hot1, scalar=-BIG, in1=e_log, op0=ALU.mult,
                                             op1=ALU.add))
            first_max(e_hot2, e_log2, PER_GROUP, r_e2, back8, r_got)
            v.tensor_tensor(rt_gap, r_e2, r_e1, ALU.subtract).then_inc(shifted, 1)
            step.link(v.tensor_tensor(e_log, e_hot1, e_hot2, ALU.add))

            def outer(dst, per_expert):
                for a in range(TT):
                    ins = v.tensor_tensor(dst[:, a, :].rearrange("p (g e) -> p g e", g=GROUPS),
                                          g_hot[:, a, :].unsqueeze(2).to_broadcast([P, GROUPS, PER_GROUP]),
                                          per_expert[:, a:a + 1, :].to_broadcast([P, GROUPS, PER_GROUP]), ALU.mult)
                    if a < TT - 1:
                        step.link(ins)
                return ins

            outer(chosen, e_log).then_inc(assigned, 1)
            dve.wait_ge(route_exp, 2)
            step.link(v.reduce_sum(r_top, rt_exp_in, X))
            step.link(v.reciprocal(r_top, r_top))
            step.link(v.tensor_scalar_add(r_got, rt_gap, 1.0))
            step.link(v.reciprocal(r_got, r_got))
            step.link(v.tensor_tensor(r_e1, r_top, r_got, ALU.mult))
            step.link(v.tensor_tensor(r_e2, r_e1, rt_gap, ALU.mult))
            step.link(v.tensor_tensor(e_hot1, e_hot1, r_e1.unsqueeze(2).to_broadcast([P, TT, PER_GROUP]), ALU.mult))
            step.link(v.tensor_tensor(e_hot2, e_hot2, r_e2.unsqueeze(2).to_broadcast([P, TT, PER_GROUP]), ALU.mult))
            step.link(v.tensor_tensor(e_hot1, e_hot1, e_hot2, ALU.add))
            step.link(outer(weight[:, :, 0:EXPERTS], e_hot1))
            dve.wait_ge(ranked, 1)
            step.link(v.scalar_tensor_tensor(out=rank1[:, :, 0:EXPERTS],
                                             in0=psum[:, B_HT, 0:64].rearrange("p (a n) -> p a n", a=TT), scalar=1.0,
                                             in1=chosen, op0=ALU.add, op1=ALU.mult))

            n_over, counts, first, upto = rt_n
            step.link(v.tensor_copy(counts, psum[:, B_HT, 64:96]))
            step.link(v.tensor_scalar(n_over, counts, float(SLOTS), None, ALU.is_gt))
            for k in range(2, T // SLOTS):
                step.link(v.scalar_tensor_tensor(out=n_over, in0=counts, scalar=float(SLOTS * k), in1=n_over,
                                                 op0=ALU.is_gt, op1=ALU.add))
            src, dst = n_over, upto
            for sh in (1, 2, 4, 8, 16):
                step.link(v.tensor_copy(dst[:, 0:sh], src[:, 0:sh]))
                step.link(v.tensor_tensor(dst[:, sh:], src[:, sh:], src[:, 0:EXPERTS - sh], ALU.add))
                src, dst = dst, (first if dst is upto else upto)
            assert src is upto
            step.link(v.tensor_tensor(first, upto, n_over, ALU.subtract))
            own, tmp, tmp2 = over
            wide = [P, EXTRA, EXPERTS]
            step.link(v.tensor_scalar_add(item_no, slot_no[:, 0:EXTRA], -1.0))
            step.link(v.tensor_tensor(own, item_no.unsqueeze(2).to_broadcast(wide),
                                      first.unsqueeze(1).to_broadcast(wide), ALU.is_ge))
            step.link(v.tensor_tensor(tmp, item_no.unsqueeze(2).to_broadcast(wide),
                                      upto.unsqueeze(1).to_broadcast(wide), ALU.is_lt))
            step.link(v.tensor_tensor(own, own, tmp, ALU.mult))

            def pick(dst, table):
                step.link(v.tensor_tensor(tmp, own, table.unsqueeze(1).to_broadcast(wide), ALU.mult))
                step.link(v.reduce_sum(dst, tmp, X))

            pick(item_a, first)
            step.link(v.tensor_tensor(item_a, slot_no[:, 0:EXTRA], item_a, ALU.subtract))
            for a in range(TT):
                pick(item_b, rank1[:, a, 0:EXPERTS])
                step.link(v.scalar_tensor_tensor(out=rank1[:, a, EXPERTS:], in0=item_a, scalar=-float(SLOTS),
                                                 in1=item_b, op0=ALU.mult, op1=ALU.add))
                pick(weight[:, a, EXPERTS:], weight[:, a, 0:EXPERTS])
            step.link(v.tensor_scalar_add(first, slot_no[:], -1.0))
            pick(item_b, first)
            step.link(v.tensor_copy(extra_i[:, 0:EXTRA], item_b))
            step.link(v.tensor_scalar(item_a[:, 0:4], item_no[:, 0:4], float(QUAD), upto[:, EXPERTS - 1:EXPERTS],
                                      ALU.mult, ALU.is_lt))
            step.link(v.reduce_sum(item_b[:, 0:1], item_a[:, 0:4], X))
            step.link(v.tensor_copy(extra_i[:, EXTRA:EXTRA + 1], item_b[:, 0:1]))
            v.memset(region_a[:], 0.0).then_inc(tables_ready, 1)
            dve.wait_ge(tables_ready, 1)

            def moe_group(g, first_group=False):
                wide4 = [P, QUAD, SLOTS]
                for a in range(TT):
                    r = rank1[:, a, bass.ds(g * QUAD, QUAD)]
                    step.link(v.tensor_tensor(sel[:, a, :, :], slot_no[:].unsqueeze(1).to_broadcast(wide4),
                                              r.unsqueeze(2).to_broadcast(wide4), ALU.is_equal))
                for a in range(TT):
                    w = weight[:, a, bass.ds(g * QUAD, QUAD)]
                    ins = v.tensor_tensor(sel_w[:, a, :, :], sel[:, a, :, :], w.unsqueeze(2).to_broadcast(wide4),
                                          ALU.mult)
                    if a < TT - 1:
                        step.link(ins)
                ins.then_inc(sel_ready, 1)
                for q in range(4):
                    ks = slice(4 * q, 4 * q + 4)
                    dve.wait_ge(gathered, g * 4 + (q + 1))
                    step.link(v.tensor_tensor(x_items[:, ks, :],
                                              psum[:, B_G + q, :].rearrange("p (k s) -> p k s", k=4),
                                              a2[:, ks].unsqueeze(2).to_broadcast([P, 4, P]), ALU.mult))
                    v.tensor_tensor(x_items[:, ks, :], x_items[:, ks, :],
                                    mod[:, SH2 + 4 * q:SH2 + 4 * q + 4].unsqueeze(2).to_broadcast([P, 4, P]), ALU.add)\
                        .then_inc(items_ready, 1)
                for i in range(QUAD):
                    m = g * QUAD + i
                    dve.wait_ge(gate_exp, m + 1)
                    step.link(v.tensor_scalar_add(hid_s[1], hid_s[0], 1.0))
                    step.link(v.reciprocal(hid_s[2], hid_s[1]))
                    step.link(v.tensor_tensor(hid_s[1], hid_s[2], psum[:, B_GU, 0:P], ALU.mult))
                    v.tensor_tensor(hid_s[3], hid_s[1], psum[:, B_GU, P:2 * P], ALU.mult).then_inc(hid_ready, 1)
                    dve.wait_ge(w_used, m * RING + (MOE_CH0 + 6))
                    for n in (2, 3):
                        v.tensor_copy(o_items[32 * i:32 * i + 32, 512 * n:512 * (n + 1)],
                                      psum[32 * n:32 * n + 32, B_D + i % 2, :]).then_inc(o_dve, 1)
                for a in range(TT):
                    for n in range(4):
                        dve.wait_ge(y_done, g * 8 + (4 * a + n + 1))
                        cols = slice(512 * n, 512 * (n + 1))
                        v.tensor_tensor(y_acc[:, a, cols], y_acc[:, a, cols], psum[:, B_G + n, :], ALU.add)\
                            .then_inc(y_added, 1)
                dve.wait_ge(y_added, g * 8 + 8)
                v.memset(stat[:, 42:43], 0.0)

            per_group = 2 + 1 + 4 + 3 * QUAD
            with dve.Fori(0, MAIN) as g:
                step.start_loop(g, per_group)
                moe_group(g)
            step.end_loop(MAIN)
            extra_groups = dve.value_load(extra_i[0:1, EXTRA:EXTRA + 1], min_val=0, max_val=EXTRA // QUAD)
            with dve.Fori(0, EXTRA // QUAD) as g:
                with dve.If(g < extra_groups):
                    step.start_loop(g, per_group)
                    moe_group(g + MAIN)
                dve.end_ifs()
            step.end_loop(0)

            for a in range(TT):
                v.tensor_tensor(y_acc[:, a, :], y_acc[:, a, :], gate2, ALU.mult).then_inc(fin_step, 1)
                dve.wait_ge(fin_step, 3 * a + 1)
                v.tensor_tensor(x_res[:, a, :], x_res[:, a, :], y_acc[:, a, :], ALU.add).then_inc(x2_ready, 1)
                dve.wait_ge(x2_squared, a + 1)
                v.tensor_scalar(rstd[:, a:a + 1], ssq[:, a:a + 1], 1.0 / D, EPS, ALU.mult, ALU.add)\
                    .then_inc(x2_mean, 1)
                dve.wait_ge(x2_root, a + 1)
                v.reciprocal(rstd[:, a:a + 1], rstd[:, a:a + 1]).then_inc(fin_step, 1)
                dve.wait_ge(fin_step, 3 * a + 2)
                v.tensor_scalar(x_res[:, a, :], x_res[:, a, :], rstd[:, a:a + 1], None, ALU.mult).then_inc(fin_step, 1)
                dve.wait_ge(fin_step, 3 * a + 3)
                dve.wait_ge(fin_spread, 1)
                v.tensor_tensor(x_res[:, a, :], x_res[:, a, :],
                                psum[:, B_GU:B_GU + 4, :].rearrange("p a b -> p (a b)"), ALU.mult)\
                    .then_inc(out_ready, 1)


_INS = ['x', 'c', 'ada_w', 'ada_b', 'norm1_g', 'norm2_g', 'router_g_w', 'router_g_b', 'router_e_w', 'router_e_b',
        'moe_w_gu', 'moe_w_d', 'da_w_in', 'da_w_out', 'da_lam_q1', 'da_lam_k1', 'da_lam_q2', 'da_lam_k2',
        'da_subln_g', 'final_g']


def kernel(**inputs):
    import numpy as _np
    import concourse.bacc as _bacc
    from concourse import mybir as _mybir
    from concourse.bass_utils import run_bass_kernel_spmd as _run

    nc = _bacc.Bacc("TRN2", target_bir_lowering=False, num_devices=1)
    arrays, args = {}, []
    for name in _INS:
        a = _np.ascontiguousarray(inputs[name])
        arrays[f"in_{name}_dram"] = a
        args.append(nc.dram_tensor(f"in_{name}_dram", a.shape, _mybir.dt.from_np(a.dtype), kind="ExternalInput").ap())
    args.append(nc.dram_tensor("out_0_dram", inputs["x"].shape, _mybir.dt.float32, kind="ExternalOutput").ap())
    encoder_layer(nc, *args)
    r = _run(nc, [arrays], core_ids=[0])
    return r.results[0]["out_0_dram"]
```

```python
import math
from contextlib import ExitStack

import concourse.bass as bass
from concourse import mybir

P = 128
T = 256
TT = T // P
D = 2048
KT = D // P
HEADS, HD = 8, 128
VD = 2 * HD
EXPERTS, GROUPS, PER_GROUP = 32, 4, 8
FF = 512
FT = FF // P
SLOTS = 32
QUAD = 4
MAIN = EXPERTS // QUAD
EXTRA = 16
ITEMS = EXPERTS + EXTRA
EPS = 1e-6
LAM_INIT = 0.8 - 0.6 * math.exp(-0.3 * 0)
RING = 6
CH = 4096
OUT_CH = 8
QKV_CH = 3 * HEADS
MOE_CH0 = QKV_CH + OUT_CH
ADA_BLK = 512
ADA_CH = 4
BIG = 1e30


class Chain:

    def __init__(self, engine, sem):
        self.engine, self.sem, self.base, self.n = engine, sem, 0, 0

    def link(self, ins):
        self.n += 1
        ins.then_inc(self.sem, 1)
        self.engine.wait_ge(self.sem, self.base + self.n)

    def start_loop(self, turn, per_turn):
        self.before, self.per_turn = self.base + self.n, per_turn
        self.base, self.n = turn * per_turn + self.before, 0

    def end_loop(self, turns):
        assert self.n == self.per_turn, (self.n, self.per_turn)
        self.base, self.n = self.before + turns * self.per_turn, 0


def encoder_layer(nc, x, c, ada_w, ada_b, norm1_g, norm2_g, router_g_w, router_g_b, router_e_w, router_e_b,
                  moe_w_gu, moe_w_d, da_w_in, da_w_out, da_lam_q1, da_lam_k1, da_lam_q2, da_lam_k2,
                  da_subln_g, final_g, out):
    f32, i32 = mybir.dt.float32, mybir.dt.int32
    ALU, ACT, AX = mybir.AluOpType, mybir.ActivationFunctionType, mybir.AxisListType
    X = AX.X

    ctx = ExitStack()
    with ctx:
        def sb(name, shape, dt=f32):
            return ctx.enter_context(nc.sbuf_tensor(name, shape, dt))

        def sem(name):
            return ctx.enter_context(nc.semaphore(name))

        ring = sb("ring", [P, RING, CH])
        ada_ring = sb("ada_ring", [P, ADA_CH, 2048])
        region_a = sb("region_a", [P, 4096])
        region_b = sb("region_b", [P, 4096])
        arena = sb("arena", [P, 6656])
        ident = sb("ident", [P, P])
        ones = sb("ones", [P, P])
        before = sb("before", [P, P])
        vcols = sb("vcols", [P, 70])
        adab = sb("adab", [P, 96])
        mod = sb("mod", [P, 96])
        a1 = sb("a1", [P, KT])
        a2 = sb("a2", [P, KT])
        silu_c = sb("silu_c", [P, KT])
        router_w = sb("router_w", [P, KT, GROUPS + EXPERTS])
        router_b = sb("router_b", [P, GROUPS + EXPERTS])
        slot_no = sb("slot_no", [P, SLOTS])
        stat = sb("stat", [P, 48])

        x_tok = region_a[:].rearrange("p (a d) -> p a d", a=TT)
        attn_t = region_a[:].rearrange("p (k t) -> p k t", k=KT)
        y_acc = x_tok
        h_t = region_b[:].rearrange("p (k t) -> p k t", k=KT)
        x_res = region_b[:].rearrange("p (a d) -> p a d", a=TT)
        x1_t = ada_ring[:, 0, 0:1024].rearrange("p (a k t) -> p a k t", a=2, k=2)
        router_wa = ada_ring[:, 0, 1024:1600].rearrange("p (k n) -> p k n", k=KT)
        over = [ada_ring[:, 1, 512 * i:512 * (i + 1)].rearrange("p (a b) -> p a b", a=EXTRA) for i in range(3)]
        junk = ada_ring[:, 1, 1536:1792]
        final_gain = ada_ring[:, 0, :]
        x_items = ada_ring[:, 2, :].rearrange("p (k s) -> p k s", k=KT)
        diag = ada_ring[:, 3, :].rearrange("p (k s) -> p k s", k=KT)
        gate1 = ada_ring[:, 2, :]

        def carve(start, *shape):
            n = math.prod(shape)
            v = arena[:, start:start + n]
            if len(shape) == 2:
                v = v.rearrange("p (a b) -> p a b", a=shape[0])
            if len(shape) == 3:
                v = v.rearrange("p (a b c) -> p a b c", a=shape[0], b=shape[1])
            return v

        q_t = carve(0, 2, 2, T)
        k_t = carve(1024, 2, 2, T)
        v_tok = carve(2048, 2, TT, VD)
        prob = carve(3072, TT, 2, T)
        prob_t = carve(4096, TT, TT, P)
        neg_dist = carve(4608, TT, T)
        o_norm = carve(5120, TT, VD)
        acc = carve(5632, 2, ADA_BLK)
        raw_vecs, raw_adab = o_norm[:, 0, 0:P], o_norm[:, 1, 0:P]
        o_items = carve(0, D)
        gate2 = carve(2048, D)
        sel = carve(4096, TT, QUAD, SLOTS)
        sel_w = carve(4352, TT, QUAD, SLOTS)
        sel_t = carve(4608, TT, P)
        hid_s = [carve(4864 + 128 * i, P) for i in range(4)]
        hid_t = carve(5376, FT, SLOTS)
        y_tmp = carve(5504, TT, T)
        rank1 = carve(6016, TT, ITEMS)
        weight = carve(6112, TT, ITEMS)
        y_part = [ada_ring[:, 1, 512 * i:512 * (i + 1)] for i in range(2)]
        rt = carve(6208, 448)
        logits = rt[:, 0:72].rearrange("p (a n) -> p a n", a=TT)
        by_group = rt[:, 72:136].rearrange("p (a n) -> p a n", a=TT * GROUPS)
        chosen = rt[:, 136:200].rearrange("p (a n) -> p a n", a=TT)
        e_log, e_log2, e_hot1, e_hot2 = (rt[:, 200 + 16 * i:216 + 16 * i].rearrange("p (a n) -> p a n", a=TT)
                                         for i in range(4))
        g_hot, rt_exp_in = (rt[:, 264 + 8 * i:272 + 8 * i].rearrange("p (a n) -> p a n", a=TT) for i in range(2))
        r_top, r_got, r_e1, r_e2, rt_gap = (rt[:, 280 + 2 * i:282 + 2 * i] for i in range(5))
        back8 = rt[:, 290:298]
        rt_n = [rt[:, 298 + 32 * i:330 + 32 * i] for i in range(4)]
        item_no, item_a, item_b = rt[:, 0:16], rt[:, 16:32], rt[:, 32:48]
        extra_i = sb("extra_i", [P, EXTRA + 1], i32)

        psum = ctx.enter_context(nc.psum_tensor("psum", [P, 8, 512], f32))
        B_Q, B_K, B_V, B_S, B_AT, B_O, B_MOD = 0, 1, 2, 3, 5, 6, 7
        EARLY_BANK = (B_Q, B_K, B_V, B_AT, B_O)
        B_LOGIT = 2
        B_G, B_GU, B_HT, B_D = 0, 4, 5, 6

        C_G, N1_G, N2_G, F_G, SUB_G, LAM = 0, 16, 32, 48, 64, 66
        SH1, SC1, G1, SH2, SC2, G2 = (KT * i for i in range(6))
        ssq, rstd = stat[:, 0:2], stat[:, 2:4]
        neg_max = stat[:, 4:8].rearrange("p (a b) -> p a b", a=2)
        den = stat[:, 8:12].rearrange("p (a b) -> p a b", a=2)
        rden = stat[:, 12:16].rearrange("p (a b) -> p a b", a=2)
        neg_lam = stat[:, 16:17]
        lam_tmp = stat[:, 17:21]
        osq, omid = stat[:, 21:23], stat[:, 23:25]
        ssq8 = stat[:, 26:42].rearrange("p (a b) -> p a b", a=2)

        w_loaded = [sem(f"w_loaded{i}") for i in range(RING)]
        w_used = sem("w_used")
        ada_loaded = [sem(f"ada_loaded{i}") for i in range(ADA_CH)]
        ada_used = sem("ada_used")
        vecs_loaded, x_loaded, router_loaded, x_again = map(sem, ("vecs_loaded", "x_loaded", "router_loaded",
                                                                  "x_again"))
        consts_step, consts_ready = sem("consts_step"), sem("consts_ready")
        dist_ready, spare_ready = sem("dist_ready"), sem("spare_ready")
        dve_step, act_step = sem("dve_step"), sem("act_step")
        vecs_transposed, cols_ready = sem("vecs_transposed"), sem("cols_ready")
        silu_exp, silu_ready = sem("silu_exp"), sem("silu_ready")
        lam_prod, lam_summed, lam_exp = sem("lam_prod"), sem("lam_summed"), sem("lam_exp")
        x_squared, x_mean, x_root, x_scaled = map(sem, ("x_squared", "x_mean", "x_root", "x_scaled"))
        x_transposed, x_copied = sem("x_transposed"), sem("x_copied")
        mod_summed, mod_ready = sem("mod_summed"), sem("mod_ready")
        h_ready = sem("h_ready")
        qkv_ready = sem("qkv_ready")
        s_done, s_read, max_ready, e_done, a_ready = map(sem, ("s_done", "s_read", "max_ready", "e_done", "a_ready"))
        at_done, at_copied, o_done, o_squared, o_mean, o_root, o_rstd, o_normed, ot_done, ot_copied = map(
            sem, ("at_done", "at_copied", "o_done", "o_squared", "o_mean", "o_root", "o_rstd", "o_normed",
                  "ot_done", "ot_copied"))
        diag_ready, gate_spread, gate_ready = sem("diag_ready"), sem("gate_spread"), sem("gate_ready")
        y_read, x1_ready, x1_squared = sem("y_read"), sem("x1_ready"), sem("x1_squared")
        x1_mean, x1_root = sem("x1_mean"), sem("x1_root")
        x1_transposed, x1_copied, logits_added, router_scaled, bias_spread, y_started = map(
            sem, ("x1_transposed", "x1_copied", "logits_added", "router_scaled", "bias_spread", "y_started"))
        shifted, route_exp, assigned, ranked, tables_ready = map(
            sem, ("shifted", "route_exp", "assigned", "ranked", "tables_ready"))
        sel_ready, selt_done, selt_copied, gathered, items_ready = map(
            sem, ("sel_ready", "selt_done", "selt_copied", "gathered", "items_ready"))
        gu_done, gate_exp, hid_ready, ht_done, ht_copied, o_dve, o_act, y_done, y_taken, y_added = map(
            sem, ("gu_done", "gate_exp", "hid_ready", "ht_done", "ht_copied", "o_dve", "o_act",
                  "y_done", "y_taken", "y_added"))
        x2_ready, x2_squared, x2_mean, x2_root, out_ready, stored, fin_step = map(
            sem, ("x2_ready", "x2_squared", "x2_mean", "x2_root", "out_ready", "stored", "fin_step"))

        w_in = da_w_in[0].rearrange("(k p) n -> p k n", p=P)
        w_out = da_w_out[0].rearrange("(k p) n -> p k n", p=P)
        w_ada = ada_w[0].rearrange("(k p) n -> p k n", p=P)

        def w_gu(e):
            return moe_w_gu[0, bass.ds(e, 1), :, :].rearrange("e (k p) n -> p (e k) n", p=P)

        def w_d(e):
            return moe_w_d[0, bass.ds(e, 1), :, :].rearrange("e (k p) n -> p (e k) n", p=P)

        def slot16(s):
            return ring[:, s, :].rearrange("p (k n) -> p k n", k=KT)

        def moe_slot(j):
            return (MOE_CH0 + j) % RING

        def moe_loads(m, j):
            return m + (MOE_CH0 + j) // RING + 1

        block = ctx.enter_context(nc.Block())

        @block.sync
        def _(sp):
            for row, v, n in ((C_G, c[0], KT), (N1_G, norm1_g[0], KT), (N2_G, norm2_g[0], KT), (F_G, final_g, KT),
                              (SUB_G, da_subln_g[0], 2), (LAM, da_lam_q1[0], 1), (LAM + 1, da_lam_q2[0], 1),
                              (LAM + 2, da_lam_k1[0], 1), (LAM + 3, da_lam_k2[0], 1)):
                sp.dma_start(raw_vecs[row:row + n, :], v.rearrange("(k p) -> k p", p=P)).then_inc(vecs_loaded, 16)
            sp.dma_start(raw_adab[0:96, :], ada_b[0].rearrange("(k p) -> k p", p=P)).then_inc(vecs_loaded, 16)
            sp.dma_start(x_tok, x[0].rearrange("(a p) d -> p a d", p=P)).then_inc(x_loaded, 16)
            sp.dma_start(router_w[:, :, 0:GROUPS],
                         router_g_w[0].rearrange("(k p) n -> p k n", p=P)).then_inc(router_loaded, 16)
            sp.dma_start(router_w[:, :, GROUPS:],
                         router_e_w[0].rearrange("(k p) n -> p k n", p=P)).then_inc(router_loaded, 16)
            sp.dma_start(router_b[:, 0:GROUPS], router_g_b[0:1, :].to_broadcast([P, GROUPS])).then_inc(router_loaded, 16)
            sp.dma_start(router_b[:, GROUPS:],
                         router_e_b[0:1, :].to_broadcast([P, EXPERTS])).then_inc(router_loaded, 16)

            def load_head(h, par):
                for j in range(3):
                    if not isinstance(h, int):
                        sp.wait_ge(w_used, h * 3 + (j - RING + 1))
                    sp.dma_start(slot16(3 * par + j), w_in[:, :, bass.ds(h * VD + D * j, VD)])\
                        .then_inc(w_loaded[3 * par + j], 16)

            sp.wait_ge(ada_used, 2 * ADA_CH)
            load_head(0, 0)
            load_head(1, 1)
            with sp.Fori(1, HEADS // 2) as pair:
                load_head(pair * 2, 0)
                load_head(pair * 2 + 1, 1)
            for ch in range(OUT_CH):
                n = QKV_CH + ch
                sp.wait_ge(w_used, n - RING + 1)
                sp.dma_start(slot16(n % RING), w_out[:, :, VD * ch:VD * (ch + 1)]).then_inc(w_loaded[n % RING], 16)

            def load_item(m, e):
                gu, dn = w_gu(e), w_d(e)
                for j in range(RING):
                    sp.wait_ge(w_used, m * RING + (MOE_CH0 + j - RING + 1))
                    s = moe_slot(j)
                    if j < 4:
                        sp.dma_start(ring[:, s, :].rearrange("p (k n) -> p k n", k=4),
                                     gu[:, 4 * j:4 * j + 4, :]).then_inc(w_loaded[s], 16)
                    else:
                        sp.dma_start(ring[:, s, :].rearrange("p (k n) -> p k n", k=2),
                                     dn[:, 2 * (j - 4):2 * (j - 4) + 2, :]).then_inc(w_loaded[s], 16)

            with sp.Fori(0, EXPERTS) as m:
                load_item(m, m)
            sp.wait_ge(tables_ready, 1)
            extra_groups = sp.value_load(extra_i[0:1, EXTRA:EXTRA + 1], min_val=0, max_val=EXTRA // QUAD)
            with sp.Fori(0, EXTRA // QUAD) as g:
                with sp.If(g < extra_groups):
                    for j in range(QUAD):
                        e = sp.value_load(extra_i[0:1, bass.ds(g * QUAD + j, 1)], min_val=0, max_val=EXPERTS - 1)
                        load_item(g * QUAD + (EXPERTS + j), e)
                sp.end_ifs()
            for a in range(TT):
                sp.wait_ge(out_ready, a + 1)
                sp.dma_start(out[0, P * a:P * (a + 1), :], x_res[:, a, :]).then_inc(stored, 16)
            sp.wait_ge(stored, 16 * TT)

        @block.gpsimd
        def _(gp):
            step = Chain(gp, consts_step)
            nc.gpsimd.memset(ones[:], 1.0).then_inc(consts_ready, 1)
            step.link(nc.gpsimd.memset(ident[:], 0.0))
            nc.gpsimd.affine_select(out=ident[:], in_=ident[:], compare_op=ALU.not_equal, fill=1.0, base=0,
                                    pattern=[[-1, P]], channel_multiplier=1).then_inc(consts_ready, 1)
            step.link(nc.gpsimd.memset(before[:], 0.0))
            nc.gpsimd.affine_select(out=before[:], in_=before[:], compare_op=ALU.is_ge, fill=1.0, base=0,
                                    pattern=[[-1, P]], channel_multiplier=1).then_inc(consts_ready, 1)
            nc.gpsimd.iota(slot_no[:], pattern=[[1, SLOTS]], base=1, channel_multiplier=0,
                           allow_small_or_imprecise_dtypes=True).then_inc(consts_ready, 1)
            nc.gpsimd.iota(neg_dist, pattern=[[P, TT], [-1, T]], base=0, channel_multiplier=1,
                           allow_small_or_imprecise_dtypes=True).then_inc(dist_ready, 1)

            def load_ada(b, cols):
                for j in range(ADA_CH):
                    if not (isinstance(b, int) and b == 0):
                        gp.wait_ge(ada_used, b * ADA_CH + (j - ADA_CH + 1))
                    gp.dma_start(ada_ring[:, j, :].rearrange("p (k n) -> p k n", k=4),
                                 w_ada[:, 4 * j:4 * j + 4, bass.ds(cols, ADA_BLK)]).then_inc(ada_loaded[j], 16)

            load_ada(0, 0)
            load_ada(1, D)
            with gp.Fori(1, 4) as m:
                load_ada(m * 2, m * ADA_BLK)
                load_ada(m * 2 + 1, m * ADA_BLK + D)
            with gp.Fori(8, 24) as b:
                load_ada(b, b * ADA_BLK)
            gp.wait_ge(ada_used, 24 * ADA_CH)
            gp.wait_ge(mod_ready, 12)
            nc.gpsimd.tensor_tensor(diag, ident[:].unsqueeze(1).to_broadcast([P, KT, P]),
                                    mod[:, G1:G1 + KT].unsqueeze(2).to_broadcast([P, KT, P]), ALU.mult)\
                .then_inc(diag_ready, 1)
            gp.wait_ge(w_used, QKV_CH)
            gp.dma_start(x_res, x[0].rearrange("(a p) d -> p a d", p=P)).then_inc(x_again, 16)
            gp.wait_ge(gate_spread, 4)
            gp.wait_ge(mod_ready, 24)
            nc.gpsimd.tensor_tensor(diag, ident[:].unsqueeze(1).to_broadcast([P, KT, P]),
                                    mod[:, G2:G2 + KT].unsqueeze(2).to_broadcast([P, KT, P]), ALU.mult)\
                .then_inc(diag_ready, 1)
            gp.wait_ge(gate_spread, 8)
            nc.gpsimd.tensor_tensor(diag, ident[:].unsqueeze(1).to_broadcast([P, KT, P]),
                                    vcols[:, F_G:F_G + KT].unsqueeze(2).to_broadcast([P, KT, P]), ALU.mult)\
                .then_inc(diag_ready, 1)

        @block.tensor
        def _(pe):
            mm = nc.tensor.matmul
            pe.wait_ge(vecs_loaded, 160)
            pe.wait_ge(consts_ready, 4)
            nc.tensor.transpose(psum[:, B_MOD, 0:70], raw_vecs[0:70, :], ident[0:70, 0:70])\
                .then_inc(vecs_transposed, 1)
            nc.tensor.transpose(psum[:, B_MOD, 128:224], raw_adab[0:96, :], ident[0:96, 0:96])\
                .then_inc(vecs_transposed, 1)
            pe.wait_ge(lam_prod, 1)
            mm(psum[:, B_O, 0:2], ones[:], lam_tmp[:, 0:2], start=True, stop=True).then_inc(lam_summed, 1)

            def sum_mod(b, par):
                pe.wait_ge(ada_used, b * ADA_CH + ADA_CH)
                if isinstance(b, int) and b == 0:
                    pe.wait_ge(cols_ready, 2)
                else:
                    pe.wait_ge(mod_ready, b)
                for j in range(4):
                    last = mm(psum[:, B_MOD, 4 * par + j:4 * par + j + 1], acc[:, par, P * j:P * (j + 1)],
                              ones[:, 0:1], start=True, stop=True)
                last.then_inc(mod_summed, 1)

            sum_mod(0, 0)
            for r in range(8):
                if r == 0:
                    pe.wait_ge(x_scaled, 2)
                if r >= 4:
                    pe.wait_ge(x_copied, r - 3)
                for k in (2 * r, 2 * r + 1):
                    for a in range(TT):
                        at = (k % 2) * T + a * P
                        last = nc.tensor.transpose(psum[:, r % 4, at:at + P], x_tok[:, a, P * k:P * (k + 1)], ident[:])
                last.then_inc(x_transposed, 1)
            sum_mod(1, 1)

            def scores(h, par):
                pe.wait_ge(qkv_ready, h * 3 + 2)
                for a in range(TT):
                    if not (isinstance(h, int) and h == 0):
                        pe.wait_ge(s_read, h * 2 + (a - 1))
                    for i in range(2):
                        last = mm(psum[:, B_S + a, T * i:T * (i + 1)], q_t[:, par, i, P * a:P * (a + 1)],
                                  k_t[:, par, i, :], start=True, stop=True)
                    last.then_inc(s_done, 1)

            def transpose_probs(h):
                if isinstance(h, int) and h == 0:
                    pe.wait_ge(qkv_ready, 4)
                else:
                    pe.wait_ge(ot_copied, h * 2)
                for a in range(TT):
                    pe.wait_ge(a_ready, h * 2 + (a + 1))
                    for kk in range(TT):
                        at = (TT * a + kk) * P
                        last = nc.tensor.transpose(psum[:, B_AT, at:at + P], prob[:, a, 0, P * kk:P * (kk + 1)],
                                                   ident[:])
                last.then_inc(at_done, 1)

            def attend(h, par):
                pe.wait_ge(at_copied, h + 1)
                if isinstance(h, int) and h == 0:
                    pe.wait_ge(qkv_ready, 5)
                else:
                    pe.wait_ge(qkv_ready, h * 3 + 3)
                for a in range(TT):
                    for kk in range(TT):
                        last = mm(psum[:, B_O, VD * a:VD * (a + 1)], prob_t[:, a, kk, :], v_tok[:, par, kk, :],
                                  start=kk == 0, stop=kk == TT - 1)
                last.then_inc(o_done, 1)

            def transpose_out(h):
                for a in range(TT):
                    pe.wait_ge(o_normed, h * 2 + (a + 1))
                    for half in range(2):
                        at = half * T + a * P
                        last = nc.tensor.transpose(psum[:, B_AT, at:at + P], o_norm[:, a, P * half:P * (half + 1)],
                                                   ident[:])
                last.then_inc(ot_done, 1)

            def qk_product(h, par, j):
                s = 3 * par + j
                pe.wait_ge(w_loaded[s], w_turn(h, par))
                pe.wait_ge(qkv_ready, h * 3 + (j - 2))
                for i in range(2):
                    for k in range(KT):
                        last = mm(psum[:, B_Q + j, T * i:T * (i + 1)], slot16(s)[:, k, P * i:P * (i + 1)],
                                  h_t[:, k, :], start=k == 0, stop=k == KT - 1)
                last.then_inc(w_used, 1)

            def v_product(h, par):
                s = 3 * par + 2
                pe.wait_ge(w_loaded[s], w_turn(h, par))
                pe.wait_ge(qkv_ready, h * 3)
                for a in range(TT):
                    for k in range(KT):
                        last = mm(psum[:, B_V, VD * a:VD * (a + 1)], h_t[:, k, P * a:P * (a + 1)],
                                  slot16(s)[:, k, :], start=k == 0, stop=k == KT - 1)
                last.then_inc(w_used, 1)

            def w_turn(h, par):
                return (h - par) * 8 + 16

            def head(h, par, b, third=False):
                scores(h - 1, 1 - par)
                qk_product(h, par, 0)
                sum_mod(*b(0))
                transpose_probs(h - 1)
                qk_product(h, par, 1)
                sum_mod(*b(1))
                attend(h - 1, 1 - par)
                v_product(h, par)
                if third:
                    sum_mod(*b(2))
                transpose_out(h - 1)

            def quarter(n, m):
                if m == 0:
                    pe.wait_ge(w_loaded[n], 16)
                for a in range(2):
                    for k in range(4 * m, 4 * m + 4):
                        w, h = slot16(n), h_t[:, k, :]
                        lhs, rhs = (h[:, P * a:P * (a + 1)], w[:, k, :]) if n == 2 else (w[:, k, P * a:P * (a + 1)], h)
                        last = mm(psum[:, EARLY_BANK[n], T * a:T * (a + 1)], lhs, rhs, start=k == 0 and a == 0,
                                  stop=k == KT - 1, skip_group_check=True)
                if m == 3:
                    last.then_inc(w_used, 1)

            for m in range(3):
                pe.wait_ge(h_ready, m + 1)
                for n in range(5):
                    quarter(n, m)
                    if n == 1:
                        sum_mod(2 * m + 2, 0)
                sum_mod(2 * m + 3, 1)
            pe.wait_ge(h_ready, 4)
            for n in range(4):
                quarter(n, 3)
            scores(0, 0)
            quarter(4, 3)
            sum_mod(8, 0)
            v_product(1, 1)
            transpose_probs(0)
            attend(0, 0)
            transpose_out(0)
            with pe.Fori(1, 3) as pair:
                head(pair * 2, 0, lambda i: (pair * 4 + (5 + i), (1 + i) % 2))
                head(pair * 2 + 1, 1, lambda i: (pair * 4 + (7 + i), (1 + i) % 2))
            head(6, 0, lambda i: (17 + i, (17 + i) % 2), third=True)
            head(7, 1, lambda i: (20 + i, (20 + i) % 2), third=True)
            last_head = HEADS - 1
            scores(last_head, 1)
            sum_mod(23, 1)
            pe.wait_ge(diag_ready, 1)
            pe.wait_ge(qkv_ready, QKV_CH)

            def spread_diag(n, b):
                mm(psum[:, b, :], ones[:], diag[:, 4 * n:4 * n + 4, :].rearrange("p a b -> p (a b)"),
                   start=True, stop=True).then_inc(gate_spread, 1)

            for n, b in enumerate((B_Q, B_K, B_V)):
                spread_diag(n, b)
            transpose_probs(last_head)
            attend(last_head, 1)
            pe.wait_ge(mod_ready, 24)
            spread_diag(3, B_MOD)
            transpose_out(last_head)
            pe.wait_ge(ot_copied, 2 * HEADS)

            def transpose_x1(ch):
                pe.wait_ge(x1_ready, ch + 1)
                if ch >= 2:
                    pe.wait_ge(x1_copied, ch - 1)
                for k in range(2):
                    for a in range(TT):
                        at = k * T + a * P
                        cols = VD * ch + P * k
                        last = nc.tensor.transpose(psum[:, ch % 2, at:at + P], x_res[:, a, cols:cols + P], ident[:])
                last.then_inc(x1_transposed, 1)

            def add_logits(ch):
                pe.wait_ge(x1_copied, ch + 1)
                if ch == 0:
                    pe.wait_ge(router_scaled, 1)
                for a in range(TT):
                    for k in range(2):
                        last = mm(psum[:, B_LOGIT, 36 * a:36 * (a + 1)], x1_t[:, ch % 2, k, P * a:P * (a + 1)],
                                  router_wa[:, 2 * ch + k, :], start=ch == 0 and a == 0 and k == 0,
                                  stop=ch == OUT_CH - 1 and k == 1, skip_group_check=True)
                last.then_inc(logits_added, 1)

            for ch in range(OUT_CH):
                n = QKV_CH + ch
                pe.wait_ge(w_loaded[n % RING], 16 * (n // RING + 1))
                if ch >= 4:
                    pe.wait_ge(y_read, ch - 3)
                for a in range(TT):
                    for k in range(KT):
                        last = mm(psum[:, 3 + ch % 4, VD * a:VD * (a + 1)], attn_t[:, k, P * a:P * (a + 1)],
                                  slot16(n % RING)[:, k, :], start=k == 0, stop=k == KT - 1)
                last.then_inc(w_used, 1)
                if ch == 0:
                    pe.wait_ge(gate_ready, 4)
                    pe.wait_ge(diag_ready, 2)
                    for i, b in enumerate((0, 1, B_LOGIT, B_MOD)):
                        spread_diag(i, b)
                if ch == 1:
                    pe.wait_ge(gate_ready, 8)
                    pe.wait_ge(router_loaded, 64)
                    for k in range(KT):
                        last = mm(psum[:, B_MOD, 0:36], mod[:, SH2 + k:SH2 + k + 1].to_broadcast([P, P]),
                                  router_w[:, k, :], start=k == 0, stop=k == KT - 1)
                    last.then_inc(bias_spread, 1)
                if ch >= 1:
                    transpose_x1(ch - 1)
                if ch >= 2:
                    add_logits(ch - 2)
            add_logits(OUT_CH - 2)
            transpose_x1(OUT_CH - 1)
            add_logits(OUT_CH - 1)
            pe.wait_ge(assigned, 1)
            mm(psum[:, B_HT, 0:32], before[:], chosen[:, 0, :], start=True, stop=True)
            mm(psum[:, B_HT, 32:64], before[:], chosen[:, 1, :], start=True, stop=False)
            mm(psum[:, B_HT, 32:64], ones[:], chosen[:, 0, :], start=False, stop=True)
            mm(psum[:, B_HT, 64:96], ones[:], chosen[:, 0, :], start=True, stop=False)
            mm(psum[:, B_HT, 64:96], ones[:], chosen[:, 1, :], start=False, stop=True).then_inc(ranked, 1)

            pe.wait_ge(diag_ready, 3)
            for n in range(4):
                spread_diag(n, B_G + n)

            def moe_group(g, first=False):
                pe.wait_ge(sel_ready, g + 1)
                if not first:
                    pe.wait_ge(ht_copied, g * QUAD)
                for a in range(TT):
                    last = nc.tensor.transpose(psum[:, B_HT, P * a:P * (a + 1)],
                                               sel_w[:, a, :, :].rearrange("p a b -> p (a b)"), ident[:])
                last.then_inc(selt_done, 1)
                if first:
                    pe.wait_ge(gate_ready, 12)
                else:
                    pe.wait_ge(y_taken, g * 8)

                def gather(q):
                    for kk in range(4):
                        for a in range(TT):
                            k = 4 * q + kk
                            last = mm(psum[:, B_G + q, P * kk:P * (kk + 1)], x_res[:, a, P * k:P * (k + 1)],
                                      sel[:, a, :, :].rearrange("p a b -> p (a b)"), start=a == 0, stop=a == TT - 1)
                    last.then_inc(gathered, 1)

                gather(0)
                for i in range(QUAD):
                    m = g * QUAD + i
                    for j in range(4):
                        s = moe_slot(j)
                        w = ring[:, s, :].rearrange("p (k two n f) -> p k two n f", k=4, two=2, n=4)
                        if i == 0 and j < 3:
                            gather(j + 1)
                        pe.wait_ge(w_loaded[s], moe_loads(m, j) * 16)
                        if i == 0:
                            pe.wait_ge(items_ready, g * 4 + (j + 1))
                        if j == 0 and not (first and i == 0):
                            pe.wait_ge(hid_ready, m)
                        for kk in range(4):
                            k = 4 * j + kk
                            for n in range(4):
                                last = mm(psum[32 * n:32 * n + 32, B_GU, 0:256].rearrange("p (a b) -> p a b", a=2),
                                          x_items[:, k, SLOTS * i:SLOTS * (i + 1)], w[:, kk, :, n, :],
                                          start=k == 0, stop=k == KT - 1)
                        if j < 3:
                            last.then_inc(w_used, 1)
                    last.then_inc(w_used, 1)
                    pe.wait_ge(hid_ready, m + 1)
                    if i == 0:
                        pe.wait_ge(selt_copied, g + 1)
                    nc.tensor.transpose(psum[:, B_HT, 0:P], hid_s[3], ident[:]).then_inc(ht_done, 1)
                    pe.wait_ge(ht_copied, m + 1)
                    if not (first and i < 2):
                        pe.wait_ge(o_act, m * 2 - 2)
                        pe.wait_ge(o_dve, m * 2 - 2)
                    for j in (4, 5):
                        s = moe_slot(j)
                        w = ring[:, s, :].rearrange("p (k n f) -> p k n f", k=2, n=4)
                        pe.wait_ge(w_loaded[s], moe_loads(m, j) * 16)
                        for kk in range(2):
                            k = 2 * (j - 4) + kk
                            for n in range(4):
                                last = mm(psum[32 * n:32 * n + 32, B_D + i % 2, :], hid_t[:, k, :], w[:, kk, n, :],
                                          start=k == 0, stop=k == FT - 1)
                        last.then_inc(w_used, 1)
                pe.wait_ge(o_act, g * 2 * QUAD + 2 * QUAD)
                pe.wait_ge(o_dve, g * 2 * QUAD + 2 * QUAD)
                for a in range(TT):
                    for n in range(4):
                        if a:
                            pe.wait_ge(y_taken, g * 8 + (n + 1))
                        mm(psum[:, B_G + n, :], sel_t[:, a, :], o_items[:, 512 * n:512 * (n + 1)],
                           start=True, stop=True).then_inc(y_done, 1)

            moe_group(0, first=True)
            with pe.Fori(1, MAIN) as g:
                moe_group(g)
            pe.wait_ge(tables_ready, 1)
            extra_groups = pe.value_load(extra_i[0:1, EXTRA:EXTRA + 1], min_val=0, max_val=EXTRA // QUAD)
            with pe.Fori(0, EXTRA // QUAD) as g:
                with pe.If(g < extra_groups):
                    moe_group(g + MAIN)
                pe.end_ifs()
        @block.scalar
        def _(act):
            A = nc.scalar.activation
            act.wait_ge(cols_ready, 1)
            A(silu_c[:], vcols[:, C_G:C_G + KT], ACT.Exp, scale=-1.0).then_inc(silu_exp, 1)
            act.wait_ge(lam_summed, 1)
            A(lam_tmp[:, 2:4], psum[:, B_O, 0:2], ACT.Exp).then_inc(lam_exp, 1)
            act.wait_ge(x_loaded, 16)
            for a in range(TT):
                A(region_b[:, D * a:D * (a + 1)], x_tok[:, a, :], ACT.Square,
                  accum_out=ssq[:, a:a + 1]).then_inc(x_squared, 1)
            act.wait_ge(x_mean, 1)
            A(rstd, rstd, ACT.Sqrt).then_inc(x_root, 1)
            for r in range(8):
                act.wait_ge(x_transposed, r + 1)
                A(region_b[:, 512 * r:512 * (r + 1)], psum[:, r % 4, :], ACT.Copy).then_inc(x_copied, 1)

            def exps(h):
                for a in range(TT):
                    act.wait_ge(max_ready, h * 2 + (a + 1))
                    for i in range(2):
                        A(prob[:, a, i, :], prob[:, a, i, :], ACT.Exp, bias=neg_max[:, a, i:i + 1],
                          accum_out=den[:, a, i:i + 1]).then_inc(e_done, 1)

            def copy_qkv(h, par, j):
                dst = (q_t, k_t, v_tok)[j][:, par, :, :].rearrange("p a b -> p (a b)")
                act.wait_ge(w_used, h * 3 + (j + 1))
                early = isinstance(h, int) and h == 1 and j < 2
                A(dst, psum[:, EARLY_BANK[3 + j] if early else B_Q + j, :], ACT.Copy, scale=HD ** -0.5 if j == 0 else 1.0).then_inc(qkv_ready, 1)

            def copy_probs(h):
                act.wait_ge(at_done, h + 1)
                A(prob_t.rearrange("p a b c -> p (a b c)"), psum[:, B_AT, :], ACT.Copy).then_inc(at_copied, 1)

            def norm_out(h):
                act.wait_ge(o_done, h + 1)
                for a in range(TT):
                    A(o_norm[:, a, :], psum[:, B_O, VD * a:VD * (a + 1)], ACT.Square,
                      accum_out=osq[:, a:a + 1]).then_inc(o_squared, 1)
                act.wait_ge(o_mean, h + 1)
                A(omid, omid, ACT.Sqrt).then_inc(o_root, 1)
                act.wait_ge(o_rstd, h + 1)
                for a in range(TT):
                    A(o_norm[:, a, :], psum[:, B_O, VD * a:VD * (a + 1)], ACT.Copy,
                      scale=omid[:, a:a + 1]).then_inc(o_normed, 1)

            def copy_out(h):
                act.wait_ge(ot_done, h + 1)
                for half in range(2):
                    A(attn_t[:, bass.ds(h * 2 + half, 1), :].rearrange("p a b -> p (a b)"),
                      psum[:, B_AT, T * half:T * (half + 1)], ACT.Copy,
                      scale=vcols[:, SUB_G + half:SUB_G + half + 1]).then_inc(ot_copied, 1)

            def head(h, par):
                exps(h - 1)
                copy_qkv(h, par, 0)
                copy_probs(h - 1)
                copy_qkv(h, par, 1)
                norm_out(h - 1)
                copy_qkv(h, par, 2)
                copy_out(h - 1)

            act.wait_ge(cols_ready, 3)
            for j in range(3):
                copy_qkv(0, 0, j)
            copy_qkv(1, 1, 0)
            copy_qkv(1, 1, 1)
            exps(0)
            copy_qkv(1, 1, 2)
            copy_probs(0)
            norm_out(0)
            copy_out(0)
            with act.Fori(1, HEADS // 2) as pair:
                head(pair * 2, 0)
                head(pair * 2 + 1, 1)
            exps(HEADS - 1)

            def keep_gate1(n, b):
                act.wait_ge(gate_spread, n + 1)
                A(gate1[:, 512 * n:512 * (n + 1)], psum[:, b, :], ACT.Copy).then_inc(gate_ready, 1)

            for n, b in enumerate((B_Q, B_K, B_V)):
                keep_gate1(n, b)
            copy_probs(HEADS - 1)
            norm_out(HEADS - 1)
            copy_out(HEADS - 1)
            keep_gate1(3, B_MOD)
            for ch in range(OUT_CH):
                act.wait_ge(x1_ready, ch + 1)
                for a in range(TT):
                    if ch + a:
                        act.wait_ge(x1_squared, TT * ch + a)
                    A(junk, x_res[:, a, VD * ch:VD * (ch + 1)], ACT.Square,
                      accum_out=ssq8[:, a, ch:ch + 1]).then_inc(x1_squared, 1)
                if ch == 0:
                    for n, b in enumerate((0, 1, B_LOGIT, B_MOD)):
                        act.wait_ge(gate_spread, 5 + n)
                        A(gate2[:, 512 * n:512 * (n + 1)], psum[:, b, :], ACT.Copy).then_inc(gate_ready, 1)
                act.wait_ge(x1_transposed, ch + 1)
                if ch >= 2:
                    act.wait_ge(logits_added, ch - 1)
                A(x1_t[:, ch % 2, :, :].rearrange("p k t -> p (k t)"), psum[:, ch % 2, :], ACT.Copy)\
                    .then_inc(x1_copied, 1)
            act.wait_ge(x1_mean, 1)
            A(rstd, rstd, ACT.Sqrt).then_inc(x1_root, 1)
            act.wait_ge(shifted, 1)
            A(rt_exp_in, rt_exp_in, ACT.Exp).then_inc(route_exp, 1)
            act.wait_ge(shifted, 2)
            A(rt_gap, rt_gap, ACT.Exp).then_inc(route_exp, 1)

            for n in range(4):
                act.wait_ge(gate_spread, 9 + n)
                A(final_gain[:, 512 * n:512 * (n + 1)], psum[:, B_G + n, :], ACT.Copy).then_inc(gate_ready, 1)
            A(region_a[:], region_b[:], ACT.Copy).then_inc(y_started, 1)

            def moe_group(g):
                act.wait_ge(selt_done, g + 1)
                A(sel_t.rearrange("p a b -> p (a b)"), psum[:, B_HT, 0:T], ACT.Copy).then_inc(selt_copied, 1)
                for i in range(QUAD):
                    m = g * QUAD + i
                    act.wait_ge(w_used, m * RING + (MOE_CH0 + 4))
                    A(hid_s[0], psum[:, B_GU, 0:P], ACT.Exp, scale=-1.0).then_inc(gate_exp, 1)
                    act.wait_ge(ht_done, m + 1)
                    A(hid_t.rearrange("p a b -> p (a b)"), psum[:, B_HT, 0:P], ACT.Copy).then_inc(ht_copied, 1)
                    act.wait_ge(w_used, m * RING + (MOE_CH0 + 6))
                    for n in (0, 1):
                        A(o_items[32 * i:32 * i + 32, 512 * n:512 * (n + 1)],
                          psum[32 * n:32 * n + 32, B_D + i % 2, :], ACT.Copy).then_inc(o_act, 1)

            with act.Fori(0, MAIN) as g:
                moe_group(g)
            act.wait_ge(tables_ready, 1)
            extra_groups = act.value_load(extra_i[0:1, EXTRA:EXTRA + 1], min_val=0, max_val=EXTRA // QUAD)
            with act.Fori(0, EXTRA // QUAD) as g:
                with act.If(g < extra_groups):
                    moe_group(g + MAIN)
                act.end_ifs()
            act.wait_ge(spare_ready, 1)
            A(stat[:, 44:45], stat[:, 43:44], ACT.Sqrt).then_inc(act_step, 1)
            act.wait_ge(x2_ready, 1)
            A(x_res[:, 0, :], y_acc[:, 0, :], ACT.Square, accum_out=ssq[:, 0:1]).then_inc(x2_squared, 1)
            for a in range(TT):
                act.wait_ge(x2_mean, a + 1)
                A(rstd[:, a:a + 1], rstd[:, a:a + 1], ACT.Sqrt).then_inc(x2_root, 1)

        @block.vector
        def _(dve):
            v = nc.vector
            v.memset(stat[:, 42:45], 1.0).then_inc(spare_ready, 1)
            step = Chain(dve, dve_step)
            dve.wait_ge(vecs_transposed, 2)
            v.tensor_copy(vcols[:], psum[:, B_MOD, 0:70]).then_inc(cols_ready, 1)
            v.tensor_copy(adab[:], psum[:, B_MOD, 128:224]).then_inc(cols_ready, 1)
            dve.wait_ge(cols_ready, 1)
            v.tensor_tensor(lam_tmp[:, 0:2], vcols[:, LAM:LAM + 2], vcols[:, LAM + 2:LAM + 4], ALU.mult)\
                .then_inc(lam_prod, 1)
            dve.wait_ge(silu_exp, 1)
            step.link(v.tensor_scalar_add(silu_c[:], silu_c[:], 1.0))
            step.link(v.reciprocal(silu_c[:], silu_c[:]))
            step.link(v.tensor_tensor(silu_c[:], silu_c[:], vcols[:, C_G:C_G + KT], ALU.mult))
            v.tensor_scalar(vcols[:, SUB_G:SUB_G + 2], vcols[:, SUB_G:SUB_G + 2], 1.0 - LAM_INIT, None, ALU.mult)\
                .then_inc(cols_ready, 1)
            dve.wait_ge(dist_ready, 1)
            step.link(v.scalar_tensor_tensor(out=neg_dist, in0=neg_dist, scalar=-1.0, in1=neg_dist, op0=ALU.mult,
                                             op1=ALU.min))
            dve.wait_ge(lam_exp, 1)
            step.link(v.tensor_tensor(neg_lam, lam_tmp[:, 3:4], lam_tmp[:, 2:3], ALU.subtract))
            step.link(v.tensor_scalar_add(neg_lam, neg_lam, -LAM_INIT))

            def ada_chunk(b, par, j):
                dve.wait_ge(ada_loaded[j], b * 16 + 16)
                if j == 0 and not (isinstance(b, int) and b < 2):
                    dve.wait_ge(mod_summed, b - 1)
                for kk in range(4):
                    k = 4 * j + kk
                    w = ada_ring[:, j, ADA_BLK * kk:ADA_BLK * (kk + 1)]
                    if k == 0:
                        ins = v.tensor_scalar(acc[:, par, :], w, silu_c[:, k:k + 1], None, ALU.mult)
                    else:
                        ins = v.scalar_tensor_tensor(out=acc[:, par, :], in0=w, scalar=silu_c[:, k:k + 1],
                                                     in1=acc[:, par, :], op0=ALU.mult, op1=ALU.add)
                    if kk < 3:
                        step.link(ins)
                ins.then_inc(ada_used, 1)
                dve.wait_ge(ada_used, b * ADA_CH + (j + 1))

            def keep_mod(b, par, col):
                dve.wait_ge(mod_summed, b + 1)
                v.tensor_tensor(mod[:, bass.ds(col, 4)], psum[:, B_MOD, 4 * par:4 * par + 4],
                                adab[:, bass.ds(col, 4)], ALU.add).then_inc(mod_ready, 1)

            def early_col(b):
                return (b % 2) * SC1 + (b // 2) * 4

            def make_h(m):
                dve.wait_ge(mod_ready, 2 * m + 2)
                step.link(v.scalar_tensor_tensor(out=a1[:, 4 * m:4 * m + 4], in0=mod[:, SC1 + 4 * m:SC1 + 4 * m + 4],
                                                 scalar=1.0, in1=vcols[:, N1_G + 4 * m:N1_G + 4 * m + 4],
                                                 op0=ALU.add, op1=ALU.mult))
                for k in range(4 * m, 4 * m + 4):
                    last = v.tensor_scalar(h_t[:, k, :], h_t[:, k, :], a1[:, k:k + 1], mod[:, SH1 + k:SH1 + k + 1],
                                           ALU.mult, ALU.add)
                last.then_inc(h_ready, 1)

            for j in range(ADA_CH):
                ada_chunk(0, 0, j)
            dve.wait_ge(x_squared, TT)
            v.tensor_scalar(rstd, ssq, 1.0 / D, EPS, ALU.mult, ALU.add).then_inc(x_mean, 1)
            dve.wait_ge(x_root, 1)
            step.link(v.reciprocal(rstd, rstd))
            for a in range(TT):
                v.tensor_scalar(x_tok[:, a, :], x_tok[:, a, :], rstd[:, a:a + 1], None, ALU.mult).then_inc(x_scaled, 1)
            for b in range(1, 8):
                for j in range(ADA_CH):
                    ada_chunk(b, b % 2, j)
                    if j == 0:
                        keep_mod(b - 1, (b - 1) % 2, early_col(b - 1))
                        if b == 2:
                            dve.wait_ge(x_copied, 8)
                        if b % 2 == 0:
                            make_h(b // 2 - 1)
            keep_mod(7, 1, early_col(7))
            make_h(3)

            def add_bias(h):
                step.link(v.tensor_scalar(neg_dist, neg_dist, 0.5, None, ALU.mult))
                for a in range(TT):
                    dve.wait_ge(s_done, h * 2 + (a + 1))
                    if a == 0 and not (isinstance(h, int) and h == 0):
                        dve.wait_ge(at_done, h)
                    v.tensor_tensor(prob[:, a, :, :], psum[:, B_S + a, :].rearrange("p (i k) -> p i k", i=2),
                                    neg_dist[:, a:a + 1, :].to_broadcast([P, 2, T]), ALU.add).then_inc(s_read, 1)
                    dve.wait_ge(s_read, h * 2 + (a + 1))
                    v.reduce_max(neg_max[:, a, :], prob[:, a, :, :], X, negate=True).then_inc(max_ready, 1)

            def combine(h):
                for a in range(TT):
                    dve.wait_ge(e_done, h * 4 + (2 * a + 2))
                    step.link(v.reciprocal(rden[:, a, :], den[:, a, :]))
                    step.link(v.tensor_tensor(rden[:, a, 1:2], rden[:, a, 1:2], neg_lam, ALU.mult))
                    step.link(v.tensor_scalar(prob[:, a, 0, :], prob[:, a, 0, :], rden[:, a, 0:1], None, ALU.mult))
                    v.scalar_tensor_tensor(out=prob[:, a, 0, :], in0=prob[:, a, 1, :], scalar=rden[:, a, 1:2],
                                           in1=prob[:, a, 0, :], op0=ALU.mult, op1=ALU.add).then_inc(a_ready, 1)

            def out_rstd(h):
                dve.wait_ge(o_squared, h * 2 + 2)
                v.tensor_scalar(omid, osq, 1.0 / VD, EPS, ALU.mult, ALU.add).then_inc(o_mean, 1)
                dve.wait_ge(o_root, h + 1)
                v.reciprocal(omid, omid).then_inc(o_rstd, 1)

            def head(h, b, par, third=False, late=False):
                add_bias(h - 1)
                if late:
                    keep_mod(b - 2, par, b * 4 - 8)
                ada_chunk(b, par, 0)
                ada_chunk(b, par, 1)
                combine(h - 1)
                ada_chunk(b, par, 2)
                ada_chunk(b, par, 3)
                keep_mod(b - 1, 1 - par, b * 4 - 4)
                for j in range(ADA_CH):
                    ada_chunk(b + 1, 1 - par, j)
                keep_mod(b, par, b * 4)
                if third:
                    for j in range(ADA_CH):
                        ada_chunk(b + 2, par, j)
                out_rstd(h - 1)

            for j in range(ADA_CH):
                ada_chunk(8, 0, j)
            ada_chunk(9, 1, 0)
            ada_chunk(9, 1, 1)
            add_bias(0)
            ada_chunk(9, 1, 2)
            combine(0)
            ada_chunk(9, 1, 3)
            keep_mod(8, 0, 32)
            out_rstd(0)
            per_head = 8 * 3 + 1 + 3 * TT
            with dve.Fori(1, 3) as pair:
                step.start_loop(pair - 1, 2 * per_head)
                head(pair * 2, pair * 4 + 6, 0)
                head(pair * 2 + 1, pair * 4 + 8, 0)
            step.end_loop(2)
            head(6, 18, 0, third=True)
            head(7, 21, 1, third=True, late=True)
            add_bias(HEADS - 1)
            keep_mod(22, 0, 88)
            combine(HEADS - 1)
            keep_mod(23, 1, 92)
            dve.wait_ge(mod_ready, 24)
            step.link(v.scalar_tensor_tensor(out=a2[:], in0=mod[:, SC2:SC2 + KT], scalar=1.0,
                                             in1=vcols[:, N2_G:N2_G + KT], op0=ALU.add, op1=ALU.mult))
            out_rstd(HEADS - 1)
            dve.wait_ge(router_loaded, 64)
            v.tensor_tensor(router_wa, router_w[:], a2[:].unsqueeze(2).to_broadcast([P, KT, 36]), ALU.mult)\
                .then_inc(router_scaled, 1)
            dve.wait_ge(gate_ready, 4)
            dve.wait_ge(x_again, 16)
            for ch in range(OUT_CH):
                cols = slice(VD * ch, VD * (ch + 1))
                dve.wait_ge(w_used, QKV_CH + ch + 1)
                if ch:
                    dve.wait_ge(x1_ready, ch)
                v.tensor_tensor(y_tmp, psum[:, 3 + ch % 4, :].rearrange("p (a n) -> p a n", a=TT),
                                gate1[:, cols].unsqueeze(1).to_broadcast([P, TT, VD]), ALU.mult).then_inc(y_read, 1)
                dve.wait_ge(y_read, ch + 1)
                v.tensor_tensor(x_res[:, :, cols], x_res[:, :, cols], y_tmp, ALU.add).then_inc(x1_ready, 1)
                if ch == 2:
                    dve.wait_ge(bias_spread, 1)
                    step.link(v.tensor_tensor(router_b[:], router_b[:], psum[:, B_MOD, 0:36], ALU.add))
            dve.wait_ge(x1_squared, OUT_CH * TT)
            step.link(v.reduce_sum(ssq, ssq8, X))
            v.tensor_scalar(rstd, ssq, 1.0 / D, EPS, ALU.mult, ALU.add).then_inc(x1_mean, 1)
            dve.wait_ge(x1_root, 1)
            step.link(v.reciprocal(rstd, rstd))

            dve.wait_ge(logits_added, OUT_CH)
            for a in range(TT):
                step.link(v.scalar_tensor_tensor(out=logits[:, a, :], in0=psum[:, B_LOGIT, 36 * a:36 * (a + 1)],
                                                 scalar=rstd[:, a:a + 1], in1=router_b[:], op0=ALU.mult,
                                                 op1=ALU.add))
            lg = logits[:, :, 0:GROUPS]

            def first_max(hot, src, n, top, back, got):
                shape = [P, TT, n]
                step.link(v.reduce_max(top, src, X))
                step.link(v.tensor_tensor(hot, src, top.unsqueeze(2).to_broadcast(shape), ALU.is_equal))
                step.link(v.tensor_tensor(hot, hot, back.unsqueeze(1).to_broadcast(shape), ALU.mult))
                step.link(v.reduce_max(got, hot, X))
                step.link(v.tensor_tensor(hot, hot, got.unsqueeze(2).to_broadcast(shape), ALU.is_equal))

            step.link(v.tensor_scalar(back8, slot_no[:, 0:8], -1.0, 9.0, ALU.mult, ALU.add))
            first_max(g_hot, lg, GROUPS, r_top, back8[:, 4:8], r_got)
            v.tensor_tensor(rt_exp_in, lg, r_top.unsqueeze(2).to_broadcast([P, TT, GROUPS]), ALU.subtract)\
                .then_inc(shifted, 1)
            for a in range(TT):
                part = by_group[:, GROUPS * a:GROUPS * (a + 1), :]
                step.link(v.tensor_tensor(part, logits[:, a, GROUPS:].rearrange("p (g e) -> p g e", g=GROUPS),
                                          g_hot[:, a, :].unsqueeze(2).to_broadcast([P, GROUPS, PER_GROUP]),
                                          ALU.mult))
                step.link(v.reduce_sum(e_log[:, a, :], part.rearrange("p g e -> p e g"), X))
            first_max(e_hot1, e_log, PER_GROUP, r_e1, back8, r_got)
            step.link(v.scalar_tensor_tensor(out=e_log2, in0=e_hot1, scalar=-BIG, in1=e_log, op0=ALU.mult,
                                             op1=ALU.add))
            first_max(e_hot2, e_log2, PER_GROUP, r_e2, back8, r_got)
            v.tensor_tensor(rt_gap, r_e2, r_e1, ALU.subtract).then_inc(shifted, 1)
            step.link(v.tensor_tensor(e_log, e_hot1, e_hot2, ALU.add))

            def outer(dst, per_expert):
                for a in range(TT):
                    ins = v.tensor_tensor(dst[:, a, :].rearrange("p (g e) -> p g e", g=GROUPS),
                                          g_hot[:, a, :].unsqueeze(2).to_broadcast([P, GROUPS, PER_GROUP]),
                                          per_expert[:, a:a + 1, :].to_broadcast([P, GROUPS, PER_GROUP]), ALU.mult)
                    if a < TT - 1:
                        step.link(ins)
                return ins

            outer(chosen, e_log).then_inc(assigned, 1)
            dve.wait_ge(route_exp, 2)
            step.link(v.reduce_sum(r_top, rt_exp_in, X))
            step.link(v.reciprocal(r_top, r_top))
            step.link(v.tensor_scalar_add(r_got, rt_gap, 1.0))
            step.link(v.reciprocal(r_got, r_got))
            step.link(v.tensor_tensor(r_e1, r_top, r_got, ALU.mult))
            step.link(v.tensor_tensor(r_e2, r_e1, rt_gap, ALU.mult))
            step.link(v.tensor_tensor(e_hot1, e_hot1, r_e1.unsqueeze(2).to_broadcast([P, TT, PER_GROUP]), ALU.mult))
            step.link(v.tensor_tensor(e_hot2, e_hot2, r_e2.unsqueeze(2).to_broadcast([P, TT, PER_GROUP]), ALU.mult))
            step.link(v.tensor_tensor(e_hot1, e_hot1, e_hot2, ALU.add))
            step.link(outer(weight[:, :, 0:EXPERTS], e_hot1))
            dve.wait_ge(ranked, 1)
            step.link(v.scalar_tensor_tensor(out=rank1[:, :, 0:EXPERTS],
                                             in0=psum[:, B_HT, 0:64].rearrange("p (a n) -> p a n", a=TT), scalar=1.0,
                                             in1=chosen, op0=ALU.add, op1=ALU.mult))

            n_over, counts, first, upto = rt_n
            step.link(v.tensor_copy(counts, psum[:, B_HT, 64:96]))

            def plan_further_items():
                step.link(v.tensor_scalar(n_over, counts, float(SLOTS), None, ALU.is_gt))
                for k in range(2, T // SLOTS):
                    step.link(v.scalar_tensor_tensor(out=n_over, in0=counts, scalar=float(SLOTS * k), in1=n_over,
                                                     op0=ALU.is_gt, op1=ALU.add))
                src, dst = n_over, upto
                for sh in (1, 2, 4, 8, 16):
                    step.link(v.tensor_copy(dst[:, 0:sh], src[:, 0:sh]))
                    step.link(v.tensor_tensor(dst[:, sh:], src[:, sh:], src[:, 0:EXPERTS - sh], ALU.add))
                    src, dst = dst, (first if dst is upto else upto)
                assert src is upto
                step.link(v.tensor_tensor(first, upto, n_over, ALU.subtract))
                own, tmp, tmp2 = over
                wide = [P, EXTRA, EXPERTS]
                step.link(v.tensor_scalar_add(item_no, slot_no[:, 0:EXTRA], -1.0))
                step.link(v.tensor_tensor(own, item_no.unsqueeze(2).to_broadcast(wide),
                                          first.unsqueeze(1).to_broadcast(wide), ALU.is_ge))
                step.link(v.tensor_tensor(tmp, item_no.unsqueeze(2).to_broadcast(wide),
                                          upto.unsqueeze(1).to_broadcast(wide), ALU.is_lt))
                step.link(v.tensor_tensor(own, own, tmp, ALU.mult))

                def pick(dst, table):
                    step.link(v.tensor_tensor(tmp, own, table.unsqueeze(1).to_broadcast(wide), ALU.mult))
                    step.link(v.reduce_sum(dst, tmp, X))

                pick(item_a, first)
                step.link(v.tensor_tensor(item_a, slot_no[:, 0:EXTRA], item_a, ALU.subtract))
                for a in range(TT):
                    pick(item_b, rank1[:, a, 0:EXPERTS])
                    step.link(v.scalar_tensor_tensor(out=rank1[:, a, EXPERTS:], in0=item_a, scalar=-float(SLOTS),
                                                     in1=item_b, op0=ALU.mult, op1=ALU.add))
                    pick(weight[:, a, EXPERTS:], weight[:, a, 0:EXPERTS])
                step.link(v.tensor_scalar_add(first, slot_no[:], -1.0))
                pick(item_b, first)
                step.link(v.tensor_copy(extra_i[:, 0:EXTRA], item_b))
                step.link(v.tensor_scalar(item_a[:, 0:4], item_no[:, 0:4], float(QUAD), upto[:, EXPERTS - 1:EXPERTS],
                                          ALU.mult, ALU.is_lt))
                step.link(v.reduce_sum(item_b[:, 0:1], item_a[:, 0:4], X))
                v.tensor_copy(extra_i[:, EXTRA:EXTRA + 1], item_b[:, 0:1]).then_inc(tables_ready, 1)
                dve.wait_ge(tables_ready, 1)

            def moe_group(g, first_group=False):
                wide4 = [P, QUAD, SLOTS]
                for a in range(TT):
                    r = rank1[:, a, bass.ds(g * QUAD, QUAD)]
                    step.link(v.tensor_tensor(sel[:, a, :, :], slot_no[:].unsqueeze(1).to_broadcast(wide4),
                                              r.unsqueeze(2).to_broadcast(wide4), ALU.is_equal))
                for a in range(TT):
                    w = weight[:, a, bass.ds(g * QUAD, QUAD)]
                    ins = v.tensor_tensor(sel_w[:, a, :, :], sel[:, a, :, :], w.unsqueeze(2).to_broadcast(wide4),
                                          ALU.mult)
                    step.link(ins)
                for a in range(TT):
                    ins = v.tensor_scalar(sel[:, a, :, :], sel[:, a, :, :], rstd[:, a:a + 1], None, ALU.mult)
                    if a < TT - 1:
                        step.link(ins)
                ins.then_inc(sel_ready, 1)
                for q in range(4):
                    ks = slice(4 * q, 4 * q + 4)
                    dve.wait_ge(gathered, g * 4 + (q + 1))
                    step.link(v.tensor_tensor(x_items[:, ks, :],
                                              psum[:, B_G + q, :].rearrange("p (k s) -> p k s", k=4),
                                              a2[:, ks].unsqueeze(2).to_broadcast([P, 4, P]), ALU.mult))
                    v.tensor_tensor(x_items[:, ks, :], x_items[:, ks, :],
                                    mod[:, SH2 + 4 * q:SH2 + 4 * q + 4].unsqueeze(2).to_broadcast([P, 4, P]), ALU.add)\
                        .then_inc(items_ready, 1)
                for i in range(QUAD):
                    m = g * QUAD + i
                    dve.wait_ge(gate_exp, m + 1)
                    step.link(v.tensor_scalar_add(hid_s[1], hid_s[0], 1.0))
                    step.link(v.reciprocal(hid_s[2], hid_s[1]))
                    step.link(v.tensor_tensor(hid_s[1], hid_s[2], psum[:, B_GU, 0:P], ALU.mult))
                    v.tensor_tensor(hid_s[3], hid_s[1], psum[:, B_GU, P:2 * P], ALU.mult).then_inc(hid_ready, 1)
                    dve.wait_ge(w_used, m * RING + (MOE_CH0 + 6))
                    for n in (2, 3):
                        v.tensor_copy(o_items[32 * i:32 * i + 32, 512 * n:512 * (n + 1)],
                                      psum[32 * n:32 * n + 32, B_D + i % 2, :]).then_inc(o_dve, 1)
                    if first_group and i == 2:
                        plan_further_items()
                if first_group:
                    dve.wait_ge(y_started, 1)
                for a in range(TT):
                    for n in range(4):
                        at = 4 * a + n
                        cols = slice(512 * n, 512 * (n + 1))
                        dve.wait_ge(y_done, g * 8 + (at + 1))
                        if at >= 2:
                            dve.wait_ge(y_added, g * 8 + (at - 1))
                        v.tensor_tensor(y_part[at % 2], psum[:, B_G + n, :], gate2[:, cols], ALU.mult)\
                            .then_inc(y_taken, 1)
                        dve.wait_ge(y_taken, g * 8 + (at + 1))
                        v.tensor_tensor(y_acc[:, a, cols], y_acc[:, a, cols], y_part[at % 2], ALU.add)\
                            .then_inc(y_added, 1)
                dve.wait_ge(y_added, g * 8 + 8)
                v.memset(stat[:, 42:43], 0.0)

            moe_group(0, first_group=True)
            per_group = 2 * TT + 1 + 4 + 3 * QUAD
            with dve.Fori(1, MAIN) as g:
                step.start_loop(g - 1, per_group)
                moe_group(g)
            step.end_loop(MAIN - 1)
            extra_groups = dve.value_load(extra_i[0:1, EXTRA:EXTRA + 1], min_val=0, max_val=EXTRA // QUAD)
            with dve.Fori(0, EXTRA // QUAD) as g:
                with dve.If(g < extra_groups):
                    step.start_loop(g, per_group)
                    moe_group(g + MAIN)
                dve.end_ifs()
            step.end_loop(0)

            v.memset(stat[:, 45:46], 0.0).then_inc(x2_ready, 1)
            v.tensor_tensor(x_res[:, 1, :], y_acc[:, 1, :], y_acc[:, 1, :], ALU.mult).then_inc(fin_step, 1)
            dve.wait_ge(fin_step, 1)
            v.reduce_sum(ssq[:, 1:2], x_res[:, 1, :], X).then_inc(fin_step, 1)
            for a in range(TT):
                if a == 0:
                    dve.wait_ge(x2_squared, 1)
                else:
                    dve.wait_ge(fin_step, 2)
                v.tensor_scalar(rstd[:, a:a + 1], ssq[:, a:a + 1], 1.0 / D, EPS, ALU.mult, ALU.add)\
                    .then_inc(x2_mean, 1)
            for a in range(TT):
                dve.wait_ge(x2_root, a + 1)
                v.reciprocal(rstd[:, a:a + 1], rstd[:, a:a + 1]).then_inc(fin_step, 1)
                dve.wait_ge(fin_step, a + 3)
                v.scalar_tensor_tensor(out=x_res[:, a, :], in0=y_acc[:, a, :], scalar=rstd[:, a:a + 1],
                                       in1=final_gain, op0=ALU.mult, op1=ALU.mult).then_inc(out_ready, 1)


_INS = ['x', 'c', 'ada_w', 'ada_b', 'norm1_g', 'norm2_g', 'router_g_w', 'router_g_b', 'router_e_w', 'router_e_b',
        'moe_w_gu', 'moe_w_d', 'da_w_in', 'da_w_out', 'da_lam_q1', 'da_lam_k1', 'da_lam_q2', 'da_lam_k2',
        'da_subln_g', 'final_g']


def kernel(**inputs):
    import numpy as _np
    import concourse.bacc as _bacc
    from concourse import mybir as _mybir
    from concourse.bass_utils import run_bass_kernel_spmd as _run

    nc = _bacc.Bacc("TRN2", target_bir_lowering=False, num_devices=1)
    arrays, args = {}, []
    for name in _INS:
        a = _np.ascontiguousarray(inputs[name])
        arrays[f"in_{name}_dram"] = a
        args.append(nc.dram_tensor(f"in_{name}_dram", a.shape, _mybir.dt.from_np(a.dtype), kind="ExternalInput").ap())
    args.append(nc.dram_tensor("out_0_dram", inputs["x"].shape, _mybir.dt.float32, kind="ExternalOutput").ap())
    encoder_layer(nc, *args)
    r = _run(nc, [arrays], core_ids=[0])
    return r.results[0]["out_0_dram"]
```

```python
import math
from contextlib import ExitStack

import concourse.bass as bass
from concourse import mybir

P = 128
T = 256
TT = T // P
D = 2048
KT = D // P
HEADS, HD = 8, 128
VD = 2 * HD
EXPERTS, GROUPS, PER_GROUP = 32, 4, 8
FF = 512
FT = FF // P
SLOTS = 32
QUAD = 4
MAIN = EXPERTS // QUAD
EXTRA = 16
ITEMS = EXPERTS + EXTRA
EPS = 1e-6
LAM_INIT = 0.8 - 0.6 * math.exp(-0.3 * 0)
RING = 6
CH = 4096
OUT_CH = 8
QKV_CH = 3 * HEADS
MOE_CH0 = QKV_CH + OUT_CH
SPARE = ((0, 3), (1, 0), (1, 1))
ADA_BLK = 512
ADA_CH = 4
BIG = 1e30


class Chain:

    def __init__(self, engine, sem):
        self.engine, self.sem, self.base, self.n = engine, sem, 0, 0

    def link(self, ins):
        self.n += 1
        ins.then_inc(self.sem, 1)
        self.engine.wait_ge(self.sem, self.base + self.n)

    def start_loop(self, turn, per_turn):
        self.before, self.per_turn = self.base + self.n, per_turn
        self.base, self.n = turn * per_turn + self.before, 0

    def end_loop(self, turns):
        assert self.n == self.per_turn, (self.n, self.per_turn)
        self.base, self.n = self.before + turns * self.per_turn, 0


def encoder_layer(nc, x, c, ada_w, ada_b, norm1_g, norm2_g, router_g_w, router_g_b, router_e_w, router_e_b,
                  moe_w_gu, moe_w_d, da_w_in, da_w_out, da_lam_q1, da_lam_k1, da_lam_q2, da_lam_k2,
                  da_subln_g, final_g, out):
    f32, i32 = mybir.dt.float32, mybir.dt.int32
    ALU, ACT, AX = mybir.AluOpType, mybir.ActivationFunctionType, mybir.AxisListType
    X = AX.X

    ctx = ExitStack()
    with ctx:
        def sb(name, shape, dt=f32):
            return ctx.enter_context(nc.sbuf_tensor(name, shape, dt))

        def sem(name):
            return ctx.enter_context(nc.semaphore(name))

        ring = sb("ring", [P, RING, CH])
        ada_ring = sb("ada_ring", [P, ADA_CH, 2048])
        region_a = sb("region_a", [P, 4096])
        region_b = sb("region_b", [P, 4096])
        arena = sb("arena", [P, 6656])
        ident = sb("ident", [P, P])
        ones = sb("ones", [P, P])
        before = sb("before", [P, P])
        vcols = sb("vcols", [P, 70])
        adab = sb("adab", [P, 96])
        mod = sb("mod", [P, 96])
        a1 = sb("a1", [P, KT])
        a2 = sb("a2", [P, KT])
        silu_c = sb("silu_c", [P, KT])
        router_w = sb("router_w", [P, KT, GROUPS + EXPERTS])
        router_b = sb("router_b", [P, GROUPS + EXPERTS])
        slot_no = sb("slot_no", [P, SLOTS])
        stat = sb("stat", [P, 48])

        x_tok = region_a[:].rearrange("p (a d) -> p a d", a=TT)
        attn_t = region_a[:].rearrange("p (k t) -> p k t", k=KT)
        y_acc = x_tok
        h_t = region_b[:].rearrange("p (k t) -> p k t", k=KT)
        x_res = region_b[:].rearrange("p (a d) -> p a d", a=TT)
        x1_t = ada_ring[:, 0, 0:1024].rearrange("p (a k t) -> p a k t", a=2, k=2)
        router_wa = ada_ring[:, 0, 1024:1600].rearrange("p (k n) -> p k n", k=KT)
        over = [ada_ring[:, 1, 512 * i:512 * (i + 1)].rearrange("p (a b) -> p a b", a=EXTRA) for i in range(2)]
        junk = arena[:, 4864:5120]
        final_gain = ada_ring[:, 0, :]
        x_items = ada_ring[:, 2, :].rearrange("p (k s) -> p k s", k=KT)
        diag = ada_ring[:, 3, :].rearrange("p (k s) -> p k s", k=KT)
        gate1 = ada_ring[:, 2, :]

        def carve(start, *shape):
            n = math.prod(shape)
            v = arena[:, start:start + n]
            if len(shape) == 2:
                v = v.rearrange("p (a b) -> p a b", a=shape[0])
            if len(shape) == 3:
                v = v.rearrange("p (a b c) -> p a b c", a=shape[0], b=shape[1])
            return v

        q_t = carve(0, 2, 2, T)
        k_t = carve(1024, 2, 2, T)
        v_tok = carve(2048, 2, TT, VD)
        prob = carve(3072, TT, 2, T)
        prob_t = carve(4096, TT, TT, P)
        neg_dist = carve(4608, TT, T)
        o_norm = carve(5120, TT, VD)
        acc = carve(5632, 2, ADA_BLK)
        raw_vecs, raw_adab = o_norm[:, 0, 0:P], o_norm[:, 1, 0:P]
        o_items = carve(0, D)
        gate2 = carve(2048, D)
        sel = carve(4096, TT, QUAD, SLOTS)
        sel_w = carve(4352, TT, QUAD, SLOTS)
        sel_t = carve(4608, TT, P)
        hid_s = [carve(4864 + 128 * i, P) for i in range(4)]
        hid_t = carve(5376, FT, SLOTS)
        y_tmp = carve(5504, TT, T)
        rank1 = carve(6016, TT, ITEMS)
        weight = carve(6112, TT, ITEMS)
        rt = carve(6208, 448)
        logits = rt[:, 0:72].rearrange("p (a n) -> p a n", a=TT)
        by_group = rt[:, 72:136].rearrange("p (a n) -> p a n", a=TT * GROUPS)
        chosen = rt[:, 136:200].rearrange("p (a n) -> p a n", a=TT)
        e_log, e_log2, e_hot1, e_hot2 = (rt[:, 200 + 16 * i:216 + 16 * i].rearrange("p (a n) -> p a n", a=TT)
                                         for i in range(4))
        g_hot, rt_exp_in = (rt[:, 264 + 8 * i:272 + 8 * i].rearrange("p (a n) -> p a n", a=TT) for i in range(2))
        r_top, r_got, r_e1, r_e2, rt_gap = (rt[:, 280 + 2 * i:282 + 2 * i] for i in range(5))
        back8 = rt[:, 290:298]
        rt_n = [rt[:, 298 + 32 * i:330 + 32 * i] for i in range(4)]
        item_no, item_a, item_b = rt[:, 0:16], rt[:, 16:32], rt[:, 32:48]
        extra_i = sb("extra_i", [P, EXTRA + 1], i32)

        psum = ctx.enter_context(nc.psum_tensor("psum", [P, 8, 512], f32))
        B_Q, B_K, B_V, B_S, B_AT, B_O, B_MOD = 0, 1, 2, 3, 5, 6, 7
        EARLY = ((0, 0), (0, 1), (1, 2), (0, 2), (1, 0), (1, 1))
        EARLY_STEP = (0, 0, 1, 2, 3, 4)
        EARLY_BANK = (B_Q, B_K, B_S + 1, B_V, B_AT, B_O)
        B_LOGIT = 2
        B_G, B_GU, B_HT, B_D = 0, 4, 5, 6

        C_G, N1_G, N2_G, F_G, SUB_G, LAM = 0, 16, 32, 48, 64, 66
        SH1, SC1, G1, SH2, SC2, G2 = (KT * i for i in range(6))
        ssq, rstd = stat[:, 0:2], stat[:, 2:4]
        neg_max = stat[:, 4:8].rearrange("p (a b) -> p a b", a=2)
        den = stat[:, 8:12].rearrange("p (a b) -> p a b", a=2)
        rden = stat[:, 12:16].rearrange("p (a b) -> p a b", a=2)
        neg_lam = stat[:, 16:17]
        lam_tmp = stat[:, 17:21]
        osq, omid = stat[:, 21:23], stat[:, 23:25]
        ssq8 = stat[:, 26:42].rearrange("p (a b) -> p a b", a=2)

        w_loaded = [sem(f"w_loaded{i}") for i in range(RING)]
        spare_loaded = [sem(f"spare_loaded{i}") for i in range(len(SPARE))]
        w_used = sem("w_used")
        ada_loaded = [sem(f"ada_loaded{i}") for i in range(ADA_CH)]
        ada_used = sem("ada_used")
        vecs_loaded, x_loaded, router_loaded, x_again = map(sem, ("vecs_loaded", "x_loaded", "router_loaded",
                                                                  "x_again"))
        consts_step, consts_ready = sem("consts_step"), sem("consts_ready")
        dist_ready, spare_ready = sem("dist_ready"), sem("spare_ready")
        dve_step, act_step = sem("dve_step"), sem("act_step")
        vecs_transposed, cols_ready = sem("vecs_transposed"), sem("cols_ready")
        silu_exp = sem("silu_exp")
        lam_prod, lam_summed, lam_exp = sem("lam_prod"), sem("lam_summed"), sem("lam_exp")
        x_squared, x_mean, x_root, x_scaled = map(sem, ("x_squared", "x_mean", "x_root", "x_scaled"))
        x_transposed, x_copied = sem("x_transposed"), sem("x_copied")
        mod_summed, mod_ready = sem("mod_summed"), sem("mod_ready")
        a1_ready, h_ready = sem("a1_ready"), sem("h_ready")
        qkv_ready = sem("qkv_ready")
        s_done, s_read, max_ready, e_done, a_ready = map(sem, ("s_done", "s_read", "max_ready", "e_done", "a_ready"))
        at_done, at_copied, o_done, o_squared, o_mean, o_root, o_rstd, o_normed, ot_done, ot_copied = map(
            sem, ("at_done", "at_copied", "o_done", "o_squared", "o_mean", "o_root", "o_rstd", "o_normed",
                  "ot_done", "ot_copied"))
        diag_ready, gate_spread, gate_ready = sem("diag_ready"), sem("gate_spread"), sem("gate_ready")
        y_read, x1_ready, x1_squared = sem("y_read"), sem("x1_ready"), sem("x1_squared")
        x1_mean, x1_root = sem("x1_mean"), sem("x1_root")
        x1_transposed, x1_copied, logits_added, router_scaled, bias_spread, y_started = map(
            sem, ("x1_transposed", "x1_copied", "logits_added", "router_scaled", "bias_spread", "y_started"))
        shifted, route_exp, assigned, ranked, tables_ready = map(
            sem, ("shifted", "route_exp", "assigned", "ranked", "tables_ready"))
        selw_ready, counted = sem("selw_ready"), sem("counted")
        sel_ready, selt_done, selt_copied, gathered, items_ready = map(
            sem, ("sel_ready", "selt_done", "selt_copied", "gathered", "items_ready"))
        gate_exp, hid_ready, ht_done, ht_copied, o_ready, o_gated, y_done, y_added = map(
            sem, ("gate_exp", "hid_ready", "ht_done", "ht_copied", "o_ready", "o_gated",
                  "y_done", "y_added"))
        x2_ready, x2_squared, x2_mean, x2_root, out_ready, stored, fin_step = map(
            sem, ("x2_ready", "x2_squared", "x2_mean", "x2_root", "out_ready", "stored", "fin_step"))

        w_in = da_w_in[0].rearrange("(k p) n -> p k n", p=P)
        w_out = da_w_out[0].rearrange("(k p) n -> p k n", p=P)
        w_ada = ada_w[0].rearrange("(k p) n -> p k n", p=P)

        def w_gu(e):
            return moe_w_gu[0, bass.ds(e, 1), :, :].rearrange("e (k p) n -> p (e k) n", p=P)

        def w_d(e):
            return moe_w_d[0, bass.ds(e, 1), :, :].rearrange("e (k p) n -> p (e k) n", p=P)

        def slot16(s):
            return ring[:, s, :].rearrange("p (k n) -> p k n", k=KT)

        def moe_at(m, j):
            skipped = sum(sp < (m, j) for sp in SPARE) if isinstance(m, int) else len(SPARE)
            return MOE_CH0 + j - skipped

        def moe_slot(m, j):
            return moe_at(m, j) % RING

        def moe_loads(m, j):
            return m + (moe_at(m, j) // RING + 1)

        def slot_free(m, j):
            if not isinstance(m, int):
                return m * RING + (MOE_CH0 + j - RING + 1)
            last = moe_at(m, j) + RING * (m - 1)
            read = {RING * i + moe_at(i, k): MOE_CH0 + RING * i + k + 1
                    for i in range(m + 1) for k in range(RING) if (i, k) not in SPARE}
            return read.get(last, last + 1)

        spare_halves = ((o_items, ada_ring[:, 1, :]), (gate2, ada_ring[:, 3, :]), (region_a[:, 0:D], region_a[:, D:]))

        def load_spare(queue, i):
            m, j = SPARE[i]
            for half, dst in enumerate(spare_halves[i]):
                at = 4 * j + 2 * half
                queue.dma_start(dst.rearrange("p (k n) -> p k n", k=2), w_gu(m)[:, at:at + 2, :])\
                    .then_inc(spare_loaded[i], 16)

        def spare_gu(i, k, n):
            rows = spare_halves[i][k // 2][:, 1024 * (k % 2):1024 * (k % 2 + 1)]
            return rows.rearrange("p (two n f) -> p two n f", two=2, n=4)[:, :, n, :]

        block = ctx.enter_context(nc.Block())

        @block.sync
        def _(sp):
            for row, v, n in ((C_G, c[0], KT), (N1_G, norm1_g[0], KT), (N2_G, norm2_g[0], KT), (F_G, final_g, KT),
                              (SUB_G, da_subln_g[0], 2), (LAM, da_lam_q1[0], 1), (LAM + 1, da_lam_q2[0], 1),
                              (LAM + 2, da_lam_k1[0], 1), (LAM + 3, da_lam_k2[0], 1)):
                sp.dma_start(raw_vecs[row:row + n, :], v.rearrange("(k p) -> k p", p=P)).then_inc(vecs_loaded, 16)
            sp.dma_start(raw_adab[0:96, :], ada_b[0].rearrange("(k p) -> k p", p=P)).then_inc(vecs_loaded, 16)
            sp.dma_start(x_tok, x[0].rearrange("(a p) d -> p a d", p=P)).then_inc(x_loaded, 16)
            def load_head(h, par):
                for j in range(3):
                    sp.wait_ge(w_used, h * 3 + (j - RING + 1))
                    sp.dma_start(slot16(3 * par + j), w_in[:, :, bass.ds(h * VD + D * j, VD)])\
                        .then_inc(w_loaded[3 * par + j], 16)

            for n, (h, j) in enumerate(EARLY):
                sp.wait_ge(ada_used, ADA_CH * EARLY_STEP[n] + 1)
                sp.dma_start(slot16(n), w_in[:, :, h * VD + D * j:(h + 1) * VD + D * j]).then_inc(w_loaded[n], 16)
            with sp.Fori(1, HEADS // 2) as pair:
                load_head(pair * 2, 0)
                load_head(pair * 2 + 1, 1)
            sp.dma_start(router_w[:, :, 0:GROUPS],
                         router_g_w[0].rearrange("(k p) n -> p k n", p=P)).then_inc(router_loaded, 16)
            sp.dma_start(router_w[:, :, GROUPS:],
                         router_e_w[0].rearrange("(k p) n -> p k n", p=P)).then_inc(router_loaded, 16)
            sp.dma_start(router_b[:, 0:GROUPS], router_g_b[0:1, :].to_broadcast([P, GROUPS])).then_inc(router_loaded, 16)
            sp.dma_start(router_b[:, GROUPS:],
                         router_e_b[0:1, :].to_broadcast([P, EXPERTS])).then_inc(router_loaded, 16)
            for ch in range(OUT_CH):
                n = QKV_CH + ch
                sp.wait_ge(w_used, n - RING + 1)
                sp.dma_start(slot16(n % RING), w_out[:, :, VD * ch:VD * (ch + 1)]).then_inc(w_loaded[n % RING], 16)
                if ch == 5:
                    sp.wait_ge(o_done, HEADS)
                    sp.wait_ge(ada_used, 24 * ADA_CH)
                    sp.wait_ge(gate_spread, 4)
                    load_spare(sp, 0)
                    load_spare(sp, 1)

            def load_item(m, e):
                gu, dn = w_gu(e), w_d(e)
                for j in range(RING):
                    if isinstance(m, int) and (m, j) in SPARE:
                        continue
                    sp.wait_ge(w_used, slot_free(m, j))
                    s = moe_slot(m, j)
                    if j < 4:
                        sp.dma_start(ring[:, s, :].rearrange("p (k n) -> p k n", k=4),
                                     gu[:, 4 * j:4 * j + 4, :]).then_inc(w_loaded[s], 16)
                    else:
                        sp.dma_start(ring[:, s, :].rearrange("p (k n) -> p k n", k=2),
                                     dn[:, 2 * (j - 4):2 * (j - 4) + 2, :]).then_inc(w_loaded[s], 16)

            load_item(0, 0)
            sp.wait_ge(w_used, MOE_CH0)
            load_spare(sp, 2)
            load_item(1, 1)
            load_item(2, 2)
            with sp.Fori(3, EXPERTS) as m:
                load_item(m, m)
            sp.wait_ge(tables_ready, 1)
            extra_groups = sp.value_load(extra_i[0:1, EXTRA:EXTRA + 1], min_val=0, max_val=EXTRA // QUAD)
            with sp.If(extra_groups > 0):
                with sp.Fori(0, EXTRA // QUAD) as g:
                    with sp.If(g < extra_groups):
                        for j in range(QUAD):
                            e = sp.value_load(extra_i[0:1, bass.ds(g * QUAD + j, 1)], min_val=0, max_val=EXPERTS - 1)
                            load_item(g * QUAD + (EXPERTS + j), e)
                    sp.end_ifs()
            sp.end_ifs()
            for a in range(TT):
                for half in range(2):
                    cols = slice(D // 2 * half, D // 2 * (half + 1))
                    sp.wait_ge(out_ready, 2 * a + half + 1)
                    sp.dma_start(out[0, P * a:P * (a + 1), cols], x_res[:, a, cols]).then_inc(stored, 16)
            sp.wait_ge(stored, 32 * TT)

        @block.gpsimd
        def _(gp):
            step = Chain(gp, consts_step)
            nc.gpsimd.memset(ones[:], 1.0).then_inc(consts_ready, 1)
            step.link(nc.gpsimd.memset(ident[:], 0.0))
            nc.gpsimd.affine_select(out=ident[:], in_=ident[:], compare_op=ALU.not_equal, fill=1.0, base=0,
                                    pattern=[[-1, P]], channel_multiplier=1).then_inc(consts_ready, 1)
            step.link(nc.gpsimd.memset(before[:], 0.0))
            nc.gpsimd.affine_select(out=before[:], in_=before[:], compare_op=ALU.is_ge, fill=1.0, base=0,
                                    pattern=[[-1, P]], channel_multiplier=1).then_inc(consts_ready, 1)
            nc.gpsimd.iota(slot_no[:], pattern=[[1, SLOTS]], base=1, channel_multiplier=0,
                           allow_small_or_imprecise_dtypes=True).then_inc(consts_ready, 1)
            nc.gpsimd.iota(neg_dist, pattern=[[P, TT], [-1, T]], base=0, channel_multiplier=1,
                           allow_small_or_imprecise_dtypes=True).then_inc(dist_ready, 1)

            def load_ada(b, early=False):
                for j in range(ADA_CH):
                    if not (isinstance(b, int) and b == 0):
                        gp.wait_ge(ada_used, b * ADA_CH + (j - ADA_CH + 1))
                    n = ADA_BLK // 2 if early else ADA_BLK
                    dst = ada_ring[:, j, :].rearrange("p (k n) -> p k n", k=4)
                    for i in range(ADA_BLK // n):
                        gp.dma_start(dst[:, :, n * i:n * (i + 1)],
                                     w_ada[:, 4 * j:4 * j + 4, bass.ds(b * n + D * i, n)]).then_inc(ada_loaded[j], 16)

            load_ada(0, early=True)
            with gp.Fori(1, 8) as b:
                load_ada(b, early=True)
            with gp.Fori(8, 24) as b:
                load_ada(b)
            gp.wait_ge(ada_used, 24 * ADA_CH)
            gp.wait_ge(mod_ready, 12)
            nc.gpsimd.tensor_tensor(diag, ident[:].unsqueeze(1).to_broadcast([P, KT, P]),
                                    mod[:, G1:G1 + KT].unsqueeze(2).to_broadcast([P, KT, P]), ALU.mult)\
                .then_inc(diag_ready, 1)
            gp.wait_ge(w_used, QKV_CH)
            gp.dma_start(x_res, x[0].rearrange("(a p) d -> p a d", p=P)).then_inc(x_again, 16)
            gp.wait_ge(w_used, MOE_CH0 + RING + 1)
            gp.wait_ge(mod_ready, 24)
            nc.gpsimd.tensor_tensor(diag, ident[:].unsqueeze(1).to_broadcast([P, KT, P]),
                                    mod[:, G2:G2 + KT].unsqueeze(2).to_broadcast([P, KT, P]), ALU.mult)\
                .then_inc(diag_ready, 1)
            gp.wait_ge(gate_spread, 8)
            nc.gpsimd.tensor_tensor(diag, ident[:].unsqueeze(1).to_broadcast([P, KT, P]),
                                    vcols[:, F_G:F_G + KT].unsqueeze(2).to_broadcast([P, KT, P]), ALU.mult)\
                .then_inc(diag_ready, 1)

        @block.tensor
        def _(pe):
            mm = nc.tensor.matmul
            pe.wait_ge(vecs_loaded, 160)
            pe.wait_ge(consts_ready, 4)
            nc.tensor.transpose(psum[:, B_MOD, 0:70], raw_vecs[0:70, :], ident[0:70, 0:70])\
                .then_inc(vecs_transposed, 1)
            nc.tensor.transpose(psum[:, B_MOD, 128:224], raw_adab[0:96, :], ident[0:96, 0:96])\
                .then_inc(vecs_transposed, 1)
            pe.wait_ge(lam_prod, 1)
            mm(psum[:, B_O, 0:2], ones[:], lam_tmp[:, 0:2], start=True, stop=True).then_inc(lam_summed, 1)

            def sum_mod(b, par):
                pe.wait_ge(ada_used, b * ADA_CH + ADA_CH)
                if isinstance(b, int) and b == 0:
                    pe.wait_ge(cols_ready, 2)
                else:
                    pe.wait_ge(mod_ready, b)
                for j in range(4):
                    last = mm(psum[:, B_MOD, 4 * par + j:4 * par + j + 1], acc[:, par, P * j:P * (j + 1)],
                              ones[:, 0:1], start=True, stop=True)
                last.then_inc(mod_summed, 1)

            sum_mod(0, 0)
            for r in range(8):
                if r == 0:
                    pe.wait_ge(x_scaled, 2)
                if r >= 4:
                    pe.wait_ge(x_copied, r - 3)
                for k in (2 * r, 2 * r + 1):
                    for a in range(TT):
                        at = (k % 2) * T + a * P
                        last = nc.tensor.transpose(psum[:, r % 4, at:at + P], x_tok[:, a, P * k:P * (k + 1)], ident[:])
                last.then_inc(x_transposed, 1)

            def scores(h, par):
                if isinstance(h, int) and h < 2:
                    pe.wait_ge(qkv_ready, 3 * h + 3)
                else:
                    pe.wait_ge(qkv_ready, h * 3 + 2)
                for a in range(TT):
                    if not (isinstance(h, int) and h == 0):
                        pe.wait_ge(s_read, h * 2 + (a - 1))
                    for i in range(2):
                        last = mm(psum[:, B_S + a, T * i:T * (i + 1)], q_t[:, par, i, P * a:P * (a + 1)],
                                  k_t[:, par, i, :], start=True, stop=True)
                    last.then_inc(s_done, 1)

            def transpose_probs(h):
                if isinstance(h, int) and h == 0:
                    pe.wait_ge(qkv_ready, 5)
                else:
                    pe.wait_ge(ot_copied, h * 2)
                for a in range(TT):
                    pe.wait_ge(a_ready, h * 2 + (a + 1))
                    for kk in range(TT):
                        at = (TT * a + kk) * P
                        last = nc.tensor.transpose(psum[:, B_AT, at:at + P], prob[:, a, 0, P * kk:P * (kk + 1)],
                                                   ident[:])
                last.then_inc(at_done, 1)

            def attend(h, par):
                pe.wait_ge(at_copied, h + 1)
                if isinstance(h, int) and h == 0:
                    pe.wait_ge(qkv_ready, 6)
                for a in range(TT):
                    for kk in range(TT):
                        last = mm(psum[:, B_O, VD * a:VD * (a + 1)], prob_t[:, a, kk, :], v_tok[:, par, kk, :],
                                  start=kk == 0, stop=kk == TT - 1)
                last.then_inc(o_done, 1)

            def transpose_out(h):
                for a in range(TT):
                    pe.wait_ge(o_normed, h * 2 + (a + 1))
                    for half in range(2):
                        at = half * T + a * P
                        last = nc.tensor.transpose(psum[:, B_AT, at:at + P], o_norm[:, a, P * half:P * (half + 1)],
                                                   ident[:])
                last.then_inc(ot_done, 1)

            def qk_product(h, par, j):
                s = 3 * par + j
                pe.wait_ge(w_loaded[s], w_turn(h, par))
                pe.wait_ge(qkv_ready, h * 3 + (j - 2))
                for i in range(2):
                    for k in range(KT):
                        last = mm(psum[:, B_Q + j, T * i:T * (i + 1)], slot16(s)[:, k, P * i:P * (i + 1)],
                                  h_t[:, k, :], start=k == 0, stop=k == KT - 1)
                last.then_inc(w_used, 1)

            def v_product(h, par):
                s = 3 * par + 2
                pe.wait_ge(w_loaded[s], w_turn(h, par))
                pe.wait_ge(qkv_ready, h * 3)
                for a in range(TT):
                    for k in range(KT):
                        last = mm(psum[:, B_V, VD * a:VD * (a + 1)], h_t[:, k, P * a:P * (a + 1)],
                                  slot16(s)[:, k, :], start=k == 0, stop=k == KT - 1)
                last.then_inc(w_used, 1)

            def w_turn(h, par):
                return (h - par) * 8 + 16

            def head(h, par, b, third=False):
                qk_product(h, par, 0)
                if third:
                    sum_mod(*b(0))
                transpose_probs(h - 1)
                qk_product(h, par, 1)
                sum_mod(*b(1 if third else 0))
                attend(h - 1, 1 - par)
                v_product(h, par)
                sum_mod(*b(2 if third else 1))
                scores(h, par)
                transpose_out(h - 1)

            def eighth(n, m):
                if m == 0:
                    pe.wait_ge(w_loaded[n], 16)
                for a in range(2):
                    for k in (2 * m, 2 * m + 1):
                        w, h = slot16(n), h_t[:, k, :]
                        if EARLY[n][1] == 2:
                            lhs, rhs = h[:, P * a:P * (a + 1)], w[:, k, :]
                        else:
                            lhs, rhs = w[:, k, P * a:P * (a + 1)], h
                        last = mm(psum[:, EARLY_BANK[n], T * a:T * (a + 1)], lhs, rhs, start=k == 0 and a == 0,
                                  stop=k == KT - 1, skip_group_check=True)
                if m == 7:
                    last.then_inc(w_used, 1)

            for m in range(7):
                pe.wait_ge(h_ready, 2 * m + 2)
                work = [(n, i) for n in range(len(EARLY)) if EARLY_STEP[n] <= m
                        for i in range(m + 1) if i == m or EARLY_STEP[n] == m]
                for at, (n, i) in enumerate(work):
                    if at == len(work) - 2:
                        sum_mod(m + 1, (m + 1) % 2)
                    eighth(n, i)
            pe.wait_ge(h_ready, KT)
            for n in range(4):
                eighth(n, 7)
            scores(0, 0)
            eighth(4, 7)
            eighth(5, 7)
            transpose_probs(0)
            attend(0, 0)
            scores(1, 1)
            transpose_out(0)
            sum_mod(8, 0)
            with pe.Fori(1, 3) as pair:
                head(pair * 2, 0, lambda i: (pair * 4 + (5 + i), (1 + i) % 2))
                head(pair * 2 + 1, 1, lambda i: (pair * 4 + (7 + i), (1 + i) % 2))
            head(6, 0, lambda i: (17 + i, (17 + i) % 2), third=True)
            head(7, 1, lambda i: (20 + i, (20 + i) % 2), third=True)
            last_head = HEADS - 1

            def spread_diag(n, b):
                mm(psum[:, b, :], ones[:], diag[:, 4 * n:4 * n + 4, :].rearrange("p a b -> p (a b)"),
                   start=True, stop=True).then_inc(gate_spread, 1)

            transpose_probs(last_head)
            attend(last_head, 1)
            transpose_out(last_head)
            pe.wait_ge(ot_copied, 2 * HEADS)

            def transpose_x1(ch):
                pe.wait_ge(x1_ready, ch + 1)
                if ch >= 2:
                    pe.wait_ge(x1_copied, ch - 1)
                for k in range(2):
                    for a in range(TT):
                        at = k * T + a * P
                        cols = VD * ch + P * k
                        last = nc.tensor.transpose(psum[:, ch % 2, at:at + P], x_res[:, a, cols:cols + P], ident[:])
                last.then_inc(x1_transposed, 1)

            def add_logits(ch):
                pe.wait_ge(x1_copied, ch + 1)
                if ch == 0:
                    pe.wait_ge(router_scaled, 1)
                for a in range(TT):
                    for k in range(2):
                        last = mm(psum[:, B_LOGIT, 36 * a:36 * (a + 1)], x1_t[:, ch % 2, k, P * a:P * (a + 1)],
                                  router_wa[:, 2 * ch + k, :], start=ch == 0 and a == 0 and k == 0,
                                  stop=ch == OUT_CH - 1 and k == 1, skip_group_check=True)
                last.then_inc(logits_added, 1)

            for ch in range(OUT_CH):
                n = QKV_CH + ch
                pe.wait_ge(w_loaded[n % RING], 16 * (n // RING + 1))
                if ch >= 4:
                    pe.wait_ge(y_read, ch - 3)
                for a in range(TT):
                    for k in range(KT):
                        last = mm(psum[:, 3 + ch % 4, VD * a:VD * (a + 1)], attn_t[:, k, P * a:P * (a + 1)],
                                  slot16(n % RING)[:, k, :], start=k == 0, stop=k == KT - 1)
                last.then_inc(w_used, 1)
                if ch == 0:
                    pe.wait_ge(diag_ready, 1)
                    pe.wait_ge(qkv_ready, QKV_CH)
                    sum_mod(23, 1)
                    for i, b in enumerate((B_Q, B_K, B_V, B_MOD)):
                        if b == B_MOD:
                            pe.wait_ge(mod_ready, 24)
                        spread_diag(i, b)
                if ch == 1:
                    pe.wait_ge(gate_ready, 4)
                    pe.wait_ge(router_loaded, 64)
                    for k in range(KT):
                        last = mm(psum[:, B_MOD, 0:36], mod[:, SH2 + k:SH2 + k + 1].to_broadcast([P, P]),
                                  router_w[:, k, :], start=k == 0, stop=k == KT - 1)
                    last.then_inc(bias_spread, 1)
                if ch >= 1:
                    transpose_x1(ch - 1)
                if ch >= 2:
                    add_logits(ch - 2)
            add_logits(OUT_CH - 2)
            transpose_x1(OUT_CH - 1)
            add_logits(OUT_CH - 1)
            pe.wait_ge(assigned, 1)
            mm(psum[:, B_HT, 0:32], before[:], chosen[:, 0, :], start=True, stop=True)
            mm(psum[:, B_HT, 32:64], before[:], chosen[:, 1, :], start=True, stop=False)
            mm(psum[:, B_HT, 32:64], ones[:], chosen[:, 0, :], start=False, stop=True).then_inc(ranked, 1)
            mm(psum[:, B_D + 1, 0:32], ones[:], chosen[:, 0, :], start=True, stop=False)
            mm(psum[:, B_D + 1, 0:32], ones[:], chosen[:, 1, :], start=False, stop=True).then_inc(counted, 1)

            def moe_group(g, first=False):
                pe.wait_ge(sel_ready, g + 1)
                if not first:
                    pe.wait_ge(y_added, g * 8)

                def gather(q):
                    for kk in range(4):
                        for a in range(TT):
                            k = 4 * q + kk
                            last = mm(psum[:, B_G + q, P * kk:P * (kk + 1)], x_res[:, a, P * k:P * (k + 1)],
                                      sel[:, a, :, :].rearrange("p a b -> p (a b)"), start=a == 0, stop=a == TT - 1)
                    last.then_inc(gathered, 1)

                gather(0)
                for i in range(QUAD):
                    m = g * QUAD + i
                    for j in range(4):
                        s = moe_slot(m, j)
                        w = ring[:, s, :].rearrange("p (k two n f) -> p k two n f", k=4, two=2, n=4)
                        spare = SPARE.index((i, j)) if first and (i, j) in SPARE else None
                        if i == 0 and j < 3:
                            gather(j + 1)
                        if spare is not None:
                            pe.wait_ge(spare_loaded[spare], 32)
                        else:
                            pe.wait_ge(w_loaded[s], moe_loads(m, j) * 16)
                        if i == 0:
                            pe.wait_ge(items_ready, g * 4 + (j + 1))
                        if j == 0 and not (first and i == 0):
                            pe.wait_ge(hid_ready, m)
                        for kk in range(4):
                            k = 4 * j + kk
                            for n in range(4):
                                last = mm(psum[32 * n:32 * n + 32, B_GU, 0:256].rearrange("p (a b) -> p a b", a=2),
                                          x_items[:, k, SLOTS * i:SLOTS * (i + 1)],
                                          w[:, kk, :, n, :] if spare is None else spare_gu(spare, kk, n),
                                          start=k == 0, stop=k == KT - 1)
                        if j < 3:
                            last.then_inc(w_used, 1)
                    last.then_inc(w_used, 1)
                    if i == 0:
                        pe.wait_ge(selw_ready, g + 1)
                        if not first:
                            pe.wait_ge(ht_copied, g * QUAD)
                        for a in range(TT):
                            last = nc.tensor.transpose(psum[:, B_HT, P * a:P * (a + 1)],
                                                       sel_w[:, a, :, :].rearrange("p a b -> p (a b)"), ident[:])
                        last.then_inc(selt_done, 1)
                    pe.wait_ge(hid_ready, m + 1)
                    if i == 0:
                        pe.wait_ge(selt_copied, g + 1)
                    nc.tensor.transpose(psum[:, B_HT, 0:P], hid_s[3], ident[:]).then_inc(ht_done, 1)
                    pe.wait_ge(ht_copied, m + 1)
                    if not (first and i < 2):
                        pe.wait_ge(o_ready, m * 4 - 4)
                    for j in (4, 5):
                        s = moe_slot(m, j)
                        w = ring[:, s, :].rearrange("p (k n f) -> p k n f", k=2, n=4)
                        pe.wait_ge(w_loaded[s], moe_loads(m, j) * 16)
                        for kk in range(2):
                            k = 2 * (j - 4) + kk
                            for n in range(4):
                                last = mm(psum[32 * n:32 * n + 32, B_D + i % 2, :], hid_t[:, k, :], w[:, kk, n, :],
                                          start=k == 0, stop=k == FT - 1)
                        last.then_inc(w_used, 1)
                    if first and i in (1, 2):
                        if i == 2:
                            pe.wait_ge(gate_ready, 8)
                        pe.wait_ge(diag_ready, i + 1)
                        for n in range(4):
                            spread_diag(n, B_G + n)
                if first:
                    pe.wait_ge(gate_ready, 12)
                for a in range(TT):
                    for n in range(4):
                        if first:
                            pe.wait_ge(o_gated, n + 1)
                        else:
                            pe.wait_ge(o_ready, g * 4 * QUAD + (4 * QUAD - 3 + n))
                        if a:
                            pe.wait_ge(y_added, g * 8 + (n + 1))
                        mm(psum[:, B_G + n, :], sel_t[:, a, :], o_items[:, 512 * n:512 * (n + 1)],
                           start=True, stop=True).then_inc(y_done, 1)

            moe_group(0, first=True)
            pe.wait_ge(tables_ready, 1)
            extra_groups = pe.value_load(extra_i[0:1, EXTRA:EXTRA + 1], min_val=0, max_val=EXTRA // QUAD)
            with pe.Fori(1, MAIN) as g:
                moe_group(g)
            with pe.If(extra_groups > 0):
                with pe.Fori(0, EXTRA // QUAD) as g:
                    with pe.If(g < extra_groups):
                        moe_group(g + MAIN)
                    pe.end_ifs()
            pe.end_ifs()

        @block.scalar
        def _(act):
            A = nc.scalar.activation
            act.wait_ge(cols_ready, 1)
            A(silu_c[:], vcols[:, C_G:C_G + KT], ACT.Exp, scale=-1.0).then_inc(silu_exp, 1)
            act.wait_ge(lam_summed, 1)
            A(lam_tmp[:, 2:4], psum[:, B_O, 0:2], ACT.Exp).then_inc(lam_exp, 1)
            act.wait_ge(x_loaded, 16)
            for a in range(TT):
                A(region_b[:, D * a:D * (a + 1)], x_tok[:, a, :], ACT.Square,
                  accum_out=ssq[:, a:a + 1]).then_inc(x_squared, 1)
            act.wait_ge(x_mean, 1)
            A(rstd, rstd, ACT.Sqrt).then_inc(x_root, 1)
            for r in range(8):
                act.wait_ge(x_transposed, r + 1)
                A(region_b[:, 512 * r:512 * (r + 1)], psum[:, r % 4, :], ACT.Copy).then_inc(x_copied, 1)

            def exps(h):
                for a in range(TT):
                    act.wait_ge(max_ready, h * 2 + (a + 1))
                    for i in range(2):
                        A(prob[:, a, i, :], prob[:, a, i, :], ACT.Exp, bias=neg_max[:, a, i:i + 1],
                          accum_out=den[:, a, i:i + 1]).then_inc(e_done, 1)

            def copy_qkv(h, par, j):
                dst = (q_t, k_t, v_tok)[j][:, par, :, :].rearrange("p a b -> p (a b)")
                n = EARLY.index((h, j)) if isinstance(h, int) and h < 2 else None
                act.wait_ge(w_used, h * 3 + (j + 1) if n is None else n + 1)
                A(dst, psum[:, B_Q + j if n is None else EARLY_BANK[n], :], ACT.Copy,
                  scale=HD ** -0.5 if j == 0 else 1.0).then_inc(qkv_ready, 1)

            def copy_probs(h):
                act.wait_ge(at_done, h + 1)
                A(prob_t.rearrange("p a b c -> p (a b c)"), psum[:, B_AT, :], ACT.Copy).then_inc(at_copied, 1)

            def norm_out(h):
                act.wait_ge(o_done, h + 1)
                for a in range(TT):
                    A(o_norm[:, a, :], psum[:, B_O, VD * a:VD * (a + 1)], ACT.Square,
                      accum_out=osq[:, a:a + 1]).then_inc(o_squared, 1)
                act.wait_ge(o_mean, h + 1)
                A(omid, omid, ACT.Sqrt).then_inc(o_root, 1)
                act.wait_ge(o_rstd, h + 1)
                for a in range(TT):
                    A(o_norm[:, a, :], psum[:, B_O, VD * a:VD * (a + 1)], ACT.Copy,
                      scale=omid[:, a:a + 1]).then_inc(o_normed, 1)

            def copy_out(h):
                act.wait_ge(ot_done, h + 1)
                for half in range(2):
                    A(attn_t[:, bass.ds(h * 2 + half, 1), :].rearrange("p a b -> p (a b)"),
                      psum[:, B_AT, T * half:T * (half + 1)], ACT.Copy,
                      scale=vcols[:, SUB_G + half:SUB_G + half + 1]).then_inc(ot_copied, 1)

            def head(h, par):
                exps(h - 1)
                copy_qkv(h, par, 0)
                copy_probs(h - 1)
                copy_qkv(h, par, 1)
                norm_out(h - 1)
                copy_qkv(h, par, 2)
                copy_out(h - 1)

            act.wait_ge(x_copied, 8)
            for k in range(KT):
                act.wait_ge(a1_ready, k // 2 + 1)
                A(h_t[:, k, :], h_t[:, k, :], ACT.Identity, scale=a1[:, k:k + 1], bias=mod[:, SH1 + k:SH1 + k + 1])\
                    .then_inc(h_ready, 1)

            act.wait_ge(cols_ready, 3)
            for h, j in EARLY:
                if (h, j) == (1, 1):
                    exps(0)
                copy_qkv(h, h, j)
            copy_probs(0)
            norm_out(0)
            copy_out(0)
            with act.Fori(1, HEADS // 2) as pair:
                head(pair * 2, 0)
                head(pair * 2 + 1, 1)
            exps(HEADS - 1)

            def keep_gate1(n, b):
                act.wait_ge(gate_spread, n + 1)
                A(gate1[:, 512 * n:512 * (n + 1)], psum[:, b, :], ACT.Copy).then_inc(gate_ready, 1)

            copy_probs(HEADS - 1)
            norm_out(HEADS - 1)
            copy_out(HEADS - 1)
            for n, b in enumerate((B_Q, B_K, B_V, B_MOD)):
                keep_gate1(n, b)
            for ch in range(OUT_CH):
                act.wait_ge(x1_ready, ch + 1)
                for a in range(TT):
                    if ch + a:
                        act.wait_ge(x1_squared, TT * ch + a)
                    A(junk, x_res[:, a, VD * ch:VD * (ch + 1)], ACT.Square,
                      accum_out=ssq8[:, a, ch:ch + 1]).then_inc(x1_squared, 1)
                act.wait_ge(x1_transposed, ch + 1)
                if ch >= 2:
                    act.wait_ge(logits_added, ch - 1)
                A(x1_t[:, ch % 2, :, :].rearrange("p k t -> p (k t)"), psum[:, ch % 2, :], ACT.Copy)\
                    .then_inc(x1_copied, 1)
            act.wait_ge(x1_mean, 1)
            A(rstd, rstd, ACT.Sqrt).then_inc(x1_root, 1)
            act.wait_ge(shifted, 1)
            A(rt_exp_in, rt_exp_in, ACT.Exp).then_inc(route_exp, 1)
            act.wait_ge(shifted, 2)
            A(rt_gap, rt_gap, ACT.Exp).then_inc(route_exp, 1)

            def keep_spread(vec, first_spread):
                for n in range(4):
                    act.wait_ge(gate_spread, first_spread + n)
                    A(vec[:, 512 * n:512 * (n + 1)], psum[:, B_G + n, :], ACT.Copy).then_inc(gate_ready, 1)

            def moe_group(g, first=False):
                for i in range(QUAD):
                    m = g * QUAD + i
                    act.wait_ge(w_used, m * RING + (MOE_CH0 + 4))
                    A(hid_s[0], psum[:, B_GU, 0:P], ACT.Exp, scale=-1.0).then_inc(gate_exp, 1)
                    if i == 0:
                        act.wait_ge(selt_done, g + 1)
                        A(sel_t.rearrange("p a b -> p (a b)"), psum[:, B_HT, 0:T], ACT.Copy).then_inc(selt_copied, 1)
                    act.wait_ge(ht_done, m + 1)
                    A(hid_t.rearrange("p a b -> p (a b)"), psum[:, B_HT, 0:P], ACT.Copy).then_inc(ht_copied, 1)
                    if first and i == 1:
                        act.wait_ge(w_used, MOE_CH0 + RING + 2)
                        A(region_a[:], region_b[:], ACT.Copy).then_inc(y_started, 1)
                        keep_spread(gate2, 5)
                    if first and i == 2:
                        keep_spread(final_gain, 9)

            moe_group(0, first=True)
            act.wait_ge(tables_ready, 1)
            extra_groups = act.value_load(extra_i[0:1, EXTRA:EXTRA + 1], min_val=0, max_val=EXTRA // QUAD)
            with act.Fori(1, MAIN) as g:
                moe_group(g)
            with act.If(extra_groups > 0):
                with act.Fori(0, EXTRA // QUAD) as g:
                    with act.If(g < extra_groups):
                        moe_group(g + MAIN)
                    act.end_ifs()
            act.end_ifs()
            act.wait_ge(spare_ready, 1)
            A(stat[:, 44:45], stat[:, 43:44], ACT.Sqrt).then_inc(act_step, 1)
            act.wait_ge(y_added, extra_groups * 8 + (MAIN * 8 - 4))
            A(x_res[:, 0, :], y_acc[:, 0, :], ACT.Square, accum_out=ssq[:, 0:1]).then_inc(x2_squared, 1)
            act.wait_ge(x2_mean, 1)
            A(rstd[:, 0:1], rstd[:, 0:1], ACT.Sqrt).then_inc(x2_root, 1)
            act.wait_ge(x2_ready, 1)
            A(x_res[:, 1, :], y_acc[:, 1, :], ACT.Square, accum_out=ssq[:, 1:2]).then_inc(x2_squared, 1)
            act.wait_ge(x2_mean, 2)
            A(rstd[:, 1:2], rstd[:, 1:2], ACT.Sqrt).then_inc(x2_root, 1)

        @block.vector
        def _(dve):
            v = nc.vector
            v.memset(stat[:, 42:45], 1.0).then_inc(spare_ready, 1)
            step = Chain(dve, dve_step)
            dve.wait_ge(vecs_transposed, 2)
            v.tensor_copy(vcols[:], psum[:, B_MOD, 0:70]).then_inc(cols_ready, 1)
            v.tensor_copy(adab[:], psum[:, B_MOD, 128:224]).then_inc(cols_ready, 1)
            dve.wait_ge(cols_ready, 1)
            v.tensor_tensor(lam_tmp[:, 0:2], vcols[:, LAM:LAM + 2], vcols[:, LAM + 2:LAM + 4], ALU.mult)\
                .then_inc(lam_prod, 1)
            dve.wait_ge(silu_exp, 1)
            step.link(v.tensor_scalar_add(silu_c[:], silu_c[:], 1.0))
            step.link(v.reciprocal(silu_c[:], silu_c[:]))
            step.link(v.tensor_tensor(silu_c[:], silu_c[:], vcols[:, C_G:C_G + KT], ALU.mult))
            v.tensor_scalar(vcols[:, SUB_G:SUB_G + 2], vcols[:, SUB_G:SUB_G + 2], 1.0 - LAM_INIT, None, ALU.mult)\
                .then_inc(cols_ready, 1)
            dve.wait_ge(dist_ready, 1)
            step.link(v.scalar_tensor_tensor(out=neg_dist, in0=neg_dist, scalar=-1.0, in1=neg_dist, op0=ALU.mult,
                                             op1=ALU.min))
            dve.wait_ge(lam_exp, 1)
            step.link(v.tensor_tensor(neg_lam, lam_tmp[:, 3:4], lam_tmp[:, 2:3], ALU.subtract))
            step.link(v.tensor_scalar_add(neg_lam, neg_lam, -LAM_INIT))

            def ada_chunk(b, par, j):
                dve.wait_ge(ada_loaded[j], b * 32 + 32 if isinstance(b, int) and b < 8 else b * 16 + 144)
                if j == 0 and not (isinstance(b, int) and b < 2):
                    dve.wait_ge(mod_summed, b - 1)
                for kk in range(4):
                    k = 4 * j + kk
                    w = ada_ring[:, j, ADA_BLK * kk:ADA_BLK * (kk + 1)]
                    if k == 0:
                        ins = v.tensor_scalar(acc[:, par, :], w, silu_c[:, k:k + 1], None, ALU.mult)
                    else:
                        ins = v.scalar_tensor_tensor(out=acc[:, par, :], in0=w, scalar=silu_c[:, k:k + 1],
                                                     in1=acc[:, par, :], op0=ALU.mult, op1=ALU.add)
                    if kk < 3:
                        step.link(ins)
                ins.then_inc(ada_used, 1)
                dve.wait_ge(ada_used, b * ADA_CH + (j + 1))

            def keep_mod(b, par, col):
                dve.wait_ge(mod_summed, b + 1)
                v.tensor_tensor(mod[:, bass.ds(col, 4)], psum[:, B_MOD, 4 * par:4 * par + 4],
                                adab[:, bass.ds(col, 4)], ALU.add).then_inc(mod_ready, 1)

            def keep_first(b):
                par, at = b % 2, slice(2 * b, 2 * b + 2)

                def by_vec(t):
                    return t[:, 0:2 * KT].rearrange("p (s k) -> p s k", s=2)[:, :, at]

                dve.wait_ge(mod_summed, b + 1)
                v.tensor_tensor(by_vec(mod), psum[:, B_MOD, 4 * par:4 * par + 4].rearrange("p (s k) -> p s k", s=2),
                                by_vec(adab), ALU.add).then_inc(mod_ready, 1)
                dve.wait_ge(mod_ready, b + 1)
                v.scalar_tensor_tensor(out=a1[:, at], in0=mod[:, SC1 + 2 * b:SC1 + 2 * b + 2], scalar=1.0,
                                       in1=vcols[:, N1_G + 2 * b:N1_G + 2 * b + 2],
                                       op0=ALU.add, op1=ALU.mult).then_inc(a1_ready, 1)

            for j in range(ADA_CH):
                ada_chunk(0, 0, j)
            dve.wait_ge(x_squared, TT)
            v.tensor_scalar(rstd, ssq, 1.0 / D, EPS, ALU.mult, ALU.add).then_inc(x_mean, 1)
            dve.wait_ge(x_root, 1)
            step.link(v.reciprocal(rstd, rstd))
            for a in range(TT):
                v.tensor_scalar(x_tok[:, a, :], x_tok[:, a, :], rstd[:, a:a + 1], None, ALU.mult).then_inc(x_scaled, 1)
            for b in range(1, 8):
                for j in range(ADA_CH):
                    ada_chunk(b, b % 2, j)
                    if j == 0:
                        keep_first(b - 1)
            keep_first(7)

            def add_bias(h):
                step.link(v.tensor_scalar(neg_dist, neg_dist, 0.5, None, ALU.mult))
                for a in range(TT):
                    dve.wait_ge(s_done, h * 2 + (a + 1))
                    if a == 0 and not (isinstance(h, int) and h == 0):
                        dve.wait_ge(at_done, h)
                    v.tensor_tensor(prob[:, a, :, :], psum[:, B_S + a, :].rearrange("p (i k) -> p i k", i=2),
                                    neg_dist[:, a:a + 1, :].to_broadcast([P, 2, T]), ALU.add).then_inc(s_read, 1)
                    dve.wait_ge(s_read, h * 2 + (a + 1))
                    v.reduce_max(neg_max[:, a, :], prob[:, a, :, :], X, negate=True).then_inc(max_ready, 1)

            def combine(h):
                for a in range(TT):
                    dve.wait_ge(e_done, h * 4 + (2 * a + 2))
                    step.link(v.reciprocal(rden[:, a, :], den[:, a, :]))
                    step.link(v.tensor_tensor(rden[:, a, 1:2], rden[:, a, 1:2], neg_lam, ALU.mult))
                    step.link(v.tensor_scalar(prob[:, a, 0, :], prob[:, a, 0, :], rden[:, a, 0:1], None, ALU.mult))
                    v.scalar_tensor_tensor(out=prob[:, a, 0, :], in0=prob[:, a, 1, :], scalar=rden[:, a, 1:2],
                                           in1=prob[:, a, 0, :], op0=ALU.mult, op1=ALU.add).then_inc(a_ready, 1)

            def out_rstd(h):
                dve.wait_ge(o_squared, h * 2 + 2)
                v.tensor_scalar(omid, osq, 1.0 / VD, EPS, ALU.mult, ALU.add).then_inc(o_mean, 1)
                dve.wait_ge(o_root, h + 1)
                v.reciprocal(omid, omid).then_inc(o_rstd, 1)

            def head(h, b, par, third=False, ahead=2):
                add_bias(h - 1)
                combine(h - 1)
                ada_chunk(b - 1, 1 - par, 2)
                ada_chunk(b - 1, 1 - par, 3)
                keep_mod(b - 2, par, b * 4 - 8)
                for j in range(ADA_CH):
                    ada_chunk(b, par, j)
                keep_mod(b - 1, 1 - par, b * 4 - 4)
                if third:
                    for j in range(ADA_CH):
                        ada_chunk(b + 1, 1 - par, j)
                    keep_mod(b, par, b * 4)
                    out_rstd(h - 1)
                    for j in range(ahead):
                        ada_chunk(b + 2, par, j)
                else:
                    out_rstd(h - 1)
                    ada_chunk(b + 1, 1 - par, 0)
                    ada_chunk(b + 1, 1 - par, 1)

            ada_chunk(8, 0, 0)
            ada_chunk(8, 0, 1)
            add_bias(0)
            combine(0)
            ada_chunk(8, 0, 2)
            ada_chunk(8, 0, 3)
            out_rstd(0)
            ada_chunk(9, 1, 0)
            ada_chunk(9, 1, 1)
            per_head = 8 * 3 + 1 + 3 * TT
            with dve.Fori(1, 3) as pair:
                step.start_loop(pair - 1, 2 * per_head)
                head(pair * 2, pair * 4 + 6, 0)
                head(pair * 2 + 1, pair * 4 + 8, 0)
            step.end_loop(2)
            head(6, 18, 0, third=True)
            head(7, 21, 1, third=True, ahead=1)
            add_bias(HEADS - 1)
            keep_mod(22, 0, 88)
            combine(HEADS - 1)
            ada_chunk(23, 1, 1)
            ada_chunk(23, 1, 2)
            out_rstd(HEADS - 1)
            ada_chunk(23, 1, 3)
            dve.wait_ge(mod_ready, 23)
            step.link(v.scalar_tensor_tensor(out=a2[:], in0=mod[:, SC2:SC2 + KT], scalar=1.0,
                                             in1=vcols[:, N2_G:N2_G + KT], op0=ALU.add, op1=ALU.mult))
            dve.wait_ge(router_loaded, 64)
            v.tensor_tensor(router_wa, router_w[:], a2[:].unsqueeze(2).to_broadcast([P, KT, 36]), ALU.mult)\
                .then_inc(router_scaled, 1)
            keep_mod(23, 1, 92)
            dve.wait_ge(gate_ready, 4)
            dve.wait_ge(x_again, 16)
            for ch in range(OUT_CH):
                cols = slice(VD * ch, VD * (ch + 1))
                dve.wait_ge(w_used, QKV_CH + ch + 1)
                if ch:
                    dve.wait_ge(x1_ready, ch)
                v.tensor_tensor(y_tmp, psum[:, 3 + ch % 4, :].rearrange("p (a n) -> p a n", a=TT),
                                gate1[:, cols].unsqueeze(1).to_broadcast([P, TT, VD]), ALU.mult).then_inc(y_read, 1)
                dve.wait_ge(y_read, ch + 1)
                v.tensor_tensor(x_res[:, :, cols], x_res[:, :, cols], y_tmp, ALU.add).then_inc(x1_ready, 1)
                if ch == 2:
                    dve.wait_ge(bias_spread, 1)
                    step.link(v.tensor_tensor(router_b[:], router_b[:], psum[:, B_MOD, 0:36], ALU.add))
            dve.wait_ge(x1_squared, OUT_CH * TT)
            step.link(v.reduce_sum(ssq, ssq8, X))
            v.tensor_scalar(rstd, ssq, 1.0 / D, EPS, ALU.mult, ALU.add).then_inc(x1_mean, 1)
            dve.wait_ge(x1_root, 1)
            step.link(v.reciprocal(rstd, rstd))

            dve.wait_ge(logits_added, OUT_CH)
            for a in range(TT):
                step.link(v.scalar_tensor_tensor(out=logits[:, a, :], in0=psum[:, B_LOGIT, 36 * a:36 * (a + 1)],
                                                 scalar=rstd[:, a:a + 1], in1=router_b[:], op0=ALU.mult,
                                                 op1=ALU.add))
            lg = logits[:, :, 0:GROUPS]

            def first_max(hot, src, n, top, back, got):
                shape = [P, TT, n]
                step.link(v.reduce_max(top, src, X))
                step.link(v.tensor_tensor(hot, src, top.unsqueeze(2).to_broadcast(shape), ALU.is_equal))
                step.link(v.tensor_tensor(hot, hot, back.unsqueeze(1).to_broadcast(shape), ALU.mult))
                step.link(v.reduce_max(got, hot, X))
                step.link(v.tensor_tensor(hot, hot, got.unsqueeze(2).to_broadcast(shape), ALU.is_equal))

            step.link(v.tensor_scalar(back8, slot_no[:, 0:8], -1.0, 9.0, ALU.mult, ALU.add))
            first_max(g_hot, lg, GROUPS, r_top, back8[:, 4:8], r_got)
            v.tensor_tensor(rt_exp_in, lg, r_top.unsqueeze(2).to_broadcast([P, TT, GROUPS]), ALU.subtract)\
                .then_inc(shifted, 1)
            for a in range(TT):
                part = by_group[:, GROUPS * a:GROUPS * (a + 1), :]
                step.link(v.tensor_tensor(part, logits[:, a, GROUPS:].rearrange("p (g e) -> p g e", g=GROUPS),
                                          g_hot[:, a, :].unsqueeze(2).to_broadcast([P, GROUPS, PER_GROUP]),
                                          ALU.mult))
                step.link(v.reduce_sum(e_log[:, a, :], part.rearrange("p g e -> p e g"), X))
            first_max(e_hot1, e_log, PER_GROUP, r_e1, back8, r_got)
            step.link(v.scalar_tensor_tensor(out=e_log2, in0=e_hot1, scalar=-BIG, in1=e_log, op0=ALU.mult,
                                             op1=ALU.add))
            first_max(e_hot2, e_log2, PER_GROUP, r_e2, back8, r_got)
            v.tensor_tensor(rt_gap, r_e2, r_e1, ALU.subtract).then_inc(shifted, 1)
            step.link(v.tensor_tensor(e_log, e_hot1, e_hot2, ALU.add))

            def outer(dst, per_expert):
                for a in range(TT):
                    ins = v.tensor_tensor(dst[:, a, :].rearrange("p (g e) -> p g e", g=GROUPS),
                                          g_hot[:, a, :].unsqueeze(2).to_broadcast([P, GROUPS, PER_GROUP]),
                                          per_expert[:, a:a + 1, :].to_broadcast([P, GROUPS, PER_GROUP]), ALU.mult)
                    if a < TT - 1:
                        step.link(ins)
                return ins

            outer(chosen, e_log).then_inc(assigned, 1)
            dve.wait_ge(ranked, 1)
            step.link(v.scalar_tensor_tensor(out=rank1[:, :, 0:EXPERTS],
                                             in0=psum[:, B_HT, 0:64].rearrange("p (a n) -> p a n", a=TT), scalar=1.0,
                                             in1=chosen, op0=ALU.add, op1=ALU.mult))

            n_over, counts, first, upto = rt_n
            def weigh():
                dve.wait_ge(counted, 1)
                step.link(v.tensor_copy(counts, psum[:, B_D + 1, 0:32]))
                dve.wait_ge(route_exp, 2)
                step.link(v.reduce_sum(r_top, rt_exp_in, X))
                step.link(v.reciprocal(r_top, r_top))
                step.link(v.tensor_scalar_add(r_got, rt_gap, 1.0))
                step.link(v.reciprocal(r_got, r_got))
                step.link(v.tensor_tensor(r_e1, r_top, r_got, ALU.mult))
                step.link(v.tensor_tensor(r_e2, r_e1, rt_gap, ALU.mult))
                step.link(v.tensor_tensor(e_hot1, e_hot1, r_e1.unsqueeze(2).to_broadcast([P, TT, PER_GROUP]), ALU.mult))
                step.link(v.tensor_tensor(e_hot2, e_hot2, r_e2.unsqueeze(2).to_broadcast([P, TT, PER_GROUP]), ALU.mult))
                step.link(v.tensor_tensor(e_hot1, e_hot1, e_hot2, ALU.add))
                step.link(outer(weight[:, :, 0:EXPERTS], e_hot1))

            def plan_further_items():
                step.link(v.tensor_scalar(n_over, counts, float(SLOTS), None, ALU.is_gt))
                for k in range(2, T // SLOTS):
                    step.link(v.scalar_tensor_tensor(out=n_over, in0=counts, scalar=float(SLOTS * k), in1=n_over,
                                                     op0=ALU.is_gt, op1=ALU.add))
                src, dst = n_over, upto
                for sh in (1, 2, 4, 8, 16):
                    step.link(v.tensor_copy(dst[:, 0:sh], src[:, 0:sh]))
                    step.link(v.tensor_tensor(dst[:, sh:], src[:, sh:], src[:, 0:EXPERTS - sh], ALU.add))
                    src, dst = dst, (first if dst is upto else upto)
                assert src is upto
                step.link(v.tensor_tensor(first, upto, n_over, ALU.subtract))
                own, tmp = over
                wide = [P, EXTRA, EXPERTS]
                step.link(v.tensor_scalar_add(item_no, slot_no[:, 0:EXTRA], -1.0))
                step.link(v.tensor_tensor(own, item_no.unsqueeze(2).to_broadcast(wide),
                                          first.unsqueeze(1).to_broadcast(wide), ALU.is_ge))
                step.link(v.tensor_tensor(tmp, item_no.unsqueeze(2).to_broadcast(wide),
                                          upto.unsqueeze(1).to_broadcast(wide), ALU.is_lt))
                step.link(v.tensor_tensor(own, own, tmp, ALU.mult))

                def pick(dst, table):
                    step.link(v.tensor_tensor(tmp, own, table.unsqueeze(1).to_broadcast(wide), ALU.mult))
                    step.link(v.reduce_sum(dst, tmp, X))

                pick(item_a, first)
                step.link(v.tensor_tensor(item_a, slot_no[:, 0:EXTRA], item_a, ALU.subtract))
                for a in range(TT):
                    pick(item_b, rank1[:, a, 0:EXPERTS])
                    step.link(v.scalar_tensor_tensor(out=rank1[:, a, EXPERTS:], in0=item_a, scalar=-float(SLOTS),
                                                     in1=item_b, op0=ALU.mult, op1=ALU.add))
                    pick(weight[:, a, EXPERTS:], weight[:, a, 0:EXPERTS])
                step.link(v.tensor_scalar_add(first, slot_no[:], -1.0))
                pick(item_b, first)
                step.link(v.tensor_copy(extra_i[:, 0:EXTRA], item_b))
                step.link(v.tensor_scalar(item_a[:, 0:4], item_no[:, 0:4], float(QUAD), upto[:, EXPERTS - 1:EXPERTS],
                                          ALU.mult, ALU.is_lt))
                step.link(v.reduce_sum(item_b[:, 0:1], item_a[:, 0:4], X))
                v.tensor_copy(extra_i[:, EXTRA:EXTRA + 1], item_b[:, 0:1]).then_inc(tables_ready, 1)
                dve.wait_ge(tables_ready, 1)

            def moe_group(g, first_group=False):
                wide4 = [P, QUAD, SLOTS]
                for a in range(TT):
                    r = rank1[:, a, bass.ds(g * QUAD, QUAD)]
                    step.link(v.tensor_tensor(sel_w[:, a, :, :], slot_no[:].unsqueeze(1).to_broadcast(wide4),
                                              r.unsqueeze(2).to_broadcast(wide4), ALU.is_equal))
                for a in range(TT):
                    ins = v.tensor_scalar(sel[:, a, :, :], sel_w[:, a, :, :], rstd[:, a:a + 1], None, ALU.mult)
                    if a < TT - 1:
                        step.link(ins)
                ins.then_inc(sel_ready, 1)
                dve.wait_ge(sel_ready, g + 1)
                for q in range(4):
                    ks = slice(4 * q, 4 * q + 4)
                    dve.wait_ge(gathered, g * 4 + (q + 1))
                    step.link(v.tensor_tensor(x_items[:, ks, :],
                                              psum[:, B_G + q, :].rearrange("p (k s) -> p k s", k=4),
                                              a2[:, ks].unsqueeze(2).to_broadcast([P, 4, P]), ALU.mult))
                    v.tensor_tensor(x_items[:, ks, :], x_items[:, ks, :],
                                    mod[:, SH2 + 4 * q:SH2 + 4 * q + 4].unsqueeze(2).to_broadcast([P, 4, P]), ALU.add)\
                        .then_inc(items_ready, 1)
                if first_group:
                    weigh()
                for a in range(TT):
                    w = weight[:, a, bass.ds(g * QUAD, QUAD)]
                    ins = v.tensor_tensor(sel_w[:, a, :, :], sel_w[:, a, :, :], w.unsqueeze(2).to_broadcast(wide4),
                                          ALU.mult)
                    if a < TT - 1:
                        step.link(ins)
                ins.then_inc(selw_ready, 1)
                for i in range(QUAD):
                    m = g * QUAD + i
                    dve.wait_ge(gate_exp, m + 1)
                    step.link(v.tensor_scalar_add(hid_s[1], hid_s[0], 1.0))
                    step.link(v.reciprocal(hid_s[2], hid_s[1]))
                    step.link(v.tensor_tensor(hid_s[1], hid_s[2], psum[:, B_GU, 0:P], ALU.mult))
                    v.tensor_tensor(hid_s[3], hid_s[1], psum[:, B_GU, P:2 * P], ALU.mult).then_inc(hid_ready, 1)
                    dve.wait_ge(w_used, m * RING + (MOE_CH0 + 6))
                    for n in range(4):
                        cols = slice(512 * n, 512 * (n + 1))
                        o, src = o_items[32 * i:32 * i + 32, cols], psum[32 * n:32 * n + 32, B_D + i % 2, :]
                        if first_group:
                            v.tensor_copy(o, src).then_inc(o_ready, 1)
                        else:
                            v.tensor_tensor(o, src, gate2[32 * n:32 * n + 32, cols], ALU.mult).then_inc(o_ready, 1)
                    if first_group and i == 2:
                        plan_further_items()
                if first_group:
                    dve.wait_ge(gate_ready, 12)
                    dve.wait_ge(o_ready, 4 * QUAD)
                    for n in range(4):
                        cols = slice(512 * n, 512 * (n + 1))
                        v.tensor_tensor(o_items[:, cols], o_items[:, cols], gate2[:, cols], ALU.mult)\
                            .then_inc(o_gated, 1)
                    dve.wait_ge(y_started, 1)
                for a in range(TT):
                    for n in range(4):
                        at = 4 * a + n
                        cols = slice(512 * n, 512 * (n + 1))
                        dve.wait_ge(y_done, g * 8 + (at + 1))
                        v.tensor_tensor(y_acc[:, a, cols], y_acc[:, a, cols], psum[:, B_G + n, :], ALU.add)\
                            .then_inc(y_added, 1)
                dve.wait_ge(y_added, g * 8 + 8)
                v.memset(stat[:, 42:43], 0.0)

            moe_group(0, first_group=True)
            per_group = TT + (TT - 1) + 4 + (TT - 1) + 3 * QUAD
            extra_groups = dve.value_load(extra_i[0:1, EXTRA:EXTRA + 1], min_val=0, max_val=EXTRA // QUAD)
            with dve.Fori(1, MAIN) as g:
                step.start_loop(g - 1, per_group)
                moe_group(g)
            step.end_loop(MAIN - 1)
            with dve.If(extra_groups > 0):
                with dve.Fori(0, EXTRA // QUAD) as g:
                    with dve.If(g < extra_groups):
                        step.start_loop(g, per_group)
                        moe_group(g + MAIN)
                    dve.end_ifs()
            dve.end_ifs()
            step.end_loop(0)

            v.memset(stat[:, 45:46], 0.0).then_inc(x2_ready, 1)
            for a in range(TT):
                dve.wait_ge(x2_squared, a + 1)
                v.tensor_scalar(rstd[:, a:a + 1], ssq[:, a:a + 1], 1.0 / D, EPS, ALU.mult, ALU.add)\
                    .then_inc(x2_mean, 1)
                dve.wait_ge(x2_root, a + 1)
                v.reciprocal(rstd[:, a:a + 1], rstd[:, a:a + 1]).then_inc(fin_step, 1)
                dve.wait_ge(fin_step, a + 1)
                for half in range(2):
                    cols = slice(D // 2 * half, D // 2 * (half + 1))
                    v.scalar_tensor_tensor(out=x_res[:, a, cols], in0=y_acc[:, a, cols], scalar=rstd[:, a:a + 1],
                                           in1=final_gain[:, cols], op0=ALU.mult, op1=ALU.mult).then_inc(out_ready, 1)


_INS = ['x', 'c', 'ada_w', 'ada_b', 'norm1_g', 'norm2_g', 'router_g_w', 'router_g_b', 'router_e_w', 'router_e_b',
        'moe_w_gu', 'moe_w_d', 'da_w_in', 'da_w_out', 'da_lam_q1', 'da_lam_k1', 'da_lam_q2', 'da_lam_k2',
        'da_subln_g', 'final_g']


def kernel(**inputs):
    import numpy as _np
    import concourse.bacc as _bacc
    from concourse import mybir as _mybir
    from concourse.bass_utils import run_bass_kernel_spmd as _run

    nc = _bacc.Bacc("TRN2", target_bir_lowering=False, num_devices=1)
    arrays, args = {}, []
    for name in _INS:
        a = _np.ascontiguousarray(inputs[name])
        arrays[f"in_{name}_dram"] = a
        args.append(nc.dram_tensor(f"in_{name}_dram", a.shape, _mybir.dt.from_np(a.dtype), kind="ExternalInput").ap())
    args.append(nc.dram_tensor("out_0_dram", inputs["x"].shape, _mybir.dt.float32, kind="ExternalOutput").ap())
    encoder_layer(nc, *args)
    r = _run(nc, [arrays], core_ids=[0])
    return r.results[0]["out_0_dram"]
```
